# Optimizing a Trainium2 kernel written in Bass

```python
import jax, jax.numpy as jnp
from jax import lax
import numpy as np

D_MODEL = 1024
BATCH = 1
SEQ = 1024
DEPTH = 2

GRID_W = 64
CTX_LEN = 256
CONV_WIDTH = 512
CONV_K = 3
N_HEADS = 8
N_KV_HEADS = 2
GROUP = N_HEADS // N_KV_HEADS
HEAD_DIM = 64
ATTN_WIDTH = N_HEADS * HEAD_DIM
KV_WIDTH = N_KV_HEADS * HEAD_DIM
WINDOW = 128
BLOCK = 128
ROPE_THETA = 10000.0
ROPE_FREQS = HEAD_DIM // 4
EPS = 1e-6
NEG = -1e30
IN_COLS = 4 * CONV_WIDTH + 2 * ATTN_WIDTH + 2 * KV_WIDTH + 2 * D_MODEL

kernel_name = "hybrid_conv_swa_dit_block"

def rms_norm(x, w):
    xf = x.astype(jnp.float32)
    y = xf * lax.rsqrt(jnp.mean(xf * xf, axis=-1, keepdims=True) + EPS)
    return (y * w.astype(jnp.float32)).astype(x.dtype)

def project(h, w_in):
    sizes = (CONV_WIDTH, CONV_WIDTH, CONV_WIDTH, CONV_WIDTH,
             ATTN_WIDTH, KV_WIDTH, KV_WIDTH, ATTN_WIDTH, D_MODEL, D_MODEL)
    points = tuple(int(p) for p in np.cumsum(sizes)[:-1])
    p = jnp.einsum('bsd,de->bse', h, w_in)
    return jnp.split(p, points, axis=-1)

def short_conv(u, w):
    L = u.shape[1]
    pad = CONV_K // 2
    up = jnp.pad(u, ((0, 0), (pad, pad), (0, 0)))
    return sum(up[:, k:k + L] * w[k] for k in range(CONV_K))

def rope_2d(x, cos, sin):
    B_, S_, H_, _ = x.shape
    xr = x.reshape(B_, S_, H_, 2, 2, ROPE_FREQS)
    x1, x2 = xr[..., 0, :], xr[..., 1, :]
    cs = cos[None, :, None]
    sn = sin[None, :, None]
    out = jnp.stack([x1 * cs - x2 * sn, x2 * cs + x1 * sn], axis=-2)
    return out.reshape(B_, S_, H_, HEAD_DIM).astype(x.dtype)

def sink_softmax(scores, sink):
    sk = jnp.broadcast_to(sink.astype(jnp.float32).reshape(N_KV_HEADS, GROUP, 1, 1),
                          scores.shape[:-1] + (1,))
    p = jax.nn.softmax(jnp.concatenate([sk, scores], axis=-1), axis=-1)
    return p[..., 1:]

def latent_attention(q, k, v, k_ctx, v_ctx, sink):
    B_, S_ = q.shape[:2]
    nb = S_ // BLOCK
    scale = HEAD_DIM ** -0.5
    k_pad = jnp.pad(k, ((0, 0), (BLOCK, BLOCK), (0, 0), (0, 0)))
    v_pad = jnp.pad(v, ((0, 0), (BLOCK, BLOCK), (0, 0), (0, 0)))
    qb = jnp.moveaxis(q.reshape(B_, nb, BLOCK, N_KV_HEADS, GROUP, HEAD_DIM), 1, 0)

    def one_block(args):
        i, q_i = args
        start = i * BLOCK
        k_i = lax.dynamic_slice_in_dim(k_pad, start, 3 * BLOCK, axis=1)
        v_i = lax.dynamic_slice_in_dim(v_pad, start, 3 * BLOCK, axis=1)
        s_loc = jnp.einsum('bqkgd,bskd->bkgqs', q_i, k_i).astype(jnp.float32) * scale
        s_ctx = jnp.einsum('bqkgd,bckd->bkgqc', q_i, k_ctx).astype(jnp.float32) * scale
        q_pos = start + jnp.arange(BLOCK)
        k_pos = start - BLOCK + jnp.arange(3 * BLOCK)
        allowed = ((jnp.abs(q_pos[:, None] - k_pos[None, :]) <= WINDOW)
                   & (k_pos[None, :] >= 0) & (k_pos[None, :] < S_))
        s_loc = jnp.where(allowed, s_loc, NEG)
        p = sink_softmax(jnp.concatenate([s_loc, s_ctx], axis=-1), sink).astype(v.dtype)
        o = (jnp.einsum('bkgqs,bskd->bqkgd', p[..., :3 * BLOCK], v_i)
             + jnp.einsum('bkgqc,bckd->bqkgd', p[..., 3 * BLOCK:], v_ctx))
        return o

    out = lax.map(one_block, (jnp.arange(nb), qb))
    return jnp.moveaxis(out, 0, 1).reshape(B_, S_, ATTN_WIDTH)

def context_attention(q_c, k_c, v_c, sink):
    B_, L_ = q_c.shape[:2]
    qg = q_c.reshape(B_, L_, N_KV_HEADS, GROUP, HEAD_DIM)
    s = jnp.einsum('bqkgd,bckd->bkgqc', qg, k_c).astype(jnp.float32) * HEAD_DIM ** -0.5
    p = sink_softmax(s, sink).astype(v_c.dtype)
    return jnp.einsum('bkgqc,bckd->bqkgd', p, v_c).reshape(B_, L_, ATTN_WIDTH)

def mixer_output(parts, attn, conv_w, w_a_out, w_b_out, w_o):
    b_g, c_g, u, z_a, _, _, _, z_b, g_a, g_b = parts
    y_a = (b_g * short_conv(c_g * u, conv_w)) * jax.nn.silu(z_a)
    y_a = jnp.einsum('bsc,cd->bsd', y_a, w_a_out)
    y_b = jnp.einsum('bsc,cd->bsd', attn * jax.nn.silu(z_b), w_b_out)
    m = jax.nn.sigmoid(g_a) * y_a + jax.nn.sigmoid(g_b) * y_b
    return jnp.einsum('bsd,de->bse', m, w_o)

def setup_inputs(seed: int = 0) -> dict:
    key = jax.random.key(seed)
    ks = jax.random.split(key, 14)
    nrm = jax.random.normal
    f32 = jnp.float32
    return {
        "x": nrm(ks[0], (BATCH, SEQ, D_MODEL), f32),
        "c": nrm(ks[1], (BATCH, D_MODEL), f32),
        "ctx": nrm(ks[2], (BATCH, CTX_LEN, D_MODEL), f32),
        "c_ctx": nrm(ks[3], (D_MODEL,), f32),
        "norm_w": 1.0 + 0.02 * nrm(ks[4], (DEPTH, D_MODEL), f32),
        "w_mod": nrm(ks[5], (DEPTH, D_MODEL, 3 * D_MODEL), f32) * (0.5 * D_MODEL ** -0.5),
        "b_mod": 0.01 * nrm(ks[6], (DEPTH, 3 * D_MODEL), f32),
        "w_in": nrm(ks[7], (DEPTH, D_MODEL, IN_COLS), f32) * D_MODEL ** -0.5,
        "conv_w": nrm(ks[8], (DEPTH, CONV_K, CONV_WIDTH), f32) * CONV_K ** -0.5,
        "w_a_out": nrm(ks[9], (DEPTH, CONV_WIDTH, D_MODEL), f32) * CONV_WIDTH ** -0.5,
        "w_b_out": nrm(ks[10], (DEPTH, ATTN_WIDTH, D_MODEL), f32) * ATTN_WIDTH ** -0.5,
        "attn_sink": 0.5 * nrm(ks[11], (DEPTH, N_HEADS), f32),
        "w_o": nrm(ks[12], (DEPTH, D_MODEL, D_MODEL), f32) * D_MODEL ** -0.5,
        "final_norm_w": 1.0 + 0.02 * nrm(ks[13], (D_MODEL,), f32),
    }

def reference(x, c, ctx, c_ctx, norm_w, w_mod, b_mod, w_in, conv_w, w_a_out, w_b_out,
              attn_sink, w_o, final_norm_w):
    B_, S_, _ = x.shape
    L_ = ctx.shape[1]
    ROWS = S_ // GRID_W
    rows = jnp.broadcast_to(jnp.arange(ROWS)[:, None], (ROWS, GRID_W)).reshape(-1)
    cols = jnp.broadcast_to(jnp.arange(GRID_W)[None, :], (ROWS, GRID_W)).reshape(-1)
    inv_freq = ROPE_THETA ** (-jnp.arange(ROPE_FREQS, dtype=jnp.float32) / ROPE_FREQS)
    ang = jnp.stack([rows.astype(jnp.float32)[:, None] * inv_freq,
                     cols.astype(jnp.float32)[:, None] * inv_freq], axis=1)
    cos, sin = jnp.cos(ang), jnp.sin(ang)

    for l in range(DEPTH):
        last = l == DEPTH - 1
        mod_x = jnp.einsum('bd,de->be', jax.nn.silu(c), w_mod[l]) + b_mod[l]
        shift_x, scale_x, gate_x = jnp.split(mod_x[:, None, :], 3, axis=-1)
        mod_c = jnp.einsum('d,de->e', jax.nn.silu(c_ctx), w_mod[l]) + b_mod[l]
        shift_c, scale_c, gate_c = jnp.split(mod_c, 3, axis=-1)

        hx = rms_norm(x, norm_w[l]) * (1.0 + scale_x) + shift_x
        hc = rms_norm(ctx, norm_w[l]) * (1.0 + scale_c) + shift_c
        px = project(hx, w_in[l])
        pc = project(hc, w_in[l])

        q_c = pc[4].reshape(B_, L_, N_HEADS, HEAD_DIM)
        k_c = pc[5].reshape(B_, L_, N_KV_HEADS, HEAD_DIM)
        v_c = pc[6].reshape(B_, L_, N_KV_HEADS, HEAD_DIM)

        q_x = rope_2d(px[4].reshape(B_, S_, N_HEADS, HEAD_DIM), cos, sin)
        k_x = rope_2d(px[5].reshape(B_, S_, N_KV_HEADS, HEAD_DIM), cos, sin)
        v_x = px[6].reshape(B_, S_, N_KV_HEADS, HEAD_DIM)
        attn_x = latent_attention(q_x, k_x, v_x, k_c, v_c, attn_sink[l])
        out_x = mixer_output(px, attn_x, conv_w[l], w_a_out[l], w_b_out[l], w_o[l])

        if not last:
            attn_c = context_attention(q_c, k_c, v_c, attn_sink[l])
            out_c = mixer_output(pc, attn_c, conv_w[l], w_a_out[l], w_b_out[l], w_o[l])
            ctx = ctx + gate_c * out_c
        x = x + gate_x * out_x

    return rms_norm(x, final_norm_w)


_drawn_inputs = setup_inputs


def setup_inputs(seed=0):
    import zlib

    import numpy as np

    out = dict(_drawn_inputs(seed))
    spreads = {}
    factors = {'ctx': 5.613, 'norm_w': 7.302, 'b_mod': 6.476, 'attn_sink': 8.0, 'final_norm_w': 2.742}
    for name, (base, spread) in spreads.items():
        noise = np.random.default_rng([zlib.crc32(name.encode()), seed]).standard_normal(out[name].shape)
        drawn = base * np.exp(spread * noise) if base else spread * noise
        out[name] = __import__('jax').numpy.asarray(drawn.astype(out[name].dtype))
    for name, factor in factors.items():
        out[name] = (out[name] * factor).astype(out[name].dtype)
    return out
```

```python
import concourse.bass as bass
import numpy as np
from concourse import mybir
from contextlib import ExitStack

F32 = mybir.dt.float32
F32R = mybir.dt.float32r
BF16 = mybir.dt.bfloat16
ACT = mybir.ActivationFunctionType
ALU = mybir.AluOpType
AX = mybir.AxisListType

D, SEQ, CTX, DEPTH, GRID_W = 1024, 1024, 256, 2, 64
CONV, CONV_K, HEADS, KV_HEADS, HD = 512, 3, 8, 2, 64
ATT, BLK, EPS, NEG = HEADS * HD, 128, 1e-6, -1e30
SCALE = HD ** -0.5
P = 128
KT = D // P
CT = CONV // P
PAIRS = HEADS // 2
TOK = SEQ + CTX
C_B, C_C, C_U, C_Z = 0, CONV, 2 * CONV, 3 * CONV
C_Q = 4 * CONV
C_K = C_Q + ATT
C_V = C_K + KV_HEADS * HD
C_ZB = C_V + KV_HEADS * HD
C_GA = C_ZB + ATT
C_GB = C_GA + D
IN_COLS = C_GB + D
CH = 512
MOD_GROUP = 4
MODS = 3 * KT


class Stream:

    def __init__(self, name, tokens, key0):
        self.name, self.T, self.key0 = name, tokens, key0
        self.chunks = [(o, min(CH, tokens - o)) for o in range(0, tokens, CH)]
        self.nch = len(self.chunks)
        self.blocks = tokens // BLK
        self.lat = name == "lat"

    def key_tiles(self, b):
        own = [k for k in (b - 1, b, b + 1) if 0 <= k < self.blocks] if self.lat else []
        return own + [SEQ // BLK + k for k in range(CTX // BLK)]

    def rounds(self, b):
        t = self.key_tiles(b)
        return [t[n:n + 2] for n in range(0, len(t), 2)]

    def round_of(self, b):
        return sum(len(self.rounds(n)) for n in range(b))


LAT = Stream("lat", SEQ, 0)
CTXS = Stream("ctx", CTX, SEQ)


SIDE_TILES = 3


def fills(st):
    todo = [(t, c, k) for t in range(SIDE_TILES) for c in range(st.nch) for k in range(KT)]
    steps = st.blocks + 1
    out, at = [], 0
    for b in range(steps):
        n = (len(todo) * (b + 1)) // steps - at
        a1 = (n + 2) // 3
        a2 = (n - a1 + 1) // 2
        part = todo[at:at + n]
        out.append((part[:a1], part[a1:a1 + a2], part[a1 + a2:]))
        at += n
    return out


def slots_done(parts):
    return [(t, c) for part in parts for t, c, k in part if k == KT - 1]


BODY = {"kv": [1, 1], "attn": [1] * 4, "mixb": [2, 2], "conv": [1] * 4, "mixa": [1, 1, 2] * 2,
        "wout": [1, 1]}


START = {"att_done": 1, "exp_done": 1, "m_done": 1, "pt_copied": 1, "pt_done": 2, "qk_done": 1,
         "tap_done": 1, "slot_read": 1, "av_done": 1, "gb_out": 16}


class Phase:

    def __init__(self, kind, st, layer, base, tile0, slot0, round0, av0):
        self.kind, self.st, self.layer, self.base = kind, st, layer, base
        self.tile0, self.slot0, self.round0, self.av0 = tile0, slot0, round0, av0


def make_phases():
    order = []
    for layer in range(DEPTH):
        order.append(("mod", None, layer))
        last = layer == DEPTH - 1
        for st in (CTXS, LAT):
            kinds = ["load"] if layer == 0 or st is CTXS else []
            kinds += ["norm", "kv"]
            if st is LAT or not last:
                kinds += ["attn", "mixb", "conv", "mixa", "wout"]
            order += [(k, st, layer) for k in kinds]
    order.append(("final", LAT, DEPTH))
    count, out = {k: v for k, v in START.items() if k not in ("slot_read", "av_done", "gb_out")}, []
    tile = slot = rnd = av = 0
    for kind, st, layer in order:
        out.append(Phase(kind, st, layer, dict(count), tile, slot, rnd, av))
        n = st.nch if st else 0
        tiles = slots = rounds = avs = 0
        gain = {}
        if kind == "mod":
            gain = {"mod_mm": MODS // MOD_GROUP, "modv_ready": 1, "mod_done": 1}
        elif kind == "load":
            gain = ({"xt_mm": 2 * st.blocks, "xt_copied": 2 * st.blocks} if layer == 0
                    else {"xc_in": 16})
        elif kind in ("norm", "final"):
            gain = {"sq_ready": KT * n, "sq_used": KT * n, "rms_ready": n, "rstd_ready": n,
                    "hn_ready": KT * n}
            if kind == "norm":
                gain.update({"hf_ready": KT * n, "hh_ready": KT * n, "hl_ready": KT * n})
                if spills(st, layer):
                    gain["x_spilled"] = 16
        elif kind == "kv":
            tiles, slots, rounds = 2, 2 * n, n
            gain = {"stack_hi": n, "stack_lo": n}
        elif kind == "attn":
            tiles, slots = 4 * PAIRS, 4 * PAIRS * n
            rounds = avs = PAIRS * st.round_of(st.blocks)
            nb = PAIRS * st.blocks
            gain = {"stack_hi": PAIRS * n, "stack_lo": PAIRS * n, "vcur_ready": PAIRS,
                    "qk_done": nb, "max_ready": nb, "negm_ready": nb, "sinkin_ready": nb,
                    "exp_done": 2 * nb, "den_ready": 2 * nb, "rden_ready": 2 * nb,
                    "p_ready": 2 * nb, "att_half": nb, "att_done": nb,
                    "gate_tanh": PAIRS * n, "yb_done": PAIRS}
        elif kind == "mixb":
            tiles, slots = KT // 2, KT * n
            gain = {"y_hi": CT, "y_lo": CT}
        elif kind == "conv":
            tiles, slots = 4 * CT, 4 * CT * n
            gain = {"halo_zero": 1, "gate_tanh": CT * n, "tap_done": 4 * CT,
                    "y_hi": CT * n, "y_lo": CT * n}
        elif kind == "mixa":
            tiles, slots = KT + KT // 2, 2 * KT * n
            gain = {"m_done": KT * n}
        elif kind == "wout":
            tiles, slots = KT, KT * n
            gain = {"mh_ready": KT, "ml_ready": KT, "x_in": 16}
        if kind in ("kv", "attn") and st.lat:
            r = n if kind == "kv" else PAIRS * n
            gain.update({"rope_shuf": r, "rope_sin": r, "rope_cos": r, "rope_out": r})
        gain["w_hi"] = gain["w_lo"] = tiles
        gain["mm_done"] = slots
        gain["pt_done"] = gain["pt_hi"] = gain["pt_copied"] = rounds
        for k, v in gain.items():
            count[k] = count.get(k, 0) + v
        tile, slot, rnd, av = tile + tiles, slot + slots, rnd + rounds, av + avs
    return out, tile, sorted(count)


def spills(st, layer):
    return st is LAT or layer < DEPTH - 1


def hybrid_block(nc, x, c, ctx, c_ctx, norm_w, w_mod, b_mod, w_in, conv_w, w_a_out, w_b_out,
                 attn_sink, w_o, final_norm_w, cos_t, sin_t, out):
    phases, n_tiles, counters = make_phases()
    stack = ExitStack()
    with stack:
        def sb(name, shape, dt=F32):
            return stack.enter_context(nc.sbuf_tensor(name, shape, dt))

        def zone(*sets):
            made = {}
            for n, tensors in enumerate(sets):
                with ExitStack() as z:
                    for name, shape, dt in tensors:
                        if n == len(sets) - 1:
                            made[name] = sb(name, shape, dt)
                        else:
                            made[name] = z.enter_context(nc.sbuf_tensor(name, shape, dt))
            return made

        ident = sb("ident", [P, P])
        ident_b = sb("ident_b", [P, P], BF16)
        mask_prev = sb("mask_prev", [P, BLK], BF16)
        mask_next = sb("mask_next", [P, BLK], BF16)
        ones = sb("ones", [P, P])
        eps = sb("eps", [P, 1])
        head_start = sb("head_start", [P, len(START) + 3])
        cos_s = sb("cos_s", [P, SEQ])
        sin_s = sb("sin_s", [P, SEQ])
        V_NW = 2 * KT
        V_BM = V_NW + DEPTH * KT
        V_CW = V_BM + DEPTH * MODS
        V_FN = V_CW + DEPTH * CONV_K * CT
        V_ALL = V_FN + KT
        vec_rows = sb("vec_rows", [V_ALL, P])
        vec = sb("vec", [P, V_ALL])
        silu_t = sb("silu_t", [P, 2 * KT])
        silu_c = sb("silu_c", [P, 2 * KT])
        modv = sb("modv", [P, MODS, 2])
        mod_a = sb("mod_a", [P, KT, 2])
        sink = sb("sink", [P, DEPTH * HEADS])
        nsink = sb("nsink", [P, DEPTH * HEADS])
        mx, negm, sinkin, sinkexp, rsum, rden = (
            sb(n, [P, 2, 2]) for n in ("mx", "negm", "sinkin", "sinkexp", "rsum", "rden"))
        raw = sb("raw", [P, 2, KT * P])
        wH = sb("wH", [P, 2, KT * P], F32R)
        wL = sb("wL", [P, 2, KT * P], F32R)
        hH = sb("hH", [P, KT, SEQ], F32R)
        hL = sb("hL", [P, KT, SEQ], F32R)
        th = sb("th", [P, CH])

        z1 = zone([("wm", [P, 2, KT, MOD_GROUP * P], F32)],
                  [("kH", [P, KV_HEADS, TOK], F32R),
                   ("kL", [P, KV_HEADS, TOK], F32R),
                   ("v_all", [P, TOK // BLK, KV_HEADS, P], F32R)],
                  [("m_lat", [P, KT, SEQ], F32)])
        z2 = zone([("q_st", [P, 2, SEQ], F32R),
                   ("prob", [P, 2, 2, 5 * BLK], F32),
                   ("ptH", [P, 2, CH], F32R), ("ptL", [P, 2, CH], F32R),
                   ("o_half", [HD, 2 * BLK], F32)],
                  [("yH", [P, CT, SEQ], F32R), ("yL", [P, CT, SEQ], F32R)],
                  [("xs", [P, KT, SEQ], F32)])
        z3 = zone([("xc", [P, KT, CTX], F32)],
                  [("o_rows", [P, 2, D], F32)],
                  [("cb_lat", [P, SEQ], F32), ("cv_lat", [P, SEQ], F32), ("sz_lat", [P, SEQ], F32)],
                  [("yb_ctx", [P, PAIRS, CTX], F32), ("m_ctx", [P, KT, CTX], F32),
                   ("cb_ctx", [P, CTX], F32), ("cv_ctx", [P, CTX], F32), ("sz_ctx", [P, CTX], F32)],
                  [("yb_lat", [P, PAIRS, SEQ], F32)])
        z4 = zone([("sq", [P, 2, CH], F32), ("rms", [P, 2, CH], F32), ("hn", [P, 2, CH], F32),
                   ("hf", [P, 2, CH], F32)],
                  [("x_rows", [P, 2, D], F32)],
                  [("tgb", [P, 2, SEQ], F32)],
                  [("tga", [P, 2, SEQ], F32), ("gm", [P, 2, CH], F32)],
                  [("cu", [P, SEQ + 2], F32), ("yv", [P, 2, CH], F32)],
                  [("v_cur", [P, TOK // BLK, P], F32R), ("rraw", [P, CH], F32),
                   ("rsh", [P, CH], F32), ("rout", [P, CH], F32), ("szb", [P, SEQ], F32),
                   ("att", [P, SEQ], F32), ("gst", [P, 2, CH], F32), ("vraw", [P, CH], F32)])
        wm, m_lat, kH, kL, v_all = (z1[n] for n in ("wm", "m_lat", "kH", "kL", "v_all"))
        q_st, prob, ptH, ptL, o_half = (z2[n] for n in ("q_st", "prob", "ptH", "ptL", "o_half"))
        yH, yL, xs, xc, o_rows = z2["yH"], z2["yL"], z2["xs"], z3["xc"], z3["o_rows"]
        sq, rms, hn, hf, x_rows = (z4[n] for n in ("sq", "rms", "hn", "hf", "x_rows"))
        tgb, tga, gm, cu, yv = (z4[n] for n in ("tgb", "tga", "gm", "cu", "yv"))
        v_cur, rraw, rsh, rout = (z4[n] for n in ("v_cur", "rraw", "rsh", "rout"))
        szb, att, gst, vraw = (z4[n] for n in ("szb", "att", "gst", "vraw"))
        yb = {"lat": z3["yb_lat"], "ctx": z3["yb_ctx"]}
        m = {"lat": m_lat, "ctx": z3["m_ctx"]}
        cb, cv, sz = ({s: z3[f"{n}_{s}"] for s in ("lat", "ctx")} for n in ("cb", "cv", "sz"))

        x_keep = nc.dram_tensor("x_keep", (P, KT, SEQ), F32).ap()
        ctx_keep = nc.dram_tensor("ctx_keep", (P, KT, CTX), F32).ap()
        gb_keep = nc.dram_tensor("gb_keep", (KT, P, SEQ), F32).ap()

        pp = stack.enter_context(nc.psum_tensor("pp", [P, 2, CH], F32))
        pS = stack.enter_context(nc.psum_tensor("pS", [P, 3 * CH], F32))
        pT = stack.enter_context(nc.psum_tensor("pT", [P, 2, CH], F32))
        pO = stack.enter_context(nc.psum_tensor("pO", [P, CH], F32))

        def new_sem(name):
            return stack.enter_context(nc.semaphore(name))

        sem = {n: new_sem(n) for n in counters}
        const_ready, vec_in, tab_in, vec_mm, vec_ready, nsink_ready, silu_tanh, silu_ready, \
            scale_ready, ctx_kept, out_left, out_right = (new_sem(n) for n in (
                "const_ready", "vec_in", "tab_in", "vec_mm", "vec_ready", "nsink_ready",
                "silu_tanh", "silu_ready", "scale_ready", "ctx_kept", "out_left", "out_right"))
        raw_in, slot_read, av_done, gb_out, gb_in, wm_in, xr_in, out_sent = (
            [new_sem(f"{n}{i}") for i in range(2)] for n in
            ("raw_in", "slot_read", "av_done", "gb_out", "gb_in", "wm_in", "xr_in", "out_sent"))
        block = stack.enter_context(nc.Block())

        w_in_v, w_a_v, w_b_v, w_o_v, w_mod_v = (
            w.rearrange("l (k p) n -> l p k n", p=P) for w in (w_in, w_a_out, w_b_out, w_o, w_mod))

        def no_less(value):
            return max(value, 0) if type(value) is int else value

        def at(name, ph, more=0, i=0, per=0):
            return no_less(i * per + (ph.base.get(name, 0) + more))

        def slots_at(ph, s, i=0, per=0):
            return no_less(i * per + (ph.slot0 + s + 1))

        def bank(ph, s):
            return (ph.slot0 + s) % 2

        def reads_at(ph, s, i=0, per=0):
            return no_less(i * (per // 2) + ((ph.slot0 + s) // 2 + 1 + START["slot_read"]))
        def before(ph, kind, of):
            return sum(of(p) for p in phases[:phases.index(ph)] if p.kind == kind)

        def gb_used(ph):
            return before(ph, "attn", lambda p: PAIRS * p.st.nch)

        def av_turn(ph):
            r = ph.st.round_of(ph.st.blocks)
            assert r % 2 == 0 and ph.av0 % 2 == 0 and ph.slot0 % 2 == 0 and ph.tile0 % 2 == 0
            return r

        def x_of(ph):
            return xc if ph.st is CTXS and ph.layer > 0 else xs

        def x_made(ph):
            made = next(p for p in phases if (p.kind, p.st, p.layer) == ("wout", LAT, ph.layer - 1))
            return (made.slot0 + KT * made.st.nch) // 2 + START["slot_read"]

        def s_of(ph):
            return 0 if ph.st.lat else 1

        def by_pair(eng, turn):
            with eng.Fori(0, KV_HEADS) as g:
                with eng.Fori(0, PAIRS // KV_HEADS) as j:
                    turn(g * (PAIRS // KV_HEADS) + j, g)

        @block.sync
        def _(sp):
            def load_tile(ph, j, src, i=0, per=0):
                n = ph.tile0 + j
                sp.wait_ge(sem["w_lo"], no_less(i * per + (n - 1)))
                dst = raw[:, n % 2, :].rearrange("p (k n) -> p k n", k=src.shape[1])
                sp.dma_start(dst, src).then_inc(raw_in[n % 2], 16)

            place_reg = sp.alloc_register("place")

            def place(value, size):
                sp.reg_mov(place_reg, value * (4 * size))
                return value

            def cols(w, layer, col, n=P):
                if type(col) is not int:
                    place(col, 1)
                return w[layer][:, :, bass.ds(col, n)]

            rows = 0
            for src in (c, c_ctx.rearrange("(a n) -> a n", a=1), norm_w, b_mod,
                        conv_w.rearrange("l k n -> (l k) n"),
                        final_norm_w.rearrange("(a n) -> a n", a=1)):
                r = src.rearrange("a (k p) -> (a k) p", p=P)
                sp.dma_start(vec_rows[rows:rows + r.shape[0], :], r).then_inc(vec_in, 16)
                rows += r.shape[0]
            assert rows == V_ALL
            sp.dma_start(sink[:], attn_sink.rearrange("(a l) h -> a (l h)", a=1)
                         .to_broadcast([P, DEPTH * HEADS])).then_inc(tab_in, 16)
            sp.dma_start(cos_s[:], cos_t).then_inc(tab_in, 16)
            sp.dma_start(sin_s[:], sin_t).then_inc(tab_in, 16)

            for ph in phases:
                L, st = ph.layer, ph.st
                if ph.kind == "mod":
                    sp.wait_ge(sem["ml_ready"], at("ml_ready", ph))
                    for g in range(MODS // MOD_GROUP):
                        sp.wait_ge(sem["mod_mm"], at("mod_mm", ph, g - 1))
                        sp.dma_start(wm[:, g % 2],
                                     cols(w_mod_v, L, g * MOD_GROUP * P, MOD_GROUP * P))\
                            .then_inc(wm_in[g % 2], 16)
                elif ph.kind == "load" and L == 0:
                    src = (x[0] if st.lat else ctx[0]).rearrange("(b p) n -> b p n", p=P)
                    sp.wait_ge(sem["m_done"], at("m_done", ph))
                    for b in range(st.blocks):
                        sp.wait_ge(sem["xt_mm"], at("xt_mm", ph, 2 * (b - 1)))
                        sp.dma_start(x_rows[:, b % 2], src[b]).then_inc(xr_in[b % 2], 16)
                elif ph.kind == "load":
                    sp.wait_ge(ctx_kept, 16)
                    sp.wait_ge(sem["m_done"], at("m_done", ph))
                    sp.dma_start(xc[:], ctx_keep).then_inc(sem["xc_in"], 16)
                elif ph.kind == "norm" and spills(st, L):
                    if L == 0:
                        sp.wait_ge(sem["xt_copied"], at("xt_copied", ph))
                    elif st is CTXS:
                        sp.wait_ge(sem["xc_in"], at("xc_in", ph))
                    else:
                        for b in range(2):
                            sp.wait_ge(slot_read[b], x_made(ph))
                    sp.dma_start(x_keep[:, :, 0:st.T], xs[:, :, 0:st.T])\
                        .then_inc(sem["x_spilled"], 16)
                elif ph.kind == "kv":
                    load_tile(ph, 0, cols(w_in_v, L, C_K))
                    load_tile(ph, 1, cols(w_in_v, L, C_V))
                elif ph.kind == "attn":
                    with sp.Fori(0, PAIRS) as i:
                        load_tile(ph, 0, cols(w_in_v, L, i * P + C_Q), i, 4)
                        load_tile(ph, 1, cols(w_in_v, L, i * P + C_ZB), i, 4)
                        load_tile(ph, 2, cols(w_in_v, L, i * (2 * P) + C_GB), i, 4)
                        load_tile(ph, 3, cols(w_in_v, L, i * (2 * P) + (C_GB + P)), i, 4)
                elif ph.kind == "mixb":
                    for t in range(2):
                        load_tile(ph, t, cols(w_b_v, L, 2 * t * P, 2 * P))
                    for b in range(2):
                        sp.wait_ge(gb_out[b], START["gb_out"] + 16 * gb_used(ph))
                    sp.wait_ge(sem["yb_done"], at("yb_done", ph))
                    for d in range(KT):
                        for s in ((d - 1) * st.nch - 1, (d - 1) * st.nch - 2):
                            sp.wait_ge(slot_read[bank(ph, s)], reads_at(ph, s))
                        sp.dma_start(tgb[:, d % 2, 0:st.T], gb_keep[d][:, 0:st.T])\
                            .then_inc(gb_in[d % 2], 16)
                        if d in (1, 2):
                            load_tile(ph, d + 1, cols(w_b_v, L, 2 * (d + 1) * P, 2 * P))
                elif ph.kind == "conv":
                    with sp.Fori(0, CT) as i:
                        for j, col in enumerate((C_C, C_U, C_Z, C_B)):
                            load_tile(ph, j, cols(w_in_v, L, i * P + col), i, 4)
                elif ph.kind == "mixa":
                    with sp.Fori(0, 2) as i:
                        for h in range(2):
                            for e in range(2):
                                load_tile(ph, 3 * h + e,
                                          cols(w_in_v, L, i * (4 * P) + (C_GA + (2 * h + e) * P)),
                                          i, 6)
                            load_tile(ph, 3 * h + 2,
                                      cols(w_a_v, L, i * (4 * P) + 2 * h * P, 2 * P), i, 6)
                elif ph.kind == "wout":
                    sp.wait_ge(sem["mm_done"], slots_at(ph, -1))
                    sp.wait_ge(sem["x_spilled"], at("x_spilled", ph))
                    sp.dma_start(xs[:, :, 0:st.T], x_keep[:, :, 0:st.T]).then_inc(sem["x_in"], 16)
                    with sp.Fori(0, KT // 2) as i:
                        for j in range(2):
                            load_tile(ph, j, cols(w_o_v, L, i * (2 * P) + j * P), i, 2)
                    if not st.lat:
                        for s in range(KT * st.nch - 2, KT * st.nch):
                            sp.wait_ge(slot_read[bank(ph, s)], reads_at(ph, s))
                        sp.dma_start(ctx_keep, xs[:, :, 0:CTX]).then_inc(ctx_kept, 16)
                elif ph.kind == "final":
                    out_v = out[0].rearrange("(b p) n -> b p n", p=P)
                    for b in range(SEQ // P):
                        sp.wait_ge(out_left, b + 1)
                        sp.wait_ge(out_right, b + 1)
                        sp.dma_start(out_v[b], o_rows[:, b % 2]).then_inc(out_sent[b % 2], 16)
                    for b in range(2):
                        sp.wait_ge(out_sent[b], 16 * (SEQ // P // 2))

        @block.gpsimd
        def _(pool):
            for t, value in ((ident, 0.0), (ident_b, 0.0), (mask_prev, 0.0), (mask_next, 0.0),
                             (ones, 1.0), (eps, EPS)):
                pool.memset(t[:], value).then_inc(const_ready, 1)
            started = [(sem[n], v) for n, v in START.items() if n in sem]
            started += [(s, START["slot_read"]) for s in slot_read]
            started += [(s, START["av_done"]) for s in av_done]
            started += [(s, START["gb_out"]) for s in gb_out]
            for at_, (s, v) in enumerate(started):
                pool.memset(head_start[:, at_:at_ + 1], 0.0).then_inc(s, v)
            pool.wait_ge(const_ready, 6)
            for mat in (ident, ident_b):
                pool.affine_select(out=mat[:], in_=mat[:], compare_op=ALU.not_equal, fill=1.0, base=0,
                                   pattern=[[-1, P]], channel_multiplier=1).then_inc(const_ready, 1)
            pool.affine_select(out=mask_prev[:], in_=mask_prev[:], compare_op=ALU.is_ge, fill=NEG,
                               base=0, pattern=[[1, BLK]], channel_multiplier=-1)\
                .then_inc(const_ready, 1)
            pool.affine_select(out=mask_next[:], in_=mask_next[:], compare_op=ALU.is_ge, fill=NEG,
                               base=0, pattern=[[-1, BLK]], channel_multiplier=1)\
                .then_inc(const_ready, 1)

            def low_part(n, i=0, per=0):
                pool.wait_ge(sem["w_hi"], no_less(i * per + (n + 1)))
                pool.tensor_tensor(wL[:, n % 2, :], raw[:, n % 2, :], wH[:, n % 2, :].bitcast(F32),
                                   ALU.subtract).then_inc(sem["w_lo"], 1)

            def rope_sin(ph, n, i=0, per=0):
                off, w = ph.st.chunks[n]
                pool.wait_ge(sem["rope_shuf"], at("rope_shuf", ph, n + 1, i, per))
                pool.tensor_tensor(rsh[:, 0:w], rsh[:, 0:w], sin_s[:, off:off + w], ALU.mult)\
                    .then_inc(sem["rope_sin"], 1)

            low_part(0)
            low_part(1)
            pool.wait_ge(tab_in, 48)
            for ph in phases:
                st, n = ph.st, ph.st.nch if ph.st else 0
                if ph.kind == "norm":
                    for r, (c_, k) in enumerate((c_, k) for c_ in range(n) for k in range(KT)):
                        off, w = st.chunks[c_]
                        pool.wait_ge(sem["hh_ready"], at("hh_ready", ph, r + 1))
                        pool.tensor_tensor(hL[:, k, off:off + w], hf[:, r % 2, 0:w],
                                           hH[:, k, off:off + w].bitcast(F32), ALU.subtract)\
                            .then_inc(sem["hl_ready"], 1)
                elif ph.kind == "kv":
                    if st.lat:
                        for c_ in range(n):
                            rope_sin(ph, c_)
                    low_part(ph.tile0 + 2)
                    low_part(ph.tile0 + 3)
                elif ph.kind == "attn":
                    def pool_pair(i, g, ph=ph, st=st, n=n):
                        if st.lat:
                            for c_ in range(n):
                                rope_sin(ph, c_, i, n)
                        low_part(ph.tile0 + 2, i, 4)
                        for b, parts in enumerate(fills(st)):
                            for t, c_ in slots_done(parts):
                                if c_ == n - 1:
                                    low_part(ph.tile0 + 3 + t, i, 4)
                    by_pair(pool, pool_pair)
                elif ph.kind in ("mixb", "conv", "mixa", "wout"):
                    turns, per = {"mixb": (2, 2), "conv": (CT, 4), "mixa": (2, 6),
                                  "wout": (KT // 2, 2)}[ph.kind]
                    if ph.tile0 + turns * per == n_tiles:
                        turns -= 1
                    with pool.Fori(0, turns) as i:
                        for j in range(per):
                            low_part(ph.tile0 + j + 2, i, per)

        @block.scalar
        def _(act):
            def high_part(ph, j, i=0):
                n, body = ph.tile0 + j + 2, BODY[ph.kind]
                if j >= 0:
                    act.wait_ge(sem["mm_done"],
                                slots_at(ph, sum(body[:j + 1]) * ph.st.nch - 1, i, sum(body) * ph.st.nch))
                act.wait_ge(raw_in[n % 2], no_less(i * (len(body) // 2 * 16) + 16 * (n // 2 + 1)))
                act.activation(wH[:, n % 2, :], raw[:, n % 2, :], ACT.Copy)\
                    .then_inc(sem["w_hi"], 1)

            act.preload_act_table(ACT.Exp)
            act.wait_ge(vec_ready, 1)
            act.activation(silu_t[:], vec[:, 0:2 * KT], ACT.Tanh, scale=0.5).then_inc(silu_tanh, 1)
            first_kv = next(p for p in phases if p.kind == "kv")
            high_part(first_kv, -2)
            high_part(first_kv, -1)
            for ph in phases:
                L, st, n = ph.layer, ph.st, ph.st.nch if ph.st else 0
                if ph.kind in ("norm", "final"):
                    src = x_of(ph)
                    if L == 0:
                        act.wait_ge(sem["xt_copied"], at("xt_copied", ph))
                    elif st is CTXS:
                        act.wait_ge(sem["xc_in"], at("xc_in", ph))
                    else:
                        for b in range(2):
                            act.wait_ge(slot_read[b], x_made(ph))
                    act.wait_ge(sem["stack_lo"], at("stack_lo", ph))
                    act.wait_ge(sem["pt_copied"], at("pt_copied", ph))
                    act.wait_ge(sem["hl_ready"], at("hl_ready", ph))
                    for c_, (off, w) in enumerate(st.chunks):
                        for k in range(KT):
                            r = c_ * KT + k
                            act.wait_ge(sem["sq_used"], at("sq_used", ph, r - 1))
                            act.activation(sq[:, r % 2, 0:w], src[:, k, off:off + w], ACT.Square)\
                                .then_inc(sem["sq_ready"], 1)
                        act.wait_ge(sem["sq_used"], at("sq_used", ph, (c_ + 1) * KT))
                        act.activation(rms[:, c_, 0:w], pS[:, c_ * CH:c_ * CH + w], ACT.Sqrt,
                                       bias=eps[:, 0:1], scale=1.0 / D).then_inc(sem["rms_ready"], 1)
                    if ph.kind == "norm":
                        act.preload_act_table(ACT.Exp)
                        act.wait_ge(sem["mm_done"], slots_at(ph, -1))
                        for r, (c_, k) in enumerate((c_, k) for c_ in range(n) for k in range(KT)):
                            off, w = st.chunks[c_]
                            act.wait_ge(sem["hf_ready"], at("hf_ready", ph, r + 1))
                            act.activation(hH[:, k, off:off + w], hf[:, r % 2, 0:w], ACT.Copy)\
                                .then_inc(sem["hh_ready"], 1)
                    else:
                        for b in range(SEQ // P):
                            act.wait_ge(sem["pt_done"], at("pt_done", ph, 2 * b + 1))
                            act.wait_ge(out_sent[b % 2], no_less(16 * (b // 2)))
                            act.activation(o_rows[:, b % 2, 0:CH], pT[:, ph.round0 % 2, :], ACT.Copy)\
                                .then_inc(out_left, 1)
                elif ph.kind == "kv":
                    for c_, (off, w) in enumerate(st.chunks):
                        act.wait_ge(sem["mm_done"], slots_at(ph, c_))
                        act.wait_ge(sem["rope_out" if st.lat else "stack_lo"],
                                    at("rope_out" if st.lat else "stack_lo", ph, c_))
                        act.activation(rraw[:, 0:w], pp[:, bank(ph, c_), 0:w], ACT.Copy)\
                            .then_inc(slot_read[bank(ph, c_)], 1)
                        if st.lat:
                            act.wait_ge(sem["rope_out"], at("rope_out", ph, c_ + 1))
                        else:
                            act.wait_ge(slot_read[bank(ph, c_)], reads_at(ph, c_))
                        r = rout if st.lat else rraw
                        cols = slice(st.key0 + off, st.key0 + off + w)
                        for g in range(KV_HEADS):
                            for half in (0, HD):
                                last = act.activation(kH[half:half + HD, g, cols],
                                                      r[g * HD:(g + 1) * HD, 0:w], ACT.Copy)
                        last.then_inc(sem["stack_hi"], 1)
                    high_part(ph, 0)
                    for c_, (off, w) in enumerate(st.chunks):
                        s = n + c_
                        act.wait_ge(sem["mm_done"], slots_at(ph, s))
                        act.wait_ge(sem["pt_done"], at("pt_done", ph, c_))
                        act.activation(vraw[:, 0:w], pp[:, bank(ph, s), 0:w], ACT.Copy)\
                            .then_inc(slot_read[bank(ph, s)], 1)
                        act.wait_ge(sem["pt_done"], at("pt_done", ph, c_ + 1))
                        t0, nt = (st.key0 + off) // BLK, w // BLK
                        act.activation(v_all[:, t0:t0 + nt, :, 0:HD],
                                       pT[:, (ph.round0 + c_) % 2, 0:w]
                                       .rearrange("p (t g d) -> p t g d", t=nt, g=KV_HEADS),
                                       ACT.Copy).then_inc(sem["pt_hi"], 1)
                    high_part(ph, 1)
                elif ph.kind == "attn":
                    nb, R, steps = st.blocks, av_turn(ph), fills(st)
                    act.wait_ge(sem["x_spilled"], at("x_spilled", ph))

                    def act_pair(i, g, ph=ph, st=st, n=n, nb=nb, R=R, steps=steps):
                        for c_, (off, w) in enumerate(st.chunks):
                            act.wait_ge(sem["mm_done"], slots_at(ph, c_, i, 4 * n))
                            if st.lat:
                                act.wait_ge(sem["rope_out"], at("rope_out", ph, c_, i, n))
                            else:
                                act.wait_ge(sem["stack_lo"], at("stack_lo", ph, c_, i, n))
                            act.activation(rraw[:, 0:w], pp[:, bank(ph, c_), 0:w], ACT.Copy)\
                                .then_inc(slot_read[bank(ph, c_)], 1)
                            if st.lat:
                                act.wait_ge(sem["rope_out"], at("rope_out", ph, c_ + 1, i, n))
                            else:
                                act.wait_ge(slot_read[bank(ph, c_)], reads_at(ph, c_, i, 4 * n))
                            act.wait_ge(sem["qk_done"], at("qk_done", ph, 0, i, nb))
                            r = rout if st.lat else rraw
                            act.activation(q_st[0:HD, 0, off:off + w], r[0:HD, 0:w], ACT.Copy)
                            act.activation(q_st[HD:P, 1, off:off + w], r[HD:P, 0:w], ACT.Copy)\
                                .then_inc(sem["stack_hi"], 1)
                        high_part(ph, 0, i)

                        def pt_high(b, r):
                            rr = st.round_of(b) + r
                            w = len(st.rounds(b)[r]) * 2 * BLK
                            act.wait_ge(sem["pt_done"], at("pt_done", ph, rr + 1, i, R))
                            act.wait_ge(av_done[rr % 2],
                                        no_less(i * (R // 2) + (START["av_done"] + ph.av0 // 2 + rr // 2)))
                            act.activation(ptH[:, rr % 2, 0:w], pT[:, (ph.round0 + rr) % 2, 0:w],
                                           ACT.Copy).then_inc(sem["pt_hi"], 1)

                        def side_slot(t, c_):
                            off, w = st.chunks[c_]
                            s = (t + 1) * n + c_
                            pb = bank(ph, s)
                            act.wait_ge(sem["mm_done"], slots_at(ph, s, i, 4 * n))
                            if t == 0:
                                act.wait_ge(slot_read[bank(ph, s - 1 if c_ else -2 * n - 1)],
                                            reads_at(ph, s - 1 if c_ else -2 * n - 1, i, 4 * n))
                                act.activation(th[:, 0:w], pp[:, pb, 0:w], ACT.Tanh, scale=0.5)\
                                    .then_inc(sem["gate_tanh"], 1)
                            else:
                                u = (t - 1) * n + c_
                                buf, used = u % 2, u // 2
                                act.wait_ge(gb_out[buf],
                                            i * (16 * n) + (START["gb_out"] + 16 * (gb_used(ph) + used)))
                                act.activation(gst[:, buf, 0:w], pp[:, pb, 0:w], ACT.Tanh, scale=0.5)\
                                    .then_inc(slot_read[pb], 1)
                                act.wait_ge(slot_read[bank(ph, s)], reads_at(ph, s, i, 4 * n))
                                act.dma_start(gb_keep[i * 2 + (t - 1)][:, off:off + w],
                                              gst[:, buf, 0:w]).then_inc(gb_out[buf], 16)
                            if c_ == n - 1:
                                high_part(ph, 1 + t, i)

                        for b, parts in enumerate(steps):
                            rounds = len(st.rounds(b - 1)) if b else 0
                            for r in range(min(rounds, 2)):
                                pt_high(b - 1, r)
                            if b < nb:
                                free = st.round_of(b - 1) if b else -len(st.rounds(nb - 1))
                                act.wait_ge(sem["sinkin_ready"],
                                            at("sinkin_ready", ph, b + 1, i, nb))
                                act.activation(sinkexp[:, b % 2, :], sinkin[:, b % 2, :], ACT.Exp)
                                act.wait_ge(sem["pt_done"], at("pt_done", ph, free, i, R))
                                W = len(st.key_tiles(b)) * BLK
                                for h in range(2):
                                    act.activation(prob[:, b % 2, h, 0:W], pS[:, h * W:(h + 1) * W],
                                                   ACT.Exp, bias=negm[:, b % 2, h:h + 1], scale=SCALE,
                                                   accum_out=rsum[:, b % 2, h:h + 1])\
                                        .then_inc(sem["exp_done"], 1)
                            for t, c_ in slots_done(parts[:2]):
                                side_slot(t, c_)
                            for r in range(2, rounds):
                                pt_high(b - 1, r)
                            for t, c_ in slots_done(parts[2:]):
                                side_slot(t, c_)
                            if b:
                                rr = st.round_of(b) - 1
                                act.wait_ge(av_done[rr % 2],
                                            no_less(i * (R // 2) + (START["av_done"] + ph.av0 // 2 + rr // 2 + 1)))
                                act.wait_ge(sem["att_done"], at("att_done", ph, b - 1, i, nb))
                                act.activation(o_half[:], pO[HD:P, 0:2 * BLK], ACT.Copy)\
                                    .then_inc(sem["att_half"], 1)
                    by_pair(act, act_pair)
                elif ph.kind == "mixb":
                    act.wait_ge(sem["yb_done"], at("yb_done", ph))
                    for k in range(CT):
                        act.activation(yH[:, k, 0:st.T], yb[st.name][:, k, :], ACT.Copy)\
                            .then_inc(sem["y_hi"], 1)
                    with act.Fori(0, 2) as i:
                        for j in range(2):
                            high_part(ph, j, i)
                elif ph.kind == "conv":
                    act.wait_ge(sem["mm_done"], slots_at(ph, -1))
                    act.wait_ge(sem["y_lo"], at("y_lo", ph))
                    with act.Fori(0, CT) as i:
                        for c_, (off, w) in enumerate(st.chunks):
                            act.wait_ge(sem["mm_done"], slots_at(ph, c_, i, 4 * n))
                            act.wait_ge(sem["y_lo"], at("y_lo", ph, 0, i, n))
                            act.activation(cb[st.name][:, off:off + w], pp[:, bank(ph, c_), 0:w],
                                           ACT.Copy).then_inc(slot_read[bank(ph, c_)], 1)
                        high_part(ph, 0, i)
                        high_part(ph, 1, i)
                        for c_, (off, w) in enumerate(st.chunks):
                            s = 2 * n + c_
                            act.wait_ge(sem["mm_done"], slots_at(ph, s, i, 4 * n))
                            if c_:
                                act.wait_ge(slot_read[bank(ph, s - 1)],
                                            reads_at(ph, s - 1, i, 4 * n))
                            act.activation(th[:, 0:w], pp[:, bank(ph, s), 0:w], ACT.Tanh, scale=0.5)\
                                .then_inc(sem["gate_tanh"], 1)
                        high_part(ph, 2, i)
                        for c_, (off, w) in enumerate(st.chunks):
                            act.wait_ge(slot_read[bank(ph, 3 * n + c_)],
                                        reads_at(ph, 3 * n + c_, i, 4 * n))
                            act.activation(yH[:, i, off:off + w], yv[:, c_, 0:w], ACT.Copy)\
                                .then_inc(sem["y_hi"], 1)
                        high_part(ph, 3, i)
                elif ph.kind == "mixa":
                    act.wait_ge(sem["y_lo"], at("y_lo", ph))
                    with act.Fori(0, 2) as i:
                        for h in range(2):
                            for e in range(2):
                                for c_, (off, w) in enumerate(st.chunks):
                                    s = (4 * h + e) * n + c_
                                    act.wait_ge(sem["mm_done"], slots_at(ph, s, i, 8 * n))
                                    act.wait_ge(sem["m_done"],
                                                at("m_done", ph, 2 * h * n, i, 4 * n))
                                    act.activation(tga[:, e, off:off + w], pp[:, bank(ph, s), 0:w],
                                                   ACT.Tanh, scale=0.5)\
                                        .then_inc(slot_read[bank(ph, s)], 1)
                                high_part(ph, 3 * h + e, i)
                            high_part(ph, 3 * h + 2, i)
                elif ph.kind == "wout":
                    act.wait_ge(sem["m_done"], at("m_done", ph))
                    act.wait_ge(sem["mm_done"], slots_at(ph, -1))
                    for k in range(KT):
                        act.activation(hH[:, k, 0:st.T], m[st.name][:, k, :], ACT.Copy)\
                            .then_inc(sem["mh_ready"], 1)
                    turns = KT // 2 - (ph.tile0 + KT == n_tiles)
                    with act.Fori(0, turns) as i:
                        for j in range(2):
                            high_part(ph, j, i)

        @block.vector
        def _(dve):
            def rope(ph, n, i=0, turn=0, slots=0):
                off, w = ph.st.chunks[n]
                dve.wait_ge(sem["stack_lo"], at("stack_lo", ph, n, i, turn))
                dve.wait_ge(slot_read[bank(ph, n)], reads_at(ph, n, i, slots))
                dve.tensor_tensor(rout[:, 0:w], rraw[:, 0:w], cos_s[:, off:off + w], ALU.mult)\
                    .then_inc(sem["rope_cos"], 1)
                dve.stream_shuffle(rsh[:, 0:w], rraw[:, 0:w], list(range(16, 32)) + list(range(16)))\
                    .then_inc(sem["rope_shuf"], 1)
                dve.wait_ge(sem["rope_cos"], at("rope_cos", ph, n + 1, i, turn))
                dve.wait_ge(sem["rope_sin"], at("rope_sin", ph, n + 1, i, turn))
                dve.tensor_tensor(rout[:, 0:w], rout[:, 0:w], rsh[:, 0:w], ALU.add)\
                    .then_inc(sem["rope_out"], 1)

            dve.wait_ge(vec_mm, 1)
            dve.tensor_copy(vec[:], pO[:, 0:V_ALL]).then_inc(vec_ready, 1)
            dve.wait_ge(tab_in, 48)
            dve.tensor_scalar(nsink[:], sink[:], -1.0, None, ALU.mult).then_inc(nsink_ready, 1)
            dve.wait_ge(vec_ready, 1)
            dve.wait_ge(silu_tanh, 1)
            dve.scalar_tensor_tensor(
                out=silu_c[:].rearrange("p (k s) -> p s k", s=2),
                in0=silu_t[:].rearrange("p (s k) -> p s k", s=2), scalar=1.0,
                in1=vec[:, 0:2 * KT].rearrange("p (s k) -> p s k", s=2),
                op0=ALU.add, op1=ALU.mult).then_inc(silu_ready, 1)
            dve.wait_ge(nsink_ready, 1)

            for ph in phases:
                L, st, n = ph.layer, ph.st, ph.st.nch if ph.st else 0
                s_ = s_of(ph) if st else 0
                if ph.kind == "mod":
                    dve.wait_ge(sem["mod_mm"], at("mod_mm", ph, MODS // MOD_GROUP))
                    for s in (-2, -1):
                        dve.wait_ge(slot_read[bank(ph, s)], reads_at(ph, s))
                    for s in range(2):
                        last = dve.scalar_tensor_tensor(
                            out=modv[:, :, s],
                            in0=pS[:, 0:2 * MODS].rearrange("p (t s) -> p t s", s=2)[:, :, s],
                            scalar=0.5, in1=vec[:, V_BM + L * MODS:V_BM + (L + 1) * MODS],
                            op0=ALU.mult, op1=ALU.add)
                    last.then_inc(sem["modv_ready"], 1)
                    dve.wait_ge(sem["modv_ready"], at("modv_ready", ph, 1))
                    dve.tensor_scalar(modv[:, 2 * KT:3 * KT, :], modv[:, 2 * KT:3 * KT, :], 0.25,
                                      None, ALU.mult)
                    for s in range(2):
                        last = dve.scalar_tensor_tensor(
                            out=mod_a[:, :, s], in0=modv[:, KT:2 * KT, s], scalar=1.0,
                            in1=vec[:, V_NW + L * KT:V_NW + (L + 1) * KT],
                            op0=ALU.add, op1=ALU.mult)
                    last.then_inc(sem["mod_done"], 1)
                    dve.wait_ge(sem["mod_done"], at("mod_done", ph, 1))
                elif ph.kind == "load" and L == 0:
                    dve.wait_ge(sem["mm_done"], slots_at(ph, -1))
                    for b in range(st.blocks):
                        for h in range(2):
                            dve.wait_ge(sem["xt_mm"], at("xt_mm", ph, 2 * b + h + 1))
                            dve.tensor_copy(xs[:, 4 * h:4 * h + 4, b * P:(b + 1) * P],
                                            pT[:, (ph.round0 + h) % 2, :]
                                            .rearrange("p (k t) -> p k t", k=4))\
                                .then_inc(sem["xt_copied"], 1)
                elif ph.kind in ("norm", "final"):
                    src = x_of(ph)
                    if L == 0:
                        dve.wait_ge(sem["xt_copied"], at("xt_copied", ph))
                    elif st is CTXS:
                        dve.wait_ge(sem["xc_in"], at("xc_in", ph))
                    else:
                        for b in range(2):
                            dve.wait_ge(slot_read[b], x_made(ph))
                    for c_, (off, w) in enumerate(st.chunks):
                        dve.wait_ge(sem["rms_ready"], at("rms_ready", ph, c_ + 1))
                        dve.reciprocal(rms[:, c_, 0:w], rms[:, c_, 0:w])\
                            .then_inc(sem["rstd_ready"], 1)
                        dve.wait_ge(sem["rstd_ready"], at("rstd_ready", ph, c_ + 1))
                        for k in range(KT):
                            r = c_ * KT + k
                            if ph.kind == "final":
                                dve.scalar_tensor_tensor(
                                    out=xs[:, k, off:off + w], in0=xs[:, k, off:off + w],
                                    scalar=vec[:, V_FN + k:V_FN + k + 1], in1=rms[:, c_, 0:w],
                                    op0=ALU.mult, op1=ALU.mult).then_inc(sem["hn_ready"], 1)
                                continue
                            dve.scalar_tensor_tensor(
                                out=hn[:, r % 2, 0:w], in0=src[:, k, off:off + w],
                                scalar=mod_a[:, k, s_:s_ + 1], in1=rms[:, c_, 0:w],
                                op0=ALU.mult, op1=ALU.mult).then_inc(sem["hn_ready"], 1)
                            dve.wait_ge(sem["hn_ready"], at("hn_ready", ph, r + 1))
                            dve.wait_ge(sem["hl_ready"], at("hl_ready", ph, r - 1))
                            dve.tensor_scalar(hf[:, r % 2, 0:w], hn[:, r % 2, 0:w],
                                              modv[:, k, s_:s_ + 1], None, ALU.add)\
                                .then_inc(sem["hf_ready"], 1)
                    if ph.kind == "final":
                        for b in range(SEQ // P):
                            dve.wait_ge(sem["pt_done"], at("pt_done", ph, 2 * b + 2))
                            dve.wait_ge(out_sent[b % 2], no_less(16 * (b // 2)))
                            dve.tensor_copy(o_rows[:, b % 2, CH:D], pT[:, (ph.round0 + 1) % 2, :])\
                                .then_inc(out_right, 1)
                elif ph.kind == "kv":
                    for c_, (off, w) in enumerate(st.chunks):
                        if st.lat:
                            rope(ph, c_)
                            dve.wait_ge(sem["rope_out"], at("rope_out", ph, c_ + 1))
                        r = rout if st.lat else rraw
                        cols = slice(st.key0 + off, st.key0 + off + w)
                        dve.wait_ge(sem["stack_hi"], at("stack_hi", ph, c_ + 1))
                        for g in range(KV_HEADS):
                            own = slice(g * HD, (g + 1) * HD)
                            for half in (0, HD):
                                last = dve.tensor_tensor(kL[half:half + HD, g, cols], r[own, 0:w],
                                                         kH[own, g, cols].bitcast(F32), ALU.subtract)
                        last.then_inc(sem["stack_lo"], 1)
                    for c_, (off, w) in enumerate(st.chunks):
                        t0, nt = (st.key0 + off) // BLK, w // BLK
                        dve.wait_ge(sem["pt_hi"], at("pt_hi", ph, c_ + 1))
                        dve.tensor_tensor(v_all[:, t0:t0 + nt, :, HD:P],
                                          pT[:, (ph.round0 + c_) % 2, 0:w]
                                          .rearrange("p (t g d) -> p t g d", t=nt, g=KV_HEADS),
                                          v_all[:, t0:t0 + nt, :, 0:HD].bitcast(F32), ALU.subtract)\
                            .then_inc(sem["pt_copied"], 1)
                elif ph.kind == "attn":
                    nb, R, steps = st.blocks, av_turn(ph), fills(st)

                    def dve_pair(i, g, ph=ph, L=L, st=st, n=n, nb=nb, R=R, steps=steps):
                        for b in range(2):
                            dve.wait_ge(av_done[b], i * (R // 2) + (START["av_done"] + ph.av0 // 2))
                        dve.wait_ge(sem["pt_copied"], at("pt_copied", ph, 0, i, R))
                        mine = slice(st.key_tiles(0)[0], TOK // BLK)
                        dve.tensor_scalar(v_cur[:, mine], v_all[:, mine, g, :].bitcast(F32), 1.0,
                                          None, ALU.mult).then_inc(sem["vcur_ready"], 1)
                        for c_, (off, w) in enumerate(st.chunks):
                            if st.lat:
                                rope(ph, c_, i, n, 4 * n)
                                dve.wait_ge(sem["rope_out"], at("rope_out", ph, c_ + 1, i, n))
                            r = rout if st.lat else rraw
                            dve.wait_ge(sem["stack_hi"], at("stack_hi", ph, c_ + 1, i, n))
                            dve.tensor_tensor(q_st[HD:P, 0, off:off + w], r[0:HD, 0:w],
                                              q_st[0:HD, 0, off:off + w].bitcast(F32), ALU.subtract)
                            dve.tensor_tensor(q_st[0:HD, 1, off:off + w], r[HD:P, 0:w],
                                              q_st[HD:P, 1, off:off + w].bitcast(F32), ALU.subtract)\
                                .then_inc(sem["stack_lo"], 1)

                        def pt_low(b, r):
                            rr = st.round_of(b) + r
                            w = len(st.rounds(b)[r]) * 2 * BLK
                            dve.wait_ge(sem["pt_hi"], at("pt_hi", ph, rr + 1, i, R))
                            dve.tensor_tensor(ptL[:, rr % 2, 0:w], pT[:, (ph.round0 + rr) % 2, 0:w],
                                              ptH[:, rr % 2, 0:w].bitcast(F32), ALU.subtract)\
                                .then_inc(sem["pt_copied"], 1)

                        def side_slot(t, c_):
                            if t:
                                return
                            off, w = st.chunks[c_]
                            dve.wait_ge(sem["gate_tanh"], at("gate_tanh", ph, c_ + 1, i, n))
                            dve.scalar_tensor_tensor(out=szb[:, off:off + w], in0=th[:, 0:w],
                                                     scalar=1.0, in1=pp[:, bank(ph, n + c_), 0:w],
                                                     op0=ALU.add, op1=ALU.mult)\
                                .then_inc(slot_read[bank(ph, n + c_)], 1)

                        for b, parts in enumerate(steps):
                            rounds = len(st.rounds(b - 1)) if b else 0
                            par = b % 2
                            if b < nb:
                                W = len(st.key_tiles(b)) * BLK
                                heads = bass.ds(i * 2 + L * HEADS, 2)
                                dve.wait_ge(sem["qk_done"], at("qk_done", ph, b + 1, i, nb))
                                dve.tensor_reduce(mx[:, par, :],
                                                  pS[:, 0:2 * W].rearrange("p (h w) -> p h w", h=2),
                                                  AX.X, ALU.max).then_inc(sem["max_ready"], 1)
                                dve.wait_ge(sem["max_ready"], at("max_ready", ph, b + 1, i, nb))
                                dve.scalar_tensor_tensor(out=negm[:, par, :], in0=mx[:, par, :],
                                                         scalar=-SCALE, in1=nsink[:, heads],
                                                         op0=ALU.mult, op1=ALU.min)\
                                    .then_inc(sem["negm_ready"], 1)
                                dve.wait_ge(sem["negm_ready"], at("negm_ready", ph, b + 1, i, nb))
                                dve.tensor_tensor(sinkin[:, par, :], negm[:, par, :], sink[:, heads],
                                                  ALU.add).then_inc(sem["sinkin_ready"], 1)
                            for r in range(min(rounds, 2)):
                                pt_low(b - 1, r)
                            if b < nb:
                                for h in range(2):
                                    one = (slice(None), par, slice(h, h + 1))
                                    dve.wait_ge(sem["exp_done"],
                                                at("exp_done", ph, 2 * b + h + 1, i, 2 * nb))
                                    dve.tensor_tensor(rsum[one], rsum[one], sinkexp[one], ALU.add)\
                                        .then_inc(sem["den_ready"], 1)
                                    dve.wait_ge(sem["den_ready"],
                                                at("den_ready", ph, 2 * b + h + 1, i, 2 * nb))
                                    dve.reciprocal(rden[one], rsum[one])\
                                        .then_inc(sem["rden_ready"], 1)
                                for h in range(2):
                                    pr = prob[:, par, h, 0:W]
                                    dve.wait_ge(sem["rden_ready"],
                                                at("rden_ready", ph, 2 * b + h + 1, i, 2 * nb))
                                    dve.tensor_scalar(pr, pr, rden[:, par, h:h + 1], None,
                                                      ALU.mult).then_inc(sem["p_ready"], 1)
                            for t, c_ in slots_done(parts[:2]):
                                side_slot(t, c_)
                            for r in range(2, rounds):
                                pt_low(b - 1, r)
                            for t, c_ in slots_done(parts[2:]):
                                side_slot(t, c_)
                            if b:
                                q = slice((b - 1) * BLK, b * BLK)
                                dve.wait_ge(sem["att_half"], at("att_half", ph, b, i, nb))
                                dve.tensor_tensor(att[0:HD, q], pO[0:HD, 0:BLK], o_half[:, 0:BLK],
                                                  ALU.add)
                                dve.tensor_tensor(att[HD:P, q], pO[0:HD, BLK:2 * BLK],
                                                  o_half[:, BLK:2 * BLK], ALU.add)\
                                    .then_inc(sem["att_done"], 1)
                        dve.wait_ge(sem["att_done"], at("att_done", ph, nb, i, nb))
                        for c_ in range(n):
                            dve.wait_ge(slot_read[bank(ph, n + c_)], reads_at(ph, n + c_, i, 4 * n))
                        dve.tensor_tensor(yb[st.name][:, i, 0:st.T], att[:, 0:st.T], szb[:, 0:st.T],
                                          ALU.mult).then_inc(sem["yb_done"], 1)
                        dve.wait_ge(sem["yb_done"], at("yb_done", ph, 1, i, 1))
                    by_pair(dve, dve_pair)
                elif ph.kind == "mixb":
                    for k in range(CT):
                        dve.wait_ge(sem["y_hi"], at("y_hi", ph, k + 1))
                        dve.tensor_tensor(yL[:, k, 0:st.T], yb[st.name][:, k, :],
                                          yH[:, k, 0:st.T].bitcast(F32), ALU.subtract)\
                            .then_inc(sem["y_lo"], 1)
                    loads = before(ph, "mixb", lambda p: 4)
                    with dve.Fori(0, 2) as i:
                        for d in range(4):
                            dve.wait_ge(gb_in[d % 2], no_less(i * 32 + 16 * (loads + d // 2 + 1)))
                            for c_, (off, w) in enumerate(st.chunks):
                                s = d * n + c_
                                dve.wait_ge(sem["mm_done"], slots_at(ph, s, i, 4 * n))
                                dve.scalar_tensor_tensor(
                                    out=m[st.name][:, i * 4 + d, off:off + w],
                                    in0=tgb[:, d % 2, off:off + w], scalar=1.0,
                                    in1=pp[:, bank(ph, s), 0:w], op0=ALU.add, op1=ALU.mult)\
                                    .then_inc(slot_read[bank(ph, s)], 1)
                elif ph.kind == "conv":
                    for s in (-2, -1):
                        dve.wait_ge(slot_read[bank(ph, s)], reads_at(ph, s))
                    dve.memset(cu[:, 0:1], 0.0)
                    dve.memset(cu[:, st.T + 1:st.T + 2], 0.0).then_inc(sem["halo_zero"], 1)
                    dve.wait_ge(sem["halo_zero"], at("halo_zero", ph, 1))
                    u, v = cb[st.name], cv[st.name]
                    with dve.Fori(0, CT) as i:
                        for c_, (off, w) in enumerate(st.chunks):
                            s = n + c_
                            dve.wait_ge(slot_read[bank(ph, c_)], reads_at(ph, c_, i, 4 * n))
                            dve.wait_ge(sem["mm_done"], slots_at(ph, s, i, 4 * n))
                            dve.wait_ge(sem["tap_done"], at("tap_done", ph, 0, i, 4))
                            dve.tensor_tensor(cu[:, 1 + off:1 + off + w], u[:, off:off + w],
                                              pp[:, bank(ph, s), 0:w], ALU.mult)\
                                .then_inc(slot_read[bank(ph, s)], 1)
                        for c_ in range(n):
                            dve.wait_ge(slot_read[bank(ph, n + c_)], reads_at(ph, n + c_, i, 4 * n))
                        for tap in range(CONV_K):
                            wt = vec[:, bass.ds(i + (V_CW + (L * CONV_K + tap) * CT), 1)]
                            if tap == 0:
                                dve.tensor_scalar(v[:, 0:st.T], cu[:, 0:st.T], wt, None, ALU.mult)\
                                    .then_inc(sem["tap_done"], 1)
                            else:
                                dve.scalar_tensor_tensor(
                                    out=v[:, 0:st.T], in0=cu[:, tap:tap + st.T], scalar=wt,
                                    in1=v[:, 0:st.T], op0=ALU.mult, op1=ALU.add)\
                                    .then_inc(sem["tap_done"], 1)
                            dve.wait_ge(sem["tap_done"], at("tap_done", ph, tap + 1, i, 4))
                        for c_, (off, w) in enumerate(st.chunks):
                            s = 2 * n + c_
                            dve.wait_ge(sem["gate_tanh"], at("gate_tanh", ph, c_ + 1, i, n))
                            dve.scalar_tensor_tensor(out=sz[st.name][:, off:off + w],
                                                     in0=th[:, 0:w], scalar=1.0,
                                                     in1=pp[:, bank(ph, s), 0:w],
                                                     op0=ALU.add, op1=ALU.mult)\
                                .then_inc(slot_read[bank(ph, s)], 1)
                        for c_ in range(n):
                            dve.wait_ge(slot_read[bank(ph, 2 * n + c_)],
                                        reads_at(ph, 2 * n + c_, i, 4 * n))
                        dve.tensor_tensor(v[:, 0:st.T], v[:, 0:st.T], sz[st.name][:, 0:st.T],
                                          ALU.mult).then_inc(sem["tap_done"], 1)
                        dve.wait_ge(sem["tap_done"], at("tap_done", ph, 4, i, 4))
                        for c_, (off, w) in enumerate(st.chunks):
                            s = 3 * n + c_
                            dve.wait_ge(sem["mm_done"], slots_at(ph, s, i, 4 * n))
                            dve.tensor_tensor(yv[:, c_, 0:w], v[:, off:off + w],
                                              pp[:, bank(ph, s), 0:w], ALU.mult)\
                                .then_inc(slot_read[bank(ph, s)], 1)
                            dve.wait_ge(slot_read[bank(ph, s)], reads_at(ph, s, i, 4 * n))
                            dve.wait_ge(sem["y_hi"], at("y_hi", ph, c_ + 1, i, n))
                            dve.tensor_tensor(yL[:, i, off:off + w], yv[:, c_, 0:w],
                                              yH[:, i, off:off + w].bitcast(F32), ALU.subtract)\
                                .then_inc(sem["y_lo"], 1)
                elif ph.kind == "mixa":
                    with dve.Fori(0, 2) as i:
                        for h in range(2):
                            for e in range(2):
                                for c_, (off, w) in enumerate(st.chunks):
                                    s = (4 * h + 2 + e) * n + c_
                                    q = (2 * h + e) * n + c_
                                    dve.wait_ge(slot_read[bank(ph, s - 2 * n)],
                                                reads_at(ph, s - 2 * n, i, 8 * n))
                                    dve.wait_ge(sem["mm_done"], slots_at(ph, s, i, 8 * n))
                                    dve.scalar_tensor_tensor(
                                        out=gm[:, q % 2, 0:w], in0=tga[:, e, off:off + w],
                                        scalar=1.0, in1=pp[:, bank(ph, s), 0:w],
                                        op0=ALU.add, op1=ALU.mult)\
                                        .then_inc(slot_read[bank(ph, s)], 1)
                                    dve.wait_ge(slot_read[bank(ph, s)], reads_at(ph, s, i, 8 * n))
                                    md = m[st.name][:, i * 4 + (2 * h + e), off:off + w]
                                    dve.tensor_tensor(md, md, gm[:, q % 2, 0:w], ALU.add)\
                                        .then_inc(sem["m_done"], 1)
                                    dve.wait_ge(sem["m_done"], at("m_done", ph, q + 1, i, 4 * n))
                elif ph.kind == "wout":
                    for k in range(KT):
                        dve.wait_ge(sem["mh_ready"], at("mh_ready", ph, k + 1))
                        dve.tensor_tensor(hL[:, k, 0:st.T], m[st.name][:, k, :],
                                          hH[:, k, 0:st.T].bitcast(F32), ALU.subtract)\
                            .then_inc(sem["ml_ready"], 1)
                    dve.wait_ge(sem["x_in"], at("x_in", ph, 16))
                    gates = modv[:].rearrange("p t s -> p (t s)")
                    with dve.Fori(0, KT // 2) as i:
                        for j in range(2):
                            for c_, (off, w) in enumerate(st.chunks):
                                s = j * n + c_
                                dve.wait_ge(sem["mm_done"], slots_at(ph, s, i, 2 * n))
                                xe = xs[:, i * 2 + j, off:off + w]
                                dve.scalar_tensor_tensor(
                                    out=xe, in0=pp[:, bank(ph, s), 0:w],
                                    scalar=gates[:, bass.ds(i * 4 + (4 * KT + 2 * j + s_), 1)],
                                    in1=xe, op0=ALU.mult, op1=ALU.add)\
                                    .then_inc(slot_read[bank(ph, s)], 1)

        @block.tensor
        def _(pe):
            def k_step(ph, j, s, c_, k, kts, a_hi, a_lo, e=0):
                off, w = ph.st.chunks[c_]
                wb = (ph.tile0 + j) % 2
                col = (k * (KT // kts) + e) * P
                o = pp[:, bank(ph, s), 0:w]
                hi, lo = wH[:, wb, col:col + P], wL[:, wb, col:col + P]
                ah, al = a_hi[:, k, off:off + w], a_lo[:, k, off:off + w]
                pe.matmul(o, hi, ah, start=(k == 0), stop=False)
                pe.matmul(o, hi, al, start=False, stop=False)
                return pe.matmul(o, lo, ah, start=False, stop=(k == kts - 1))

            def open_slot(ph, s, i=0, per=0):
                pe.wait_ge(slot_read[bank(ph, s - 2)], reads_at(ph, s - 2, i, per))

            def open_tile(ph, j, i=0, per=0):
                pe.wait_ge(sem["w_lo"], no_less(i * per + (ph.tile0 + j + 1)))

            def project(ph, j, s0, a_hi, a_lo, kts=KT, outs=1, i=0, tiles=0, slots=0, ready=None):
                open_tile(ph, j, i, tiles)
                n = ph.st.nch
                for e in range(outs):
                    for c_ in range(n):
                        s = s0 + e * n + c_
                        open_slot(ph, s, i, slots)
                        for k in range(kts):
                            if ready and e == 0 and c_ == 0:
                                pe.wait_ge(sem[ready], at(ready, ph, k + 1))
                            last = k_step(ph, j, s, c_, k, kts, a_hi, a_lo, e)
                            if k == kts - 1:
                                last.then_inc(sem["mm_done"], 1)

            def score_pieces(st, b, h):
                tiles = st.key_tiles(b)
                pieces, masks = [], []
                for t, kb in enumerate(tiles):
                    col = (h * len(tiles) + t) * BLK
                    if pieces and col % CH and pieces[-1][1] + pieces[-1][2] == kb * BLK:
                        pieces[-1][2] += BLK
                    else:
                        pieces.append([col, kb * BLK, BLK])
                    if st.lat and kb < st.blocks and kb != b:
                        masks.append((col, mask_prev if kb < b else mask_next))
                return pieces, masks

            pe.wait_ge(const_ready, 10)
            pe.wait_ge(vec_in, 16 * 6)
            pe.transpose(pO[:, 0:V_ALL], vec_rows[:], ident[0:V_ALL, 0:V_ALL]).then_inc(vec_mm, 1)
            pe.wait_ge(silu_ready, 1)

            for ph in phases:
                L, st, n = ph.layer, ph.st, ph.st.nch if ph.st else 0
                if ph.kind == "mod":
                    groups = MODS // MOD_GROUP
                    pe.wait_ge(sem["exp_done"], at("exp_done", ph))
                    pe.wait_ge(sem["rms_ready"], at("rms_ready", ph))
                    for g in range(groups):
                        pe.wait_ge(wm_in[g % 2], 16 * (L * groups // 2 + g // 2 + 1))
                        for t in range(MOD_GROUP):
                            col = 2 * (g * MOD_GROUP + t)
                            for k in range(KT):
                                last = pe.matmul(pS[:, col:col + 2], wm[:, g % 2, k, t * P:(t + 1) * P],
                                                 silu_c[:, 2 * k:2 * k + 2],
                                                 start=(k == 0), stop=(k == KT - 1))
                        last.then_inc(sem["mod_mm"], 1)
                elif ph.kind == "load" and L == 0:
                    earlier = before(ph, "load", lambda p: p.st.blocks // 2)
                    pe.wait_ge(sem["pt_copied"], at("pt_copied", ph))
                    for b in range(st.blocks):
                        pe.wait_ge(xr_in[b % 2], 16 * (earlier + b // 2 + 1))
                        for h in range(2):
                            pe.wait_ge(sem["xt_copied"], at("xt_copied", ph, 2 * b + h - 1))
                            for k in range(4):
                                last = pe.transpose(
                                    pT[:, (ph.round0 + h) % 2, k * P:(k + 1) * P],
                                    x_rows[:, b % 2, (4 * h + k) * P:(4 * h + k + 1) * P], ident[:])
                            last.then_inc(sem["xt_mm"], 1)
                elif ph.kind in ("norm", "final"):
                    pe.wait_ge(sem["exp_done"], at("exp_done", ph))
                    pe.wait_ge(sem["modv_ready"], at("modv_ready", ph))
                    pe.wait_ge(sem["rms_ready"], at("rms_ready", ph))
                    for c_, (off, w) in enumerate(st.chunks):
                        for k in range(KT):
                            r = c_ * KT + k
                            pe.wait_ge(sem["sq_ready"], at("sq_ready", ph, r + 1))
                            pe.matmul(pS[:, c_ * CH:c_ * CH + w], ones[:], sq[:, r % 2, 0:w],
                                      start=(k == 0), stop=(k == KT - 1)).then_inc(sem["sq_used"], 1)
                    if ph.kind == "final":
                        pe.wait_ge(sem["pt_copied"], at("pt_copied", ph))
                        for b in range(SEQ // P):
                            pe.wait_ge(sem["hn_ready"], at("hn_ready", ph, (b * P // CH + 1) * KT))
                            for h in range(2):
                                pe.wait_ge((out_left, out_right)[h], no_less(b))
                                for k in range(4):
                                    last = pe.transpose(
                                        pT[:, (ph.round0 + h) % 2, k * P:(k + 1) * P],
                                        xs[:, 4 * h + k, b * P:(b + 1) * P], ident[:])
                                last.then_inc(sem["pt_done"], 1)
                elif ph.kind == "kv":
                    for j in range(2):
                        open_tile(ph, j)
                        for c_ in range(n):
                            s = j * n + c_
                            open_slot(ph, s)
                            for k in range(KT):
                                if j == 0:
                                    pe.wait_ge(sem["hl_ready"],
                                               at("hl_ready", ph, (c_ - n) * KT + k + 1))
                                last = k_step(ph, j, s, c_, k, KT, hH, hL)
                            last.then_inc(sem["mm_done"], 1)
                    for c_, (off, w) in enumerate(st.chunks):
                        pe.wait_ge(slot_read[bank(ph, n + c_)], reads_at(ph, n + c_))
                        pe.wait_ge(sem["pt_copied"], at("pt_copied", ph, c_ - 1))
                        for t in range(w // P):
                            last = pe.transpose(pT[:, (ph.round0 + c_) % 2, t * P:(t + 1) * P],
                                                vraw[:, t * P:(t + 1) * P], ident[:])
                        last.then_inc(sem["pt_done"], 1)
                elif ph.kind == "attn":
                    nb, R, steps = st.blocks, av_turn(ph), fills(st)

                    def pe_pair(i, g, ph=ph, st=st, n=n, nb=nb, R=R, steps=steps):
                        project(ph, 0, 0, hH, hL, i=i, tiles=4, slots=4 * n)

                        def side(part):
                            for t, c_, k in part:
                                s = (t + 1) * n + c_
                                if c_ == 0 and k == 0:
                                    open_tile(ph, t + 1, i, 4)
                                if k == 0:
                                    open_slot(ph, s, i, 4 * n)
                                last = k_step(ph, t + 1, s, c_, k, KT, hH, hL)
                                if k == KT - 1:
                                    last.then_inc(sem["mm_done"], 1)

                        def scores(b):
                            pe.wait_ge(sem["stack_lo"], at("stack_lo", ph, b * BLK // CH + 1, i, n))
                            pe.wait_ge(sem["exp_done"], at("exp_done", ph, 2 * b, i, 2 * nb))
                            for h in range(2):
                                q = q_st[:, h, b * BLK:(b + 1) * BLK]
                                pieces, masks = score_pieces(st, b, h)
                                for col, key, keys in pieces:
                                    inside = [x for x in masks if col <= x[0] < col + keys]
                                    o = pS[:, col:col + keys]
                                    pe.matmul(o, q, kH[:, g, key:key + keys], start=True, stop=False)
                                    last = pe.matmul(o, q, kL[:, g, key:key + keys],
                                                     start=False, stop=not inside)
                                    for x in inside:
                                        last = pe.matmul(pS[:, x[0]:x[0] + BLK], ident_b[:], x[1][:],
                                                         start=False, stop=x is inside[-1])
                            last.then_inc(sem["qk_done"], 1)

                        def turn_round(b, r):
                            rr = st.round_of(b) + r
                            pe.wait_ge(sem["pt_copied"], at("pt_copied", ph, rr - 1, i, R))
                            for t in range(len(st.rounds(b)[r])):
                                for h in range(2):
                                    key = (2 * r + t) * BLK
                                    last = pe.transpose(
                                        pT[:, (ph.round0 + rr) % 2,
                                           (2 * t + h) * BLK:(2 * t + h + 1) * BLK],
                                        prob[:, b % 2, h, key:key + BLK], ident[:])
                            last.then_inc(sem["pt_done"], 1)

                        def times_v(b, r):
                            rr = st.round_of(b) + r
                            pe.wait_ge(sem["pt_copied"], at("pt_copied", ph, rr + 1, i, R))
                            if r == 0:
                                pe.wait_ge(sem["att_done"], at("att_done", ph, b, i, nb))
                            for t, kb in enumerate(st.rounds(b)[r]):
                                cols = slice(2 * t * BLK, 2 * (t + 1) * BLK)
                                end = r == len(st.rounds(b)) - 1 and t == len(st.rounds(b)[r]) - 1
                                pe.matmul(pO[:, 0:2 * BLK], v_cur[:, kb, :], ptH[:, rr % 2, cols],
                                          start=(r == 0 and t == 0), stop=False)
                                last = pe.matmul(pO[:, 0:2 * BLK], v_cur[:, kb, :],
                                                 ptL[:, rr % 2, cols], start=False, stop=end)
                            last.then_inc(av_done[rr % 2], 1)

                        for b, parts in enumerate(steps):
                            rounds = len(st.rounds(b - 1)) if b else 0
                            if b < nb:
                                scores(b)
                            side(parts[0])
                            if b:
                                pe.wait_ge(sem["p_ready"], at("p_ready", ph, 2 * b, i, 2 * nb))
                            for r in range(min(rounds, 2)):
                                turn_round(b - 1, r)
                            side(parts[1])
                            if b == 1:
                                pe.wait_ge(sem["vcur_ready"], at("vcur_ready", ph, 1, i, 1))
                            for r in range(min(rounds, 2)):
                                times_v(b - 1, r)
                            for r in range(2, rounds):
                                turn_round(b - 1, r)
                            side(parts[2])
                            for r in range(2, rounds):
                                times_v(b - 1, r)
                    by_pair(pe, pe_pair)
                elif ph.kind == "mixb":
                    with pe.Fori(0, 2) as i:
                        for j in range(2):
                            project(ph, j, 2 * j * n, yH, yL, kts=CT, outs=2, i=i, tiles=2,
                                    slots=4 * n, ready="y_lo")
                elif ph.kind == "conv":
                    with pe.Fori(0, CT) as i:
                        for j in range(4):
                            project(ph, j, j * n, hH, hL, i=i, tiles=4, slots=4 * n)
                elif ph.kind == "mixa":
                    pe.wait_ge(sem["y_lo"], at("y_lo", ph))
                    with pe.Fori(0, 2) as i:
                        for h in range(2):
                            for e in range(2):
                                project(ph, 3 * h + e, (4 * h + e) * n, hH, hL, i=i, tiles=6,
                                        slots=8 * n)
                            project(ph, 3 * h + 2, (4 * h + 2) * n, yH, yL, kts=CT, outs=2, i=i,
                                    tiles=6, slots=8 * n)
                elif ph.kind == "wout":
                    with pe.Fori(0, KT // 2) as i:
                        for j in range(2):
                            project(ph, j, j * n, hH, hL, i=i, tiles=2, slots=2 * n,
                                    ready="ml_ready")


def rope_tables():
    freqs = HD // 4
    p, t = np.arange(P)[:, None], np.arange(SEQ)[None, :]
    inv_freq = (10000.0 ** (-np.arange(freqs, dtype=np.float32) / freqs)).astype(np.float32)
    place = np.where((p // 32) % 2 == 0, t // GRID_W, t % GRID_W).astype(np.float32)
    ang = place * inv_freq[p % freqs]
    sign = np.where((p // freqs) % 2 == 0, -1.0, 1.0).astype(np.float32)
    return np.cos(ang).astype(np.float32), (np.sin(ang) * sign).astype(np.float32)


_INS = ["x", "c", "ctx", "c_ctx", "norm_w", "w_mod", "b_mod", "w_in", "conv_w", "w_a_out",
        "w_b_out", "attn_sink", "w_o", "final_norm_w"]


def kernel(**inputs):
    import concourse.bacc as bacc
    from concourse.bass_utils import run_bass_kernel_spmd as run

    nc = bacc.Bacc("TRN2", target_bir_lowering=False, num_devices=1)
    cos_t, sin_t = rope_tables()
    arrays = {f"in_{n}": np.ascontiguousarray(inputs[n]) for n in _INS}
    arrays.update({"in_cos": cos_t, "in_sin": sin_t})
    args = [nc.dram_tensor(n, a.shape, mybir.dt.from_np(a.dtype), kind="ExternalInput").ap()
            for n, a in arrays.items()]
    out = nc.dram_tensor("out", (1, SEQ, D), F32, kind="ExternalOutput").ap()
    hybrid_block(nc, *args, out)
    r = run(nc, [arrays], core_ids=[0])
    return r.results[0]["out"]
```

```python
import concourse.bass as bass
import numpy as np
from concourse import mybir
from contextlib import ExitStack

F32 = mybir.dt.float32
F32R = mybir.dt.float32r
BF16 = mybir.dt.bfloat16
ACT = mybir.ActivationFunctionType
ALU = mybir.AluOpType
AX = mybir.AxisListType

D, SEQ, CTX, DEPTH, GRID_W = 1024, 1024, 256, 2, 64
CONV, CONV_K, HEADS, KV_HEADS, HD = 512, 3, 8, 2, 64
ATT, BLK, EPS, NEG = HEADS * HD, 128, 1e-6, -1e30
SCALE = HD ** -0.5
P = 128
KT = D // P
CT = CONV // P
PAIRS = HEADS // 2
TOK = SEQ + CTX
C_B, C_C, C_U, C_Z = 0, CONV, 2 * CONV, 3 * CONV
C_Q = 4 * CONV
C_K = C_Q + ATT
C_V = C_K + KV_HEADS * HD
C_ZB = C_V + KV_HEADS * HD
C_GA = C_ZB + ATT
C_GB = C_GA + D
IN_COLS = C_GB + D
CH = 512
X_PARTS = 4
MOD_GROUP = 4
MODS = 3 * KT


class Stream:

    def __init__(self, name, tokens, key0):
        self.name, self.T, self.key0 = name, tokens, key0
        self.chunks = [(o, min(CH, tokens - o)) for o in range(0, tokens, CH)]
        self.nch = len(self.chunks)
        self.blocks = tokens // BLK
        self.lat = name == "lat"

    def key_tiles(self, b):
        own = [k for k in (b - 1, b, b + 1) if 0 <= k < self.blocks] if self.lat else []
        return own + [SEQ // BLK + k for k in range(CTX // BLK)]

    def rounds(self, b):
        t = self.key_tiles(b)
        return [t[n:n + 2] for n in range(0, len(t), 2)]

    def round_of(self, b):
        return sum(len(self.rounds(n)) for n in range(b))


LAT = Stream("lat", SEQ, 0)
CTXS = Stream("ctx", CTX, SEQ)


SIDE_TILES = 3


LEAD, FIRST = 4, 10


def fills(st):
    todo = [(t, c, k) for t in range(SIDE_TILES) for c in range(st.nch) for k in range(KT)]
    first = LEAD + FIRST
    out = [(todo[LEAD:first], [], [], todo[:LEAD])]
    at = first
    for b in range(1, st.blocks + 1):
        n = first + (len(todo) - first) * b // st.blocks - at
        a1 = (n + 2) // 3
        a2 = (n - a1 + 1) // 2
        part = todo[at:at + n]
        out.append((part[:a1], part[a1:a1 + a2], part[a1 + a2:], []))
        at += n
    return out


def slots_done(parts):
    return [(t, c) for part in parts for t, c, k in part if k == KT - 1]


BODY = {"kv": [1, 1], "attn": [1] * 4, "mixb": [2, 2], "conv": [1] * 4, "mixa": [1, 1, 2] * 2,
        "wout": [1, 1]}


START = {"att_done": 1, "exp_done": 1, "m_done": 1, "pt_copied": 1, "pt_done": 2, "qk_done": 1,
         "tap_done": 1, "slot_read": 1, "av_done": 1, "gb_out": 16}


class Phase:

    def __init__(self, kind, st, layer, base, tile0, slot0, round0, av0):
        self.kind, self.st, self.layer, self.base = kind, st, layer, base
        self.tile0, self.slot0, self.round0, self.av0 = tile0, slot0, round0, av0


def make_phases():
    order = []
    for layer in range(DEPTH):
        order.append(("mod", None, layer))
        last = layer == DEPTH - 1
        for st in (CTXS, LAT):
            if layer == 0 and st is CTXS:
                order.append(("load", st, layer))
            order += [("norm", st, layer), ("kv", st, layer)]
            if st is LAT or not last:
                order += [(k, st, layer) for k in ("attn", "mixb", "conv", "mixa")]
                if layer == 0 and st is CTXS:
                    order.append(("load", LAT, layer))
                order.append(("wout", st, layer))
    order.append(("final", LAT, DEPTH))
    count, out = {k: v for k, v in START.items() if k not in ("slot_read", "av_done", "gb_out")}, []
    tile = slot = rnd = av = 0
    for kind, st, layer in order:
        out.append(Phase(kind, st, layer, dict(count), tile, slot, rnd, av))
        n = st.nch if st else 0
        tiles = slots = rounds = avs = 0
        gain = {}
        if kind == "mod":
            gain = {"mod_mm": MODS // MOD_GROUP, "modv_ready": 1, "mod_done": 1}
        elif kind == "load":
            gain = {"xt_mm": 2 * st.blocks, "xt_copied": 2 * st.blocks}
        elif kind in ("norm", "final"):
            gain = {"sum_done": n, "rms_ready": n, "rstd_ready": n, "hn_ready": KT * n}
            if kind == "norm":
                gain.update({"hf_ready": KT * n, "hh_ready": KT * n, "hl_ready": KT * n})
                if st.lat:
                    gain["x_spilled"] = 16
        elif kind == "kv":
            tiles, slots, rounds = 2, 2 * n, n
            gain = {"stack_hi": n, "stack_lo": n}
        elif kind == "attn":
            tiles, slots = 4 * PAIRS, 4 * PAIRS * n
            rounds = avs = PAIRS * st.round_of(st.blocks)
            nb = PAIRS * st.blocks
            gain = {"stack_hi": PAIRS * n, "stack_lo": PAIRS * n, "vcur_ready": PAIRS,
                    "qk_done": nb, "max_ready": nb, "negm_ready": nb, "sinkin_ready": nb,
                    "exp_done": 2 * nb, "den_ready": 2 * nb, "rden_ready": 2 * nb,
                    "p_ready": 2 * nb, "att_half": nb, "att_done": nb,
                    "gate_tanh": PAIRS * n, "yb_done": PAIRS}
        elif kind == "mixb":
            tiles, slots = KT // 2, KT * n
            gain = {"y_hi": CT, "y_lo": CT}
        elif kind == "conv":
            tiles, slots = 4 * CT, 4 * CT * n
            gain = {"halo_zero": 1, "gate_tanh": CT * n, "tap_done": 4 * CT,
                    "y_hi": CT * n, "y_lo": CT * n}
        elif kind == "mixa":
            tiles, slots = KT + KT // 2, 2 * KT * n
            gain = {"m_done": KT * n}
        elif kind == "wout":
            tiles, slots = KT, KT * n
            gain = {"mh_ready": KT, "ml_ready": KT}
            if st.lat:
                gain["x_in"] = 16 * X_PARTS
        if kind in ("load", "wout"):
            gain.update({"acc_zero": 1, "sq_ready": KT * n, "sq_added": KT * n})
        if kind in ("kv", "attn") and st.lat:
            r = n if kind == "kv" else PAIRS * n
            gain.update({"rope_shuf": r, "rope_sin": r, "rope_cos": r, "rope_out": r})
        gain["w_hi"] = gain["w_lo"] = tiles
        gain["mm_done"] = slots
        gain["pt_done"] = gain["pt_hi"] = gain["pt_copied"] = rounds
        for k, v in gain.items():
            count[k] = count.get(k, 0) + v
        tile, slot, rnd, av = tile + tiles, slot + slots, rnd + rounds, av + avs
    return out, tile, sorted(count)


def hybrid_block(nc, x, c, ctx, c_ctx, norm_w, w_mod, b_mod, w_in, conv_w, w_a_out, w_b_out,
                 attn_sink, w_o, final_norm_w, cos_t, sin_t, out):
    phases, n_tiles, counters = make_phases()
    stack = ExitStack()
    with stack:
        def sb(name, shape, dt=F32):
            return stack.enter_context(nc.sbuf_tensor(name, shape, dt))

        def zone(*sets):
            made = {}
            for n, tensors in enumerate(sets):
                with ExitStack() as z:
                    for name, shape, dt in tensors:
                        if n == len(sets) - 1:
                            made[name] = sb(name, shape, dt)
                        else:
                            made[name] = z.enter_context(nc.sbuf_tensor(name, shape, dt))
            return made

        ident = sb("ident", [P, P])
        ident_b = sb("ident_b", [P, P], BF16)
        mask_prev = sb("mask_prev", [P, BLK], BF16)
        mask_next = sb("mask_next", [P, BLK], BF16)
        ones = sb("ones", [P, P])
        eps = sb("eps", [P, 1])
        cos_s = sb("cos_s", [P, SEQ])
        sin_s = sb("sin_s", [P, SEQ])
        V_NW = 2 * KT
        V_BM = V_NW + DEPTH * KT
        V_CW = V_BM + DEPTH * MODS
        V_FN = V_CW + DEPTH * CONV_K * CT
        V_ALL = V_FN + KT
        vec = sb("vec", [P, V_ALL])
        silu_t = sb("silu_t", [P, 2 * KT])
        silu_c = sb("silu_c", [P, 2 * KT])
        modv = sb("modv", [P, MODS, 2])
        mod_a = sb("mod_a", [P, KT, 2])
        sink = sb("sink", [P, DEPTH * HEADS])
        nsink = sb("nsink", [P, DEPTH * HEADS])
        mx, negm, sinkin, sinkexp, rsum, rden = (
            sb(n, [P, 2, 2]) for n in ("mx", "negm", "sinkin", "sinkexp", "rsum", "rden"))
        raw = sb("raw", [P, 2, KT * P])
        wH = sb("wH", [P, 2, KT * P], F32R)
        wL = sb("wL", [P, 2, KT * P], F32R)
        hH = sb("hH", [P, KT, SEQ], F32R)
        hL = sb("hL", [P, KT, SEQ], F32R)
        xc = sb("xc", [P, KT, CTX])
        acc_ctx = sb("acc_ctx", [P, CTX])

        z1 = zone([("wm", [P, 2, KT, MOD_GROUP * P], F32)],
                  [("kH", [P, KV_HEADS, TOK], F32R),
                   ("kL", [P, KV_HEADS, TOK], F32R),
                   ("v_all", [P, TOK // BLK, KV_HEADS, P], F32R)],
                  [("m_lat", [P, KT, SEQ], F32)])
        z2 = zone([("q_st", [P, 2, SEQ], F32R),
                   ("prob", [P, 2, 2, 5 * BLK], F32),
                   ("ptH", [P, 2, CH], F32R), ("ptL", [P, 2, CH], F32R),
                   ("o_half", [HD, 2 * BLK], F32)],
                  [("yH", [P, CT, SEQ], F32R), ("yL", [P, CT, SEQ], F32R)],
                  [("xs", [P, KT, SEQ], F32)])
        z3 = zone([("o_rows", [P, 2, D], F32)],
                  [("cb_lat", [P, SEQ], F32), ("cv_lat", [P, SEQ], F32), ("sz_lat", [P, SEQ], F32)],
                  [("yb_ctx", [P, PAIRS, CTX], F32), ("m_ctx", [P, KT, CTX], F32),
                   ("cb_ctx", [P, CTX], F32), ("cv_ctx", [P, CTX], F32), ("sz_ctx", [P, CTX], F32)],
                  [("yb_lat", [P, PAIRS, SEQ], F32)])
        z4 = zone([("vec_rows", [V_ALL, P], F32), ("head_start", [P, len(START) + 3], F32)],
                  [("acc_lat", [P, SEQ], F32), ("sq", [P, 2, CH], F32), ("hn", [P, 2, CH], F32),
                   ("hf", [P, 2, CH], F32)],
                  [("above", [P, 2, SEQ], F32), ("x_rows", [P, 2, D], F32)],
                  [("tgb", [P, 2, SEQ], F32)],
                  [("tga", [P, 2, SEQ], F32), ("gm", [P, 2, CH], F32)],
                  [("cu", [P, SEQ + 2], F32), ("yv", [P, 2, CH], F32), ("th", [P, CH], F32)],
                  [("v_cur", [P, TOK // BLK, P], F32R), ("szb", [P, SEQ], F32),
                   ("rraw", [P, CH], F32), ("rsh", [P, CH], F32), ("rout", [P, CH], F32),
                   ("gst", [P, 2, CH], F32)])
        wm, m_lat, kH, kL, v_all = (z1[n] for n in ("wm", "m_lat", "kH", "kL", "v_all"))
        q_st, prob, ptH, ptL, o_half = (z2[n] for n in ("q_st", "prob", "ptH", "ptL", "o_half"))
        yH, yL, xs, o_rows = z2["yH"], z2["yL"], z2["xs"], z3["o_rows"]
        vec_rows, head_start, sq, hn, hf, x_rows = (
            z4[n] for n in ("vec_rows", "head_start", "sq", "hn", "hf", "x_rows"))
        tgb, tga, gm, cu, yv, th = (z4[n] for n in ("tgb", "tga", "gm", "cu", "yv", "th"))
        v_cur, rraw, rsh, rout = (z4[n] for n in ("v_cur", "rraw", "rsh", "rout"))
        szb, gst = z4["szb"], z4["gst"]
        vraw = gst[:, 0]
        acc = {"lat": z4["acc_lat"], "ctx": acc_ctx}
        x_st = {"lat": xs, "ctx": xc}
        yb = {"lat": z3["yb_lat"], "ctx": z3["yb_ctx"]}
        m = {"lat": m_lat, "ctx": z3["m_ctx"]}
        cb, cv, sz = ({s: z3[f"{n}_{s}"] for s in ("lat", "ctx")} for n in ("cb", "cv", "sz"))

        x_keep = nc.dram_tensor("x_keep", (P, KT, SEQ), F32).ap()
        gb_keep = nc.dram_tensor("gb_keep", (KT, P, SEQ), F32).ap()

        pp = stack.enter_context(nc.psum_tensor("pp", [P, 2, CH], F32))
        pS = stack.enter_context(nc.psum_tensor("pS", [P, 3 * CH], F32))
        pT = stack.enter_context(nc.psum_tensor("pT", [P, 2, CH], F32))
        pO = stack.enter_context(nc.psum_tensor("pO", [P, CH], F32))

        def new_sem(name):
            return stack.enter_context(nc.semaphore(name))

        sem = {n: new_sem(n) for n in counters}
        const_ready, vec_in, tab_in, vec_mm, vec_ready, nsink_ready, silu_tanh, silu_ready, \
            out_left, out_right = (new_sem(n) for n in (
                "const_ready", "vec_in", "tab_in", "vec_mm", "vec_ready", "nsink_ready",
                "silu_tanh", "silu_ready", "out_left", "out_right"))
        raw_in, slot_read, av_done, gb_out, gb_in, wm_in, xr_in, out_sent = (
            [new_sem(f"{n}{i}") for i in range(2)] for n in
            ("raw_in", "slot_read", "av_done", "gb_out", "gb_in", "wm_in", "xr_in", "out_sent"))
        block = stack.enter_context(nc.Block())

        w_in_v, w_a_v, w_b_v, w_o_v, w_mod_v = (
            w.rearrange("l (k p) n -> l p k n", p=P) for w in (w_in, w_a_out, w_b_out, w_o, w_mod))

        def no_less(value):
            return max(value, 0) if type(value) is int else value

        def at(name, ph, more=0, i=0, per=0):
            return no_less(i * per + (ph.base.get(name, 0) + more))

        def slots_at(ph, s, i=0, per=0):
            return no_less(i * per + (ph.slot0 + s + 1))

        def bank(ph, s):
            return (ph.slot0 + s) % 2

        def reads_at(ph, s, i=0, per=0):
            return no_less(i * (per // 2) + ((ph.slot0 + s) // 2 + 1 + START["slot_read"]))
        def before(ph, kind, of):
            return sum(of(p) for p in phases[:phases.index(ph)] if p.kind == kind)

        def gb_used(ph):
            return before(ph, "attn", lambda p: PAIRS * p.st.nch)

        def av_turn(ph):
            r = ph.st.round_of(ph.st.blocks)
            assert r % 2 == 0 and ph.av0 % 2 == 0 and ph.slot0 % 2 == 0 and ph.tile0 % 2 == 0
            return r

        def x_made(ph):
            made = next(p for p in phases if (p.kind, p.st, p.layer) == ("wout", LAT, ph.layer - 1))
            return (made.slot0 + KT * made.st.nch) // 2 + START["slot_read"]

        def s_of(ph):
            return 0 if ph.st.lat else 1

        def by_pair(eng, turn):
            with eng.Fori(0, KV_HEADS) as g:
                with eng.Fori(0, PAIRS // KV_HEADS) as j:
                    turn(g * (PAIRS // KV_HEADS) + j, g)

        @block.sync
        def _(sp):
            def load_tile(ph, j, src, i=0, per=0):
                n = ph.tile0 + j
                sp.wait_ge(sem["w_lo"], no_less(i * per + (n - 1)))
                dst = raw[:, n % 2, :].rearrange("p (k n) -> p k n", k=src.shape[1])
                sp.dma_start(dst, src).then_inc(raw_in[n % 2], 16)

            place_reg = sp.alloc_register("place")

            def place(value, size):
                sp.reg_mov(place_reg, value * (4 * size))
                return value

            def cols(w, layer, col, n=P):
                if type(col) is not int:
                    place(col, 1)
                return w[layer][:, :, bass.ds(col, n)]

            rows = 0
            for src in (c, c_ctx.rearrange("(a n) -> a n", a=1), norm_w, b_mod,
                        conv_w.rearrange("l k n -> (l k) n"),
                        final_norm_w.rearrange("(a n) -> a n", a=1)):
                r = src.rearrange("a (k p) -> (a k) p", p=P)
                sp.dma_start(vec_rows[rows:rows + r.shape[0], :], r).then_inc(vec_in, 16)
                rows += r.shape[0]
            assert rows == V_ALL
            sp.dma_start(sink[:], attn_sink.rearrange("(a l) h -> a (l h)", a=1)
                         .to_broadcast([P, DEPTH * HEADS])).then_inc(tab_in, 16)
            sp.dma_start(cos_s[:], cos_t).then_inc(tab_in, 16)
            sp.dma_start(sin_s[:], sin_t).then_inc(tab_in, 16)

            for ph in phases:
                L, st = ph.layer, ph.st
                if ph.kind == "mod":
                    sp.wait_ge(sem["ml_ready"], at("ml_ready", ph))
                    for g in range(MODS // MOD_GROUP):
                        sp.wait_ge(sem["mod_mm"], at("mod_mm", ph, g - 1))
                        sp.dma_start(wm[:, g % 2],
                                     cols(w_mod_v, L, g * MOD_GROUP * P, MOD_GROUP * P))\
                            .then_inc(wm_in[g % 2], 16)
                elif ph.kind == "load":
                    src = (x[0] if st.lat else ctx[0]).rearrange("(b p) n -> b p n", p=P)
                    if st.lat:
                        for j in range(2):
                            load_tile(phases[phases.index(ph) + 1], j, cols(w_o_v, L, j * P))
                    sp.wait_ge(vec_mm, 1)
                    sp.wait_ge(sem["m_done"], at("m_done", ph))
                    for b in range(st.blocks):
                        sp.wait_ge(sem["xt_mm"], at("xt_mm", ph, 2 * (b - 1)))
                        sp.dma_start(x_rows[:, b % 2], src[b]).then_inc(xr_in[b % 2], 16)
                elif ph.kind == "norm":
                    kv = phases[phases.index(ph) + 1]
                    load_tile(kv, 0, cols(w_in_v, L, C_V))
                    load_tile(kv, 1, cols(w_in_v, L, C_K))
                    if st.lat:
                        sp.wait_ge(sem["xt_copied"], at("xt_copied", ph))
                        if L:
                            for b in range(2):
                                sp.wait_ge(slot_read[b], x_made(ph))
                        sp.dma_start(x_keep, xs[:]).then_inc(sem["x_spilled"], 16)
                elif ph.kind == "attn":
                    with sp.Fori(0, PAIRS) as i:
                        load_tile(ph, 0, cols(w_in_v, L, i * P + C_Q), i, 4)
                        load_tile(ph, 1, cols(w_in_v, L, i * P + C_ZB), i, 4)
                        load_tile(ph, 2, cols(w_in_v, L, i * (2 * P) + C_GB), i, 4)
                        load_tile(ph, 3, cols(w_in_v, L, i * (2 * P) + (C_GB + P)), i, 4)
                elif ph.kind == "mixb":
                    for t in range(2):
                        load_tile(ph, t, cols(w_b_v, L, 2 * t * P, 2 * P))
                    for b in range(2):
                        sp.wait_ge(gb_out[b], START["gb_out"] + 16 * gb_used(ph))
                    sp.wait_ge(sem["yb_done"], at("yb_done", ph))
                    for d in range(KT):
                        for s in ((d - 1) * st.nch - 1, (d - 1) * st.nch - 2):
                            sp.wait_ge(slot_read[bank(ph, s)], reads_at(ph, s))
                        sp.dma_start(tgb[:, d % 2, 0:st.T], gb_keep[d][:, 0:st.T])\
                            .then_inc(gb_in[d % 2], 16)
                        if d in (1, 2):
                            load_tile(ph, d + 1, cols(w_b_v, L, 2 * (d + 1) * P, 2 * P))
                elif ph.kind == "conv":
                    with sp.Fori(0, CT) as i:
                        for j, col in enumerate((C_C, C_U, C_Z, C_B)):
                            load_tile(ph, j, cols(w_in_v, L, i * P + col), i, 4)
                elif ph.kind == "mixa":
                    with sp.Fori(0, 2) as i:
                        for h in range(2):
                            for e in range(2):
                                load_tile(ph, 3 * h + e,
                                          cols(w_in_v, L, i * (4 * P) + (C_GA + (2 * h + e) * P)),
                                          i, 6)
                            load_tile(ph, 3 * h + 2,
                                      cols(w_a_v, L, i * (4 * P) + 2 * h * P, 2 * P), i, 6)
                elif ph.kind == "wout":
                    for j in range(KT):
                        if st.lat or j >= 2:
                            load_tile(ph, j, cols(w_o_v, L, j * P))
                        part = j - 1
                        if st.lat and 0 <= part < X_PARTS:
                            k = slice(part * KT // X_PARTS, (part + 1) * KT // X_PARTS)
                            if part == 0:
                                sp.wait_ge(sem["mm_done"], slots_at(ph, -1))
                                sp.wait_ge(sem["x_spilled"], at("x_spilled", ph))
                            else:
                                sp.wait_ge(sem["x_in"], at("x_in", ph, 16 * part))
                            sp.dma_start(xs[:, k], x_keep[:, k]).then_inc(sem["x_in"], 16)
                elif ph.kind == "final":
                    out_v = out[0].rearrange("(b p) n -> b p n", p=P)
                    for b in range(SEQ // P):
                        sp.wait_ge(out_left, b + 1)
                        sp.wait_ge(out_right, b + 1)
                        sp.dma_start(out_v[b], o_rows[:, b % 2]).then_inc(out_sent[b % 2], 16)
                    for b in range(2):
                        sp.wait_ge(out_sent[b], 16 * (SEQ // P // 2))

        @block.gpsimd
        def _(pool):
            for t, value in ((ident, 0.0), (ident_b, 0.0), (mask_prev, 0.0), (mask_next, 0.0),
                             (ones, 1.0), (eps, EPS)):
                pool.memset(t[:], value).then_inc(const_ready, 1)
            started = [(sem[n], v) for n, v in START.items() if n in sem]
            started += [(s, START["slot_read"]) for s in slot_read]
            started += [(s, START["av_done"]) for s in av_done]
            started += [(s, START["gb_out"]) for s in gb_out]
            for at_, (s, v) in enumerate(started):
                pool.memset(head_start[:, at_:at_ + 1], 0.0).then_inc(s, v)
            pool.wait_ge(const_ready, 6)
            for mat in (ident, ident_b):
                pool.affine_select(out=mat[:], in_=mat[:], compare_op=ALU.not_equal, fill=1.0, base=0,
                                   pattern=[[-1, P]], channel_multiplier=1).then_inc(const_ready, 1)
            pool.affine_select(out=mask_prev[:], in_=mask_prev[:], compare_op=ALU.is_ge, fill=NEG,
                               base=0, pattern=[[1, BLK]], channel_multiplier=-1)\
                .then_inc(const_ready, 1)
            pool.affine_select(out=mask_next[:], in_=mask_next[:], compare_op=ALU.is_ge, fill=NEG,
                               base=0, pattern=[[-1, BLK]], channel_multiplier=1)\
                .then_inc(const_ready, 1)

            def low_part(n, i=0, per=0):
                pool.wait_ge(sem["w_hi"], no_less(i * per + (n + 1)))
                pool.tensor_tensor(wL[:, n % 2, :], raw[:, n % 2, :], wH[:, n % 2, :].bitcast(F32),
                                   ALU.subtract).then_inc(sem["w_lo"], 1)

            def rope_sin(ph, n, i=0, per=0):
                off, w = ph.st.chunks[n]
                pool.wait_ge(sem["rope_shuf"], at("rope_shuf", ph, n + 1, i, per))
                pool.tensor_tensor(rsh[:, 0:w], rsh[:, 0:w], sin_s[:, off:off + w], ALU.mult)\
                    .then_inc(sem["rope_sin"], 1)

            low_part(0)
            low_part(1)
            pool.wait_ge(tab_in, 48)
            for ph in phases:
                st, n = ph.st, ph.st.nch if ph.st else 0
                if ph.kind == "norm":
                    for r, (c_, k) in enumerate((c_, k) for c_ in range(n) for k in range(KT)):
                        off, w = st.chunks[c_]
                        pool.wait_ge(sem["hh_ready"], at("hh_ready", ph, r + 1))
                        pool.tensor_tensor(hL[:, k, off:off + w], hf[:, r % 2, 0:w],
                                           hH[:, k, off:off + w].bitcast(F32), ALU.subtract)\
                            .then_inc(sem["hl_ready"], 1)
                elif ph.kind == "kv":
                    if st.lat:
                        for c_ in range(n):
                            rope_sin(ph, c_)
                    low_part(ph.tile0 + 2)
                    low_part(ph.tile0 + 3)
                elif ph.kind == "attn":
                    def pool_pair(i, g, ph=ph, st=st, n=n):
                        if st.lat:
                            for c_ in range(n):
                                rope_sin(ph, c_, i, n)
                        low_part(ph.tile0 + 2, i, 4)
                        for b, parts in enumerate(fills(st)):
                            for t, c_ in slots_done(parts):
                                if c_ == n - 1:
                                    low_part(ph.tile0 + 3 + t, i, 4)
                    by_pair(pool, pool_pair)
                elif ph.kind in ("mixb", "conv", "mixa", "wout"):
                    turns, per = {"mixb": (2, 2), "conv": (CT, 4), "mixa": (2, 6),
                                  "wout": (KT // 2, 2)}[ph.kind]
                    if ph.tile0 + turns * per == n_tiles:
                        turns -= 1
                    with pool.Fori(0, turns) as i:
                        for j in range(per):
                            low_part(ph.tile0 + j + 2, i, per)

        @block.scalar
        def _(act):
            def high_part(ph, j, i=0):
                n, body = ph.tile0 + j + 2, BODY[ph.kind]
                if j >= 0:
                    act.wait_ge(sem["mm_done"],
                                slots_at(ph, sum(body[:j + 1]) * ph.st.nch - 1, i, sum(body) * ph.st.nch))
                act.wait_ge(raw_in[n % 2], no_less(i * (len(body) // 2 * 16) + 16 * (n // 2 + 1)))
                act.activation(wH[:, n % 2, :], raw[:, n % 2, :], ACT.Copy)\
                    .then_inc(sem["w_hi"], 1)

            def square(ph, r, k, c_, i=0, per=0):
                st = ph.st
                off, w = st.chunks[c_]
                act.wait_ge(sem["sq_added"], at("sq_added", ph, r - 1, i, per))
                act.activation(sq[:, r % 2, 0:w], x_st[st.name][:, k, off:off + w], ACT.Square)\
                    .then_inc(sem["sq_ready"], 1)

            act.preload_act_table(ACT.Exp)
            act.wait_ge(vec_ready, 1)
            act.activation(silu_t[:], vec[:, 0:2 * KT], ACT.Tanh, scale=0.5).then_inc(silu_tanh, 1)
            first_kv = next(p for p in phases if p.kind == "kv")
            high_part(first_kv, -2)
            high_part(first_kv, -1)
            for ph in phases:
                L, st, n = ph.layer, ph.st, ph.st.nch if ph.st else 0
                if ph.kind == "load":
                    for c_ in range(n):
                        blocks = min(st.blocks, (c_ + 1) * CH // P)
                        act.wait_ge(sem["xt_copied"], at("xt_copied", ph, 2 * blocks))
                        for k in range(KT):
                            square(ph, c_ * KT + k, k, c_)
                elif ph.kind in ("norm", "final"):
                    for c_, (off, w) in enumerate(st.chunks):
                        act.wait_ge(sem["sum_done"], at("sum_done", ph, c_ + 1))
                        act.activation(acc[st.name][:, off:off + w], pS[:, c_ * CH:c_ * CH + w],
                                       ACT.Sqrt, bias=eps[:, 0:1], scale=1.0 / D)\
                            .then_inc(sem["rms_ready"], 1)
                    if ph.kind == "norm":
                        act.preload_act_table(ACT.Exp)
                        act.wait_ge(sem["mm_done"], slots_at(ph, -1))
                        for r, (c_, k) in enumerate((c_, k) for c_ in range(n) for k in range(KT)):
                            off, w = st.chunks[c_]
                            act.wait_ge(sem["hf_ready"], at("hf_ready", ph, r + 1))
                            act.activation(hH[:, k, off:off + w], hf[:, r % 2, 0:w], ACT.Copy)\
                                .then_inc(sem["hh_ready"], 1)
                    else:
                        for b in range(SEQ // P):
                            act.wait_ge(sem["pt_done"], at("pt_done", ph, 2 * b + 1))
                            act.wait_ge(out_sent[b % 2], no_less(16 * (b // 2)))
                            act.activation(o_rows[:, b % 2, 0:CH], pT[:, ph.round0 % 2, :], ACT.Copy)\
                                .then_inc(out_left, 1)
                elif ph.kind == "kv":
                    def v_high(c_, ph=ph, st=st):
                        off, w = st.chunks[c_]
                        act.wait_ge(sem["pt_done"], at("pt_done", ph, c_ + 1))
                        t0, nt = (st.key0 + off) // BLK, w // BLK
                        act.activation(v_all[:, t0:t0 + nt, :, 0:HD],
                                       pT[:, (ph.round0 + c_) % 2, 0:w]
                                       .rearrange("p (t g d) -> p t g d", t=nt, g=KV_HEADS),
                                       ACT.Copy).then_inc(sem["pt_hi"], 1)

                    for c_, (off, w) in enumerate(st.chunks):
                        act.wait_ge(sem["mm_done"], slots_at(ph, c_))
                        act.wait_ge(sem["hl_ready"], at("hl_ready", ph))
                        act.wait_ge(sem["pt_done"], at("pt_done", ph, c_))
                        act.activation(vraw[:, 0:w], pp[:, bank(ph, c_), 0:w], ACT.Copy)\
                            .then_inc(slot_read[bank(ph, c_)], 1)
                        if c_ == n - 1:
                            high_part(ph, 0)
                        v_high(c_)
                    for c_, (off, w) in enumerate(st.chunks):
                        s = n + c_
                        act.wait_ge(sem["mm_done"], slots_at(ph, s))
                        free = "rope_out" if st.lat else "stack_lo"
                        act.wait_ge(sem[free], at(free, ph, c_))
                        act.activation(rraw[:, 0:w], pp[:, bank(ph, s), 0:w], ACT.Copy)\
                            .then_inc(slot_read[bank(ph, s)], 1)
                        if c_ == n - 1:
                            high_part(ph, 1)
                        if st.lat:
                            act.wait_ge(sem["rope_out"], at("rope_out", ph, c_ + 1))
                        else:
                            act.wait_ge(slot_read[bank(ph, s)], reads_at(ph, s))
                        r = rout if st.lat else rraw
                        cols = slice(st.key0 + off, st.key0 + off + w)
                        for g in range(KV_HEADS):
                            for half in (0, HD):
                                last = act.activation(kH[half:half + HD, g, cols],
                                                      r[g * HD:(g + 1) * HD, 0:w], ACT.Copy)
                        last.then_inc(sem["stack_hi"], 1)
                elif ph.kind == "attn":
                    nb, R, steps = st.blocks, av_turn(ph), fills(st)
                    act.wait_ge(sem["x_spilled"], at("x_spilled", ph))

                    def act_pair(i, g, ph=ph, st=st, n=n, nb=nb, R=R, steps=steps):
                        def q_chunk(c_):
                            off, w = st.chunks[c_]
                            act.wait_ge(sem["mm_done"], slots_at(ph, c_, i, 4 * n))
                            if st.lat:
                                act.wait_ge(sem["rope_out"], at("rope_out", ph, c_, i, n))
                            else:
                                act.wait_ge(sem["stack_lo"], at("stack_lo", ph, c_, i, n))
                            act.activation(rraw[:, 0:w], pp[:, bank(ph, c_), 0:w], ACT.Copy)\
                                .then_inc(slot_read[bank(ph, c_)], 1)
                            if st.lat:
                                act.wait_ge(sem["rope_out"], at("rope_out", ph, c_ + 1, i, n))
                            else:
                                act.wait_ge(slot_read[bank(ph, c_)], reads_at(ph, c_, i, 4 * n))
                            act.wait_ge(sem["qk_done"], at("qk_done", ph, 0, i, nb))
                            r = rout if st.lat else rraw
                            act.activation(q_st[0:HD, 0, off:off + w], r[0:HD, 0:w], ACT.Copy)
                            act.activation(q_st[HD:P, 1, off:off + w], r[HD:P, 0:w], ACT.Copy)\
                                .then_inc(sem["stack_hi"], 1)

                        def pt_high(b, r):
                            rr = st.round_of(b) + r
                            w = len(st.rounds(b)[r]) * 2 * BLK
                            act.wait_ge(sem["pt_done"], at("pt_done", ph, rr + 1, i, R))
                            act.wait_ge(av_done[rr % 2],
                                        no_less(i * (R // 2) + (START["av_done"] + ph.av0 // 2 + rr // 2)))
                            act.activation(ptH[:, rr % 2, 0:w], pT[:, (ph.round0 + rr) % 2, 0:w],
                                           ACT.Copy).then_inc(sem["pt_hi"], 1)

                        def side_slot(t, c_):
                            off, w = st.chunks[c_]
                            s = (t + 1) * n + c_
                            pb = bank(ph, s)
                            act.wait_ge(sem["mm_done"], slots_at(ph, s, i, 4 * n))
                            u = t * n + c_
                            buf, used = u % 2, max(0, u - n) // 2
                            act.wait_ge(gb_out[buf],
                                        i * (16 * n) + (START["gb_out"] + 16 * (gb_used(ph) + used)))
                            act.wait_ge(slot_read[bank(ph, 2 * n - 1)],
                                        reads_at(ph, 2 * n - 1 - (4 * n if t == 0 else 0), i, 4 * n))
                            gate = act.activation(gst[:, buf, 0:w], pp[:, pb, 0:w], ACT.Tanh,
                                                  scale=0.5)
                            if t == 0:
                                gate.then_inc(sem["gate_tanh"], 1)
                            else:
                                gate.then_inc(slot_read[pb], 1)
                                act.wait_ge(slot_read[bank(ph, s)], reads_at(ph, s, i, 4 * n))
                                act.dma_start(gb_keep[i * 2 + (t - 1)][:, off:off + w],
                                              gst[:, buf, 0:w]).then_inc(gb_out[buf], 16)
                            if c_ == n - 1:
                                high_part(ph, 1 + t, i)

                        q_chunk(0)
                        for b, parts in enumerate(steps):
                            rounds = len(st.rounds(b - 1)) if b else 0
                            for r in range(min(rounds, 2)):
                                pt_high(b - 1, r)
                            if b < nb:
                                free = st.round_of(b - 1) if b else -len(st.rounds(nb - 1))
                                act.wait_ge(sem["sinkin_ready"],
                                            at("sinkin_ready", ph, b + 1, i, nb))
                                act.activation(sinkexp[:, b % 2, :], sinkin[:, b % 2, :], ACT.Exp)
                                act.wait_ge(sem["pt_done"], at("pt_done", ph, free, i, R))
                                W = len(st.key_tiles(b)) * BLK
                                for h in range(2):
                                    act.activation(prob[:, b % 2, h, 0:W], pS[:, h * W:(h + 1) * W],
                                                   ACT.Exp, bias=negm[:, b % 2, h:h + 1], scale=SCALE,
                                                   accum_out=rsum[:, b % 2, h:h + 1])\
                                        .then_inc(sem["exp_done"], 1)
                            if b == 0:
                                for c_ in range(1, n):
                                    q_chunk(c_)
                                high_part(ph, 0, i)
                            for t, c_ in slots_done(parts[:2]):
                                side_slot(t, c_)
                            for r in range(2, rounds):
                                pt_high(b - 1, r)
                            for t, c_ in slots_done(parts[2:3]):
                                side_slot(t, c_)
                            if b:
                                rr = st.round_of(b) - 1
                                act.wait_ge(av_done[rr % 2],
                                            no_less(i * (R // 2) + (START["av_done"] + ph.av0 // 2 + rr // 2 + 1)))
                                act.wait_ge(sem["att_done"], at("att_done", ph, b - 1, i, nb))
                                act.activation(o_half[:], pO[HD:P, 0:2 * BLK], ACT.Copy)\
                                    .then_inc(sem["att_half"], 1)
                    by_pair(act, act_pair)
                elif ph.kind == "mixb":
                    act.wait_ge(sem["yb_done"], at("yb_done", ph))
                    for k in range(CT):
                        act.activation(yH[:, k, 0:st.T], yb[st.name][:, k, :], ACT.Copy)\
                            .then_inc(sem["y_hi"], 1)
                    with act.Fori(0, 2) as i:
                        for j in range(2):
                            high_part(ph, j, i)
                elif ph.kind == "conv":
                    act.wait_ge(sem["mm_done"], slots_at(ph, -1))
                    act.wait_ge(sem["y_lo"], at("y_lo", ph))
                    with act.Fori(0, CT) as i:
                        for c_, (off, w) in enumerate(st.chunks):
                            act.wait_ge(sem["mm_done"], slots_at(ph, c_, i, 4 * n))
                            act.wait_ge(sem["y_lo"], at("y_lo", ph, 0, i, n))
                            act.activation(cb[st.name][:, off:off + w], pp[:, bank(ph, c_), 0:w],
                                           ACT.Copy).then_inc(slot_read[bank(ph, c_)], 1)
                        high_part(ph, 0, i)
                        high_part(ph, 1, i)
                        for c_, (off, w) in enumerate(st.chunks):
                            s = 2 * n + c_
                            act.wait_ge(sem["mm_done"], slots_at(ph, s, i, 4 * n))
                            if c_:
                                act.wait_ge(slot_read[bank(ph, s - 1)],
                                            reads_at(ph, s - 1, i, 4 * n))
                            act.activation(th[:, 0:w], pp[:, bank(ph, s), 0:w], ACT.Tanh, scale=0.5)\
                                .then_inc(sem["gate_tanh"], 1)
                        high_part(ph, 2, i)
                        for c_, (off, w) in enumerate(st.chunks):
                            act.wait_ge(slot_read[bank(ph, 3 * n + c_)],
                                        reads_at(ph, 3 * n + c_, i, 4 * n))
                            act.activation(yH[:, i, off:off + w], yv[:, c_, 0:w], ACT.Copy)\
                                .then_inc(sem["y_hi"], 1)
                        high_part(ph, 3, i)
                elif ph.kind == "mixa":
                    act.wait_ge(sem["y_lo"], at("y_lo", ph))
                    with act.Fori(0, 2) as i:
                        for h in range(2):
                            for e in range(2):
                                for c_, (off, w) in enumerate(st.chunks):
                                    s = (4 * h + e) * n + c_
                                    act.wait_ge(sem["mm_done"], slots_at(ph, s, i, 8 * n))
                                    act.wait_ge(sem["m_done"],
                                                at("m_done", ph, 2 * h * n, i, 4 * n))
                                    act.activation(tga[:, e, off:off + w], pp[:, bank(ph, s), 0:w],
                                                   ACT.Tanh, scale=0.5)\
                                        .then_inc(slot_read[bank(ph, s)], 1)
                                high_part(ph, 3 * h + e, i)
                            high_part(ph, 3 * h + 2, i)
                elif ph.kind == "wout":
                    act.wait_ge(sem["m_done"], at("m_done", ph))
                    act.wait_ge(sem["mm_done"], slots_at(ph, -1))
                    for k in range(KT):
                        act.activation(hH[:, k, 0:st.T], m[st.name][:, k, :], ACT.Copy)\
                            .then_inc(sem["mh_ready"], 1)

                    def wout_turn(i, more=True, ph=ph, n=n):
                        for j in range(2):
                            for c_ in range(n):
                                act.wait_ge(slot_read[bank(ph, j * n + c_)],
                                            reads_at(ph, j * n + c_, i, 2 * n))
                                square(ph, j * n + c_, i * 2 + j, c_, i, 2 * n)
                            if more:
                                high_part(ph, j, i)

                    if ph.tile0 + KT == n_tiles:
                        with act.Fori(0, KT // 2 - 1) as i:
                            wout_turn(i)
                        wout_turn(KT // 2 - 1, more=False)
                    else:
                        with act.Fori(0, KT // 2) as i:
                            wout_turn(i)

        @block.vector
        def _(dve):
            def rope(ph, n, s, i=0, turn=0, slots=0):
                off, w = ph.st.chunks[n]
                dve.wait_ge(sem["stack_lo"], at("stack_lo", ph, n, i, turn))
                dve.wait_ge(slot_read[bank(ph, s)], reads_at(ph, s, i, slots))
                dve.tensor_tensor(rout[:, 0:w], rraw[:, 0:w], cos_s[:, off:off + w], ALU.mult)\
                    .then_inc(sem["rope_cos"], 1)
                dve.stream_shuffle(rsh[:, 0:w], rraw[:, 0:w], list(range(16, 32)) + list(range(16)))\
                    .then_inc(sem["rope_shuf"], 1)
                dve.wait_ge(sem["rope_cos"], at("rope_cos", ph, n + 1, i, turn))
                dve.wait_ge(sem["rope_sin"], at("rope_sin", ph, n + 1, i, turn))
                dve.tensor_tensor(rout[:, 0:w], rout[:, 0:w], rsh[:, 0:w], ALU.add)\
                    .then_inc(sem["rope_out"], 1)

            def add_square(ph, r, c_, i=0, per=0):
                off, w = ph.st.chunks[c_]
                a = acc[ph.st.name][:, off:off + w]
                dve.wait_ge(sem["sq_ready"], at("sq_ready", ph, r + 1, i, per))
                dve.wait_ge(sem["sq_added"], at("sq_added", ph, r, i, per))
                dve.tensor_tensor(a, a, sq[:, r % 2, 0:w], ALU.add).then_inc(sem["sq_added"], 1)

            dve.wait_ge(vec_mm, 1)
            dve.tensor_copy(vec[:], pO[:, 0:V_ALL]).then_inc(vec_ready, 1)
            dve.wait_ge(tab_in, 48)
            dve.tensor_scalar(nsink[:], sink[:], -1.0, None, ALU.mult).then_inc(nsink_ready, 1)
            dve.wait_ge(vec_ready, 1)
            dve.wait_ge(silu_tanh, 1)
            dve.scalar_tensor_tensor(
                out=silu_c[:].rearrange("p (k s) -> p s k", s=2),
                in0=silu_t[:].rearrange("p (s k) -> p s k", s=2), scalar=1.0,
                in1=vec[:, 0:2 * KT].rearrange("p (s k) -> p s k", s=2),
                op0=ALU.add, op1=ALU.mult).then_inc(silu_ready, 1)
            dve.wait_ge(nsink_ready, 1)

            for ph in phases:
                L, st, n = ph.layer, ph.st, ph.st.nch if ph.st else 0
                s_ = s_of(ph) if st else 0
                if ph.kind == "mod":
                    dve.wait_ge(sem["mod_mm"], at("mod_mm", ph, MODS // MOD_GROUP))
                    for s in (-2, -1):
                        dve.wait_ge(slot_read[bank(ph, s)], reads_at(ph, s))
                    for s in range(2):
                        last = dve.scalar_tensor_tensor(
                            out=modv[:, :, s],
                            in0=pS[:, 0:2 * MODS].rearrange("p (t s) -> p t s", s=2)[:, :, s],
                            scalar=0.5, in1=vec[:, V_BM + L * MODS:V_BM + (L + 1) * MODS],
                            op0=ALU.mult, op1=ALU.add)
                    last.then_inc(sem["modv_ready"], 1)
                    dve.wait_ge(sem["modv_ready"], at("modv_ready", ph, 1))
                    dve.tensor_scalar(modv[:, 2 * KT:3 * KT, :], modv[:, 2 * KT:3 * KT, :], 0.25,
                                      None, ALU.mult)
                    for s in range(2):
                        last = dve.scalar_tensor_tensor(
                            out=mod_a[:, :, s], in0=modv[:, KT:2 * KT, s], scalar=1.0,
                            in1=vec[:, V_NW + L * KT:V_NW + (L + 1) * KT],
                            op0=ALU.add, op1=ALU.mult)
                    last.then_inc(sem["mod_done"], 1)
                    dve.wait_ge(sem["mod_done"], at("mod_done", ph, 1))
                elif ph.kind == "load":
                    dve.wait_ge(vec_mm, 1)
                    dve.wait_ge(sem["mm_done"], slots_at(ph, -1))
                    dve.wait_ge(sem["m_done"], at("m_done", ph))
                    dve.memset(acc[st.name][:, 0:st.T], 0.0).then_inc(sem["acc_zero"], 1)
                    for b in range(st.blocks):
                        for h in range(2):
                            dve.wait_ge(sem["xt_mm"], at("xt_mm", ph, 2 * b + h + 1))
                            dve.tensor_copy(x_st[st.name][:, 4 * h:4 * h + 4, b * P:(b + 1) * P],
                                            pT[:, (ph.round0 + h) % 2, :]
                                            .rearrange("p (k t) -> p k t", k=4))\
                                .then_inc(sem["xt_copied"], 1)
                        c_ = b * P // CH
                        if b == min(st.blocks, (c_ + 1) * CH // P) - 1:
                            dve.wait_ge(sem["acc_zero"], at("acc_zero", ph, 1))
                            for k in range(KT):
                                add_square(ph, c_ * KT + k, c_)
                elif ph.kind in ("norm", "final"):
                    src, rms = x_st[st.name], acc[st.name]
                    for c_, (off, w) in enumerate(st.chunks):
                        dve.wait_ge(sem["rms_ready"], at("rms_ready", ph, c_ + 1))
                        dve.reciprocal(rms[:, off:off + w], rms[:, off:off + w])\
                            .then_inc(sem["rstd_ready"], 1)
                        dve.wait_ge(sem["rstd_ready"], at("rstd_ready", ph, c_ + 1))
                        for k in range(KT):
                            r = c_ * KT + k
                            if ph.kind == "final":
                                dve.scalar_tensor_tensor(
                                    out=xs[:, k, off:off + w], in0=xs[:, k, off:off + w],
                                    scalar=vec[:, V_FN + k:V_FN + k + 1], in1=rms[:, off:off + w],
                                    op0=ALU.mult, op1=ALU.mult).then_inc(sem["hn_ready"], 1)
                                continue
                            dve.scalar_tensor_tensor(
                                out=hn[:, r % 2, 0:w], in0=src[:, k, off:off + w],
                                scalar=mod_a[:, k, s_:s_ + 1], in1=rms[:, off:off + w],
                                op0=ALU.mult, op1=ALU.mult).then_inc(sem["hn_ready"], 1)
                            dve.wait_ge(sem["hn_ready"], at("hn_ready", ph, r + 1))
                            dve.wait_ge(sem["hl_ready"], at("hl_ready", ph, r - 1))
                            dve.tensor_scalar(hf[:, r % 2, 0:w], hn[:, r % 2, 0:w],
                                              modv[:, k, s_:s_ + 1], None, ALU.add)\
                                .then_inc(sem["hf_ready"], 1)
                    if ph.kind == "final":
                        for b in range(SEQ // P):
                            dve.wait_ge(sem["pt_done"], at("pt_done", ph, 2 * b + 2))
                            dve.wait_ge(out_sent[b % 2], no_less(16 * (b // 2)))
                            dve.tensor_copy(o_rows[:, b % 2, CH:D], pT[:, (ph.round0 + 1) % 2, :])\
                                .then_inc(out_right, 1)
                elif ph.kind == "kv":
                    for c_, (off, w) in enumerate(st.chunks):
                        t0, nt = (st.key0 + off) // BLK, w // BLK
                        dve.wait_ge(sem["pt_hi"], at("pt_hi", ph, c_ + 1))
                        dve.tensor_tensor(v_all[:, t0:t0 + nt, :, HD:P],
                                          pT[:, (ph.round0 + c_) % 2, 0:w]
                                          .rearrange("p (t g d) -> p t g d", t=nt, g=KV_HEADS),
                                          v_all[:, t0:t0 + nt, :, 0:HD].bitcast(F32), ALU.subtract)\
                            .then_inc(sem["pt_copied"], 1)
                    for c_, (off, w) in enumerate(st.chunks):
                        if st.lat:
                            rope(ph, c_, n + c_)
                            dve.wait_ge(sem["rope_out"], at("rope_out", ph, c_ + 1))
                        r = rout if st.lat else rraw
                        cols = slice(st.key0 + off, st.key0 + off + w)
                        dve.wait_ge(sem["stack_hi"], at("stack_hi", ph, c_ + 1))
                        for g in range(KV_HEADS):
                            own = slice(g * HD, (g + 1) * HD)
                            for half in (0, HD):
                                last = dve.tensor_tensor(kL[half:half + HD, g, cols], r[own, 0:w],
                                                         kH[own, g, cols].bitcast(F32), ALU.subtract)
                        last.then_inc(sem["stack_lo"], 1)
                elif ph.kind == "attn":
                    nb, R, steps = st.blocks, av_turn(ph), fills(st)

                    def dve_pair(i, g, ph=ph, L=L, st=st, n=n, nb=nb, R=R, steps=steps):
                        for b in range(2):
                            dve.wait_ge(av_done[b], i * (R // 2) + (START["av_done"] + ph.av0 // 2))
                        dve.wait_ge(sem["pt_copied"], at("pt_copied", ph, 0, i, R))
                        mine = slice(st.key_tiles(0)[0], TOK // BLK)
                        dve.tensor_scalar(v_cur[:, mine], v_all[:, mine, g, :].bitcast(F32), 1.0,
                                          None, ALU.mult).then_inc(sem["vcur_ready"], 1)

                        def q_chunk(c_):
                            off, w = st.chunks[c_]
                            if st.lat:
                                rope(ph, c_, c_, i, n, 4 * n)
                                dve.wait_ge(sem["rope_out"], at("rope_out", ph, c_ + 1, i, n))
                            r = rout if st.lat else rraw
                            dve.wait_ge(sem["stack_hi"], at("stack_hi", ph, c_ + 1, i, n))
                            dve.tensor_tensor(q_st[HD:P, 0, off:off + w], r[0:HD, 0:w],
                                              q_st[0:HD, 0, off:off + w].bitcast(F32), ALU.subtract)
                            dve.tensor_tensor(q_st[0:HD, 1, off:off + w], r[HD:P, 0:w],
                                              q_st[HD:P, 1, off:off + w].bitcast(F32), ALU.subtract)\
                                .then_inc(sem["stack_lo"], 1)

                        def pt_low(b, r):
                            rr = st.round_of(b) + r
                            w = len(st.rounds(b)[r]) * 2 * BLK
                            dve.wait_ge(sem["pt_hi"], at("pt_hi", ph, rr + 1, i, R))
                            dve.tensor_tensor(ptL[:, rr % 2, 0:w], pT[:, (ph.round0 + rr) % 2, 0:w],
                                              ptH[:, rr % 2, 0:w].bitcast(F32), ALU.subtract)\
                                .then_inc(sem["pt_copied"], 1)

                        def side_slot(t, c_):
                            if t:
                                return
                            off, w = st.chunks[c_]
                            dve.wait_ge(sem["gate_tanh"], at("gate_tanh", ph, c_ + 1, i, n))
                            dve.scalar_tensor_tensor(out=szb[:, off:off + w],
                                                     in0=gst[:, c_ % 2, 0:w],
                                                     scalar=1.0, in1=pp[:, bank(ph, n + c_), 0:w],
                                                     op0=ALU.add, op1=ALU.mult)\
                                .then_inc(slot_read[bank(ph, n + c_)], 1)

                        q_chunk(0)
                        for b, parts in enumerate(steps):
                            rounds = len(st.rounds(b - 1)) if b else 0
                            par = b % 2
                            if b < nb:
                                W = len(st.key_tiles(b)) * BLK
                                heads = bass.ds(i * 2 + L * HEADS, 2)
                                dve.wait_ge(sem["qk_done"], at("qk_done", ph, b + 1, i, nb))
                                dve.tensor_reduce(mx[:, par, :],
                                                  pS[:, 0:2 * W].rearrange("p (h w) -> p h w", h=2),
                                                  AX.X, ALU.max).then_inc(sem["max_ready"], 1)
                                dve.wait_ge(sem["max_ready"], at("max_ready", ph, b + 1, i, nb))
                                dve.scalar_tensor_tensor(out=negm[:, par, :], in0=mx[:, par, :],
                                                         scalar=-SCALE, in1=nsink[:, heads],
                                                         op0=ALU.mult, op1=ALU.min)\
                                    .then_inc(sem["negm_ready"], 1)
                                dve.wait_ge(sem["negm_ready"], at("negm_ready", ph, b + 1, i, nb))
                                dve.tensor_tensor(sinkin[:, par, :], negm[:, par, :], sink[:, heads],
                                                  ALU.add).then_inc(sem["sinkin_ready"], 1)
                            for r in range(min(rounds, 2)):
                                pt_low(b - 1, r)
                            if b < nb:
                                for h in range(2):
                                    one = (slice(None), par, slice(h, h + 1))
                                    dve.wait_ge(sem["exp_done"],
                                                at("exp_done", ph, 2 * b + h + 1, i, 2 * nb))
                                    dve.tensor_tensor(rsum[one], rsum[one], sinkexp[one], ALU.add)\
                                        .then_inc(sem["den_ready"], 1)
                                    dve.wait_ge(sem["den_ready"],
                                                at("den_ready", ph, 2 * b + h + 1, i, 2 * nb))
                                    dve.reciprocal(rden[one], rsum[one])\
                                        .then_inc(sem["rden_ready"], 1)
                                for h in range(2):
                                    pr = prob[:, par, h, 0:W]
                                    dve.wait_ge(sem["rden_ready"],
                                                at("rden_ready", ph, 2 * b + h + 1, i, 2 * nb))
                                    dve.tensor_scalar(pr, pr, rden[:, par, h:h + 1], None,
                                                      ALU.mult).then_inc(sem["p_ready"], 1)
                            if b == 0:
                                for c_ in range(1, n):
                                    q_chunk(c_)
                            for t, c_ in slots_done(parts[:2]):
                                side_slot(t, c_)
                            for r in range(2, rounds):
                                pt_low(b - 1, r)
                            for t, c_ in slots_done(parts[2:3]):
                                side_slot(t, c_)
                            if b:
                                q = slice((b - 1) * BLK, b * BLK)
                                dve.wait_ge(sem["att_half"], at("att_half", ph, b, i, nb))
                                y = yb[st.name]
                                dve.tensor_tensor(y[0:HD, i, q], pO[0:HD, 0:BLK], o_half[:, 0:BLK],
                                                  ALU.add)
                                dve.tensor_tensor(y[HD:P, i, q], pO[0:HD, BLK:2 * BLK],
                                                  o_half[:, BLK:2 * BLK], ALU.add)\
                                    .then_inc(sem["att_done"], 1)
                        dve.wait_ge(sem["att_done"], at("att_done", ph, nb, i, nb))
                        for c_ in range(n):
                            dve.wait_ge(slot_read[bank(ph, n + c_)], reads_at(ph, n + c_, i, 4 * n))
                        y = yb[st.name][:, i, 0:st.T]
                        dve.tensor_tensor(y, y, szb[:, 0:st.T], ALU.mult)\
                            .then_inc(sem["yb_done"], 1)
                        dve.wait_ge(sem["yb_done"], at("yb_done", ph, 1, i, 1))
                    by_pair(dve, dve_pair)
                elif ph.kind == "mixb":
                    for k in range(CT):
                        dve.wait_ge(sem["y_hi"], at("y_hi", ph, k + 1))
                        dve.tensor_tensor(yL[:, k, 0:st.T], yb[st.name][:, k, :],
                                          yH[:, k, 0:st.T].bitcast(F32), ALU.subtract)\
                            .then_inc(sem["y_lo"], 1)
                    loads = before(ph, "mixb", lambda p: 4)
                    with dve.Fori(0, 2) as i:
                        for d in range(4):
                            dve.wait_ge(gb_in[d % 2], no_less(i * 32 + 16 * (loads + d // 2 + 1)))
                            for c_, (off, w) in enumerate(st.chunks):
                                s = d * n + c_
                                dve.wait_ge(sem["mm_done"], slots_at(ph, s, i, 4 * n))
                                dve.scalar_tensor_tensor(
                                    out=m[st.name][:, i * 4 + d, off:off + w],
                                    in0=tgb[:, d % 2, off:off + w], scalar=1.0,
                                    in1=pp[:, bank(ph, s), 0:w], op0=ALU.add, op1=ALU.mult)\
                                    .then_inc(slot_read[bank(ph, s)], 1)
                elif ph.kind == "conv":
                    for s in (-2, -1):
                        dve.wait_ge(slot_read[bank(ph, s)], reads_at(ph, s))
                    dve.memset(cu[:, 0:1], 0.0)
                    dve.memset(cu[:, st.T + 1:st.T + 2], 0.0).then_inc(sem["halo_zero"], 1)
                    dve.wait_ge(sem["halo_zero"], at("halo_zero", ph, 1))
                    u, v = cb[st.name], cv[st.name]
                    with dve.Fori(0, CT) as i:
                        for c_, (off, w) in enumerate(st.chunks):
                            s = n + c_
                            dve.wait_ge(slot_read[bank(ph, c_)], reads_at(ph, c_, i, 4 * n))
                            dve.wait_ge(sem["mm_done"], slots_at(ph, s, i, 4 * n))
                            dve.wait_ge(sem["tap_done"], at("tap_done", ph, 0, i, 4))
                            dve.tensor_tensor(cu[:, 1 + off:1 + off + w], u[:, off:off + w],
                                              pp[:, bank(ph, s), 0:w], ALU.mult)\
                                .then_inc(slot_read[bank(ph, s)], 1)
                        for c_ in range(n):
                            dve.wait_ge(slot_read[bank(ph, n + c_)], reads_at(ph, n + c_, i, 4 * n))
                        for tap in range(CONV_K):
                            wt = vec[:, bass.ds(i + (V_CW + (L * CONV_K + tap) * CT), 1)]
                            if tap == 0:
                                dve.tensor_scalar(v[:, 0:st.T], cu[:, 0:st.T], wt, None, ALU.mult)\
                                    .then_inc(sem["tap_done"], 1)
                            else:
                                dve.scalar_tensor_tensor(
                                    out=v[:, 0:st.T], in0=cu[:, tap:tap + st.T], scalar=wt,
                                    in1=v[:, 0:st.T], op0=ALU.mult, op1=ALU.add)\
                                    .then_inc(sem["tap_done"], 1)
                            dve.wait_ge(sem["tap_done"], at("tap_done", ph, tap + 1, i, 4))
                        for c_, (off, w) in enumerate(st.chunks):
                            s = 2 * n + c_
                            dve.wait_ge(sem["gate_tanh"], at("gate_tanh", ph, c_ + 1, i, n))
                            dve.scalar_tensor_tensor(out=sz[st.name][:, off:off + w],
                                                     in0=th[:, 0:w], scalar=1.0,
                                                     in1=pp[:, bank(ph, s), 0:w],
                                                     op0=ALU.add, op1=ALU.mult)\
                                .then_inc(slot_read[bank(ph, s)], 1)
                        for c_ in range(n):
                            dve.wait_ge(slot_read[bank(ph, 2 * n + c_)],
                                        reads_at(ph, 2 * n + c_, i, 4 * n))
                        dve.tensor_tensor(v[:, 0:st.T], v[:, 0:st.T], sz[st.name][:, 0:st.T],
                                          ALU.mult).then_inc(sem["tap_done"], 1)
                        dve.wait_ge(sem["tap_done"], at("tap_done", ph, 4, i, 4))
                        for c_, (off, w) in enumerate(st.chunks):
                            s = 3 * n + c_
                            dve.wait_ge(sem["mm_done"], slots_at(ph, s, i, 4 * n))
                            dve.tensor_tensor(yv[:, c_, 0:w], v[:, off:off + w],
                                              pp[:, bank(ph, s), 0:w], ALU.mult)\
                                .then_inc(slot_read[bank(ph, s)], 1)
                            dve.wait_ge(slot_read[bank(ph, s)], reads_at(ph, s, i, 4 * n))
                            dve.wait_ge(sem["y_hi"], at("y_hi", ph, c_ + 1, i, n))
                            dve.tensor_tensor(yL[:, i, off:off + w], yv[:, c_, 0:w],
                                              yH[:, i, off:off + w].bitcast(F32), ALU.subtract)\
                                .then_inc(sem["y_lo"], 1)
                elif ph.kind == "mixa":
                    with dve.Fori(0, 2) as i:
                        for h in range(2):
                            for e in range(2):
                                for c_, (off, w) in enumerate(st.chunks):
                                    s = (4 * h + 2 + e) * n + c_
                                    q = (2 * h + e) * n + c_
                                    dve.wait_ge(slot_read[bank(ph, s - 2 * n)],
                                                reads_at(ph, s - 2 * n, i, 8 * n))
                                    dve.wait_ge(sem["mm_done"], slots_at(ph, s, i, 8 * n))
                                    dve.scalar_tensor_tensor(
                                        out=gm[:, q % 2, 0:w], in0=tga[:, e, off:off + w],
                                        scalar=1.0, in1=pp[:, bank(ph, s), 0:w],
                                        op0=ALU.add, op1=ALU.mult)\
                                        .then_inc(slot_read[bank(ph, s)], 1)
                                    dve.wait_ge(slot_read[bank(ph, s)], reads_at(ph, s, i, 8 * n))
                                    md = m[st.name][:, i * 4 + (2 * h + e), off:off + w]
                                    dve.tensor_tensor(md, md, gm[:, q % 2, 0:w], ALU.add)\
                                        .then_inc(sem["m_done"], 1)
                                    dve.wait_ge(sem["m_done"], at("m_done", ph, q + 1, i, 4 * n))
                elif ph.kind == "wout":
                    for k in range(KT):
                        dve.wait_ge(sem["mh_ready"], at("mh_ready", ph, k + 1))
                        dve.tensor_tensor(hL[:, k, 0:st.T], m[st.name][:, k, :],
                                          hH[:, k, 0:st.T].bitcast(F32), ALU.subtract)\
                            .then_inc(sem["ml_ready"], 1)
                    dve.memset(acc[st.name][:, 0:st.T], 0.0).then_inc(sem["acc_zero"], 1)
                    dve.wait_ge(sem["acc_zero"], at("acc_zero", ph, 1))
                    gates = modv[:].rearrange("p t s -> p (t s)")
                    with dve.Fori(0, KT // 2) as i:
                        for j in range(2):
                            for c_, (off, w) in enumerate(st.chunks):
                                s = j * n + c_
                                dve.wait_ge(sem["mm_done"], slots_at(ph, s, i, 2 * n))
                                if st.lat and j == 0 and c_ == 0:
                                    dve.wait_ge(sem["x_in"], at("x_in", ph, 16, i, 16))
                                xe = x_st[st.name][:, i * 2 + j, off:off + w]
                                dve.scalar_tensor_tensor(
                                    out=xe, in0=pp[:, bank(ph, s), 0:w],
                                    scalar=gates[:, bass.ds(i * 4 + (4 * KT + 2 * j + s_), 1)],
                                    in1=xe, op0=ALU.mult, op1=ALU.add)\
                                    .then_inc(slot_read[bank(ph, s)], 1)
                                add_square(ph, s, c_, i, 2 * n)

        @block.tensor
        def _(pe):
            def k_step(ph, j, s, c_, k, kts, a_hi, a_lo, e=0):
                off, w = ph.st.chunks[c_]
                wb = (ph.tile0 + j) % 2
                col = (k * (KT // kts) + e) * P
                o = pp[:, bank(ph, s), 0:w]
                hi, lo = wH[:, wb, col:col + P], wL[:, wb, col:col + P]
                ah, al = a_hi[:, k, off:off + w], a_lo[:, k, off:off + w]
                pe.matmul(o, hi, ah, start=(k == 0), stop=False)
                pe.matmul(o, hi, al, start=False, stop=False)
                return pe.matmul(o, lo, ah, start=False, stop=(k == kts - 1))

            def open_slot(ph, s, i=0, per=0):
                pe.wait_ge(slot_read[bank(ph, s - 2)], reads_at(ph, s - 2, i, per))

            def open_tile(ph, j, i=0, per=0):
                pe.wait_ge(sem["w_lo"], no_less(i * per + (ph.tile0 + j + 1)))

            def project(ph, j, s0, a_hi, a_lo, kts=KT, outs=1, i=0, tiles=0, slots=0, ready=None):
                open_tile(ph, j, i, tiles)
                n = ph.st.nch
                for e in range(outs):
                    for c_ in range(n):
                        s = s0 + e * n + c_
                        open_slot(ph, s, i, slots)
                        for k in range(kts):
                            if ready and e == 0 and c_ == 0:
                                pe.wait_ge(sem[ready], at(ready, ph, k + 1))
                            last = k_step(ph, j, s, c_, k, kts, a_hi, a_lo, e)
                            if k == kts - 1:
                                last.then_inc(sem["mm_done"], 1)

            def score_pieces(st, b, h):
                tiles = st.key_tiles(b)
                pieces, masks = [], []
                for t, kb in enumerate(tiles):
                    col = (h * len(tiles) + t) * BLK
                    if pieces and col % CH and pieces[-1][1] + pieces[-1][2] == kb * BLK:
                        pieces[-1][2] += BLK
                    else:
                        pieces.append([col, kb * BLK, BLK])
                    if st.lat and kb < st.blocks and kb != b:
                        masks.append((col, mask_prev if kb < b else mask_next))
                return pieces, masks

            pe.wait_ge(const_ready, 10)
            pe.wait_ge(vec_in, 16 * 6)
            pe.transpose(pO[:, 0:V_ALL], vec_rows[:], ident[0:V_ALL, 0:V_ALL]).then_inc(vec_mm, 1)
            pe.wait_ge(silu_ready, 1)

            for ph in phases:
                L, st, n = ph.layer, ph.st, ph.st.nch if ph.st else 0
                if ph.kind == "mod":
                    groups = MODS // MOD_GROUP
                    pe.wait_ge(sem["exp_done"], at("exp_done", ph))
                    pe.wait_ge(sem["rms_ready"], at("rms_ready", ph))
                    for g in range(groups):
                        pe.wait_ge(wm_in[g % 2], 16 * (L * groups // 2 + g // 2 + 1))
                        for t in range(MOD_GROUP):
                            col = 2 * (g * MOD_GROUP + t)
                            for k in range(KT):
                                last = pe.matmul(pS[:, col:col + 2], wm[:, g % 2, k, t * P:(t + 1) * P],
                                                 silu_c[:, 2 * k:2 * k + 2],
                                                 start=(k == 0), stop=(k == KT - 1))
                        last.then_inc(sem["mod_mm"], 1)
                elif ph.kind == "load":
                    earlier = before(ph, "load", lambda p: p.st.blocks // 2)
                    pe.wait_ge(sem["pt_copied"], at("pt_copied", ph))
                    for b in range(st.blocks):
                        pe.wait_ge(xr_in[b % 2], 16 * (earlier + b // 2 + 1))
                        for h in range(2):
                            pe.wait_ge(sem["xt_copied"], at("xt_copied", ph, 2 * b + h - 1))
                            for k in range(4):
                                last = pe.transpose(
                                    pT[:, (ph.round0 + h) % 2, k * P:(k + 1) * P],
                                    x_rows[:, b % 2, (4 * h + k) * P:(4 * h + k + 1) * P], ident[:])
                            last.then_inc(sem["xt_mm"], 1)
                elif ph.kind in ("norm", "final"):
                    pe.wait_ge(sem["exp_done"], at("exp_done", ph))
                    pe.wait_ge(sem["modv_ready"], at("modv_ready", ph))
                    pe.wait_ge(sem["rms_ready"], at("rms_ready", ph))
                    made = next(p for p in reversed(phases[:phases.index(ph)])
                                if p.kind in ("load", "wout") and p.st is st)
                    pe.wait_ge(sem["sq_added"], at("sq_added", made, KT * n))
                    for c_, (off, w) in enumerate(st.chunks):
                        pe.matmul(pS[:, c_ * CH:c_ * CH + w], ones[:], acc[st.name][:, off:off + w],
                                  start=True, stop=True).then_inc(sem["sum_done"], 1)
                    if ph.kind == "final":
                        pe.wait_ge(sem["pt_copied"], at("pt_copied", ph))
                        for b in range(SEQ // P):
                            pe.wait_ge(sem["hn_ready"], at("hn_ready", ph, (b * P // CH + 1) * KT))
                            for h in range(2):
                                pe.wait_ge((out_left, out_right)[h], no_less(b))
                                for k in range(4):
                                    last = pe.transpose(
                                        pT[:, (ph.round0 + h) % 2, k * P:(k + 1) * P],
                                        xs[:, 4 * h + k, b * P:(b + 1) * P], ident[:])
                                last.then_inc(sem["pt_done"], 1)
                elif ph.kind == "kv":
                    for j in range(2):
                        open_tile(ph, j)
                        for c_ in range(n):
                            s = j * n + c_
                            open_slot(ph, s)
                            for k in range(KT):
                                if j == 0:
                                    pe.wait_ge(sem["hl_ready"],
                                               at("hl_ready", ph, (c_ - n) * KT + k + 1))
                                last = k_step(ph, j, s, c_, k, KT, hH, hL)
                            last.then_inc(sem["mm_done"], 1)
                            if j == 1:
                                pe.wait_ge(slot_read[bank(ph, c_)], reads_at(ph, c_))
                                pe.wait_ge(sem["pt_copied"], at("pt_copied", ph, c_ - 1))
                                for t in range(ph.st.chunks[c_][1] // P):
                                    last = pe.transpose(
                                        pT[:, (ph.round0 + c_) % 2, t * P:(t + 1) * P],
                                        vraw[:, t * P:(t + 1) * P], ident[:])
                                last.then_inc(sem["pt_done"], 1)
                elif ph.kind == "attn":
                    nb, R, steps = st.blocks, av_turn(ph), fills(st)

                    def pe_pair(i, g, ph=ph, st=st, n=n, nb=nb, R=R, steps=steps):
                        project(ph, 0, 0, hH, hL, i=i, tiles=4, slots=4 * n)

                        def side(part):
                            for t, c_, k in part:
                                s = (t + 1) * n + c_
                                if c_ == 0 and k == 0:
                                    open_tile(ph, t + 1, i, 4)
                                if k == 0:
                                    open_slot(ph, s, i, 4 * n)
                                last = k_step(ph, t + 1, s, c_, k, KT, hH, hL)
                                if k == KT - 1:
                                    last.then_inc(sem["mm_done"], 1)

                        def scores(b):
                            pe.wait_ge(sem["stack_lo"], at("stack_lo", ph, b * BLK // CH + 1, i, n))
                            pe.wait_ge(sem["exp_done"], at("exp_done", ph, 2 * b, i, 2 * nb))
                            for h in range(2):
                                q = q_st[:, h, b * BLK:(b + 1) * BLK]
                                pieces, masks = score_pieces(st, b, h)
                                for col, key, keys in pieces:
                                    inside = [x for x in masks if col <= x[0] < col + keys]
                                    o = pS[:, col:col + keys]
                                    pe.matmul(o, q, kH[:, g, key:key + keys], start=True, stop=False)
                                    last = pe.matmul(o, q, kL[:, g, key:key + keys],
                                                     start=False, stop=not inside)
                                    for x in inside:
                                        last = pe.matmul(pS[:, x[0]:x[0] + BLK], ident_b[:], x[1][:],
                                                         start=False, stop=x is inside[-1])
                            last.then_inc(sem["qk_done"], 1)

                        def turn_round(b, r):
                            rr = st.round_of(b) + r
                            pe.wait_ge(sem["pt_copied"], at("pt_copied", ph, rr - 1, i, R))
                            for t in range(len(st.rounds(b)[r])):
                                for h in range(2):
                                    key = (2 * r + t) * BLK
                                    last = pe.transpose(
                                        pT[:, (ph.round0 + rr) % 2,
                                           (2 * t + h) * BLK:(2 * t + h + 1) * BLK],
                                        prob[:, b % 2, h, key:key + BLK], ident[:])
                            last.then_inc(sem["pt_done"], 1)

                        def times_v(b, r):
                            rr = st.round_of(b) + r
                            pe.wait_ge(sem["pt_copied"], at("pt_copied", ph, rr + 1, i, R))
                            if r == 0:
                                pe.wait_ge(sem["att_done"], at("att_done", ph, b, i, nb))
                            for t, kb in enumerate(st.rounds(b)[r]):
                                cols = slice(2 * t * BLK, 2 * (t + 1) * BLK)
                                end = r == len(st.rounds(b)) - 1 and t == len(st.rounds(b)[r]) - 1
                                pe.matmul(pO[:, 0:2 * BLK], v_cur[:, kb, :], ptH[:, rr % 2, cols],
                                          start=(r == 0 and t == 0), stop=False)
                                last = pe.matmul(pO[:, 0:2 * BLK], v_cur[:, kb, :],
                                                 ptL[:, rr % 2, cols], start=False, stop=end)
                            last.then_inc(av_done[rr % 2], 1)

                        for b, parts in enumerate(steps):
                            rounds = len(st.rounds(b - 1)) if b else 0
                            side(parts[3])
                            if b < nb:
                                scores(b)
                            side(parts[0])
                            if b:
                                pe.wait_ge(sem["p_ready"], at("p_ready", ph, 2 * b, i, 2 * nb))
                            for r in range(min(rounds, 2)):
                                turn_round(b - 1, r)
                            side(parts[1])
                            if b == 1:
                                pe.wait_ge(sem["vcur_ready"], at("vcur_ready", ph, 1, i, 1))
                            for r in range(min(rounds, 2)):
                                times_v(b - 1, r)
                            for r in range(2, rounds):
                                turn_round(b - 1, r)
                            side(parts[2])
                            for r in range(2, rounds):
                                times_v(b - 1, r)
                    by_pair(pe, pe_pair)
                elif ph.kind == "mixb":
                    with pe.Fori(0, 2) as i:
                        for j in range(2):
                            project(ph, j, 2 * j * n, yH, yL, kts=CT, outs=2, i=i, tiles=2,
                                    slots=4 * n, ready="y_lo")
                elif ph.kind == "conv":
                    with pe.Fori(0, CT) as i:
                        for j in range(4):
                            project(ph, j, j * n, hH, hL, i=i, tiles=4, slots=4 * n)
                elif ph.kind == "mixa":
                    pe.wait_ge(sem["y_lo"], at("y_lo", ph))
                    with pe.Fori(0, 2) as i:
                        for h in range(2):
                            for e in range(2):
                                project(ph, 3 * h + e, (4 * h + e) * n, hH, hL, i=i, tiles=6,
                                        slots=8 * n)
                            project(ph, 3 * h + 2, (4 * h + 2) * n, yH, yL, kts=CT, outs=2, i=i,
                                    tiles=6, slots=8 * n)
                elif ph.kind == "wout":
                    with pe.Fori(0, KT // 2) as i:
                        for j in range(2):
                            project(ph, j, j * n, hH, hL, i=i, tiles=2, slots=2 * n,
                                    ready="ml_ready")


def rope_tables():
    freqs = HD // 4
    p, t = np.arange(P)[:, None], np.arange(SEQ)[None, :]
    inv_freq = (10000.0 ** (-np.arange(freqs, dtype=np.float32) / freqs)).astype(np.float32)
    place = np.where((p // 32) % 2 == 0, t // GRID_W, t % GRID_W).astype(np.float32)
    ang = place * inv_freq[p % freqs]
    sign = np.where((p // freqs) % 2 == 0, -1.0, 1.0).astype(np.float32)
    return np.cos(ang).astype(np.float32), (np.sin(ang) * sign).astype(np.float32)


_INS = ["x", "c", "ctx", "c_ctx", "norm_w", "w_mod", "b_mod", "w_in", "conv_w", "w_a_out",
        "w_b_out", "attn_sink", "w_o", "final_norm_w"]


def kernel(**inputs):
    import concourse.bacc as bacc
    from concourse.bass_utils import run_bass_kernel_spmd as run

    nc = bacc.Bacc("TRN2", target_bir_lowering=False, num_devices=1)
    cos_t, sin_t = rope_tables()
    arrays = {f"in_{n}": np.ascontiguousarray(inputs[n]) for n in _INS}
    arrays.update({"in_cos": cos_t, "in_sin": sin_t})
    args = [nc.dram_tensor(n, a.shape, mybir.dt.from_np(a.dtype), kind="ExternalInput").ap()
            for n, a in arrays.items()]
    out = nc.dram_tensor("out", (1, SEQ, D), F32, kind="ExternalOutput").ap()
    hybrid_block(nc, *args, out)
    r = run(nc, [arrays], core_ids=[0])
    return r.results[0]["out"]
```

```python
import concourse.bass as bass
import numpy as np
from concourse import mybir
from contextlib import ExitStack

F32 = mybir.dt.float32
F32R = mybir.dt.float32r
BF16 = mybir.dt.bfloat16
ACT = mybir.ActivationFunctionType
ALU = mybir.AluOpType
AX = mybir.AxisListType

D, SEQ, CTX, DEPTH, GRID_W = 1024, 1024, 256, 2, 64
CONV, CONV_K, HEADS, KV_HEADS, HD = 512, 3, 8, 2, 64
ATT, BLK, EPS, NEG = HEADS * HD, 128, 1e-6, -1e30
SCALE = HD ** -0.5
P = 128
KT = D // P
CT = CONV // P
PAIRS = HEADS // 2
TOK = SEQ + CTX
C_B, C_C, C_U, C_Z = 0, CONV, 2 * CONV, 3 * CONV
C_Q = 4 * CONV
C_K = C_Q + ATT
C_V = C_K + KV_HEADS * HD
C_ZB = C_V + KV_HEADS * HD
C_GA = C_ZB + ATT
C_GB = C_GA + D
IN_COLS = C_GB + D
CH = 512
X_PARTS = 4
MODS = 3 * KT
MG = 2 * P
SHIFT_SCALE = 2 * D // MG


class Stream:

    def __init__(self, name, tokens, key0):
        self.name, self.T, self.key0 = name, tokens, key0
        self.chunks = [(o, min(CH, tokens - o)) for o in range(0, tokens, CH)]
        self.nch = len(self.chunks)
        self.blocks = tokens // BLK
        self.lat = name == "lat"

    def key_tiles(self, b):
        own = [k for k in (b - 1, b, b + 1) if 0 <= k < self.blocks] if self.lat else []
        return own + [SEQ // BLK + k for k in range(CTX // BLK)]

    def rounds(self, b):
        t = self.key_tiles(b)
        return [t[n:n + 2] for n in range(0, len(t), 2)]

    def round_of(self, b):
        return sum(len(self.rounds(n)) for n in range(b))


LAT = Stream("lat", SEQ, 0)
CTXS = Stream("ctx", CTX, SEQ)


SIDE_TILES = 3


LEAD, FIRST = 4, 10


def fills(st):
    todo = [(t, c, k) for t in range(SIDE_TILES) for c in range(st.nch) for k in range(KT)]
    first = LEAD + FIRST
    out = [(todo[LEAD:first], [], [], todo[:LEAD])]
    at = first
    for b in range(1, st.blocks + 1):
        n = first + (len(todo) - first) * b // st.blocks - at
        a1 = 1
        a2 = n - 1
        part = todo[at:at + n]
        out.append((part[:a1], part[a1:a1 + a2], part[a1 + a2:], []))
        at += n
    return out


def early(st, b):
    return b >= 2 and len(st.rounds(b - 2)) > 2


def late(st, b):
    return b >= 1 and len(st.rounds(b - 1)) <= 2


def slots_done(parts):
    return [(t, c) for part in parts for t, c, k in part if k == KT - 1]


BODY = {"kv": [1, 1], "attn": [1] * 4, "mixb": [2, 2], "conv": [1] * 4, "mixa": [1, 1, 2] * 2,
        "wout": [1, 1]}


START = {"att_done": 1, "mod_part": 1, "exp_done": 1, "m_done": 1, "pt_copied": 1, "pt_done": 2, "qk_done": 1,
         "tap_done": 1, "slot_read": 1, "av_done": 1, "gb_out": 16}


class Phase:

    def __init__(self, kind, st, layer, base, tile0, slot0, round0, av0):
        self.kind, self.st, self.layer, self.base = kind, st, layer, base
        self.tile0, self.slot0, self.round0, self.av0 = tile0, slot0, round0, av0


def mod_groups(ph):
    if ph.kind != "conv" or ph.layer > 0:
        return 0, 0, 0
    first, layer = (0, 1) if ph.st is LAT else (SHIFT_SCALE, 0)
    return (MODS * P // MG - first) // CT, first, layer


def lows(r):
    return r - r // 3, r // 3


def make_phases():
    order = [("load", CTXS, 0), ("stat", CTXS, 0), ("mod", None, 0)]
    for layer in range(DEPTH):
        last = layer == DEPTH - 1
        for st in (CTXS, LAT):
            order.append(("norm", st, layer))
            if last and st is CTXS:
                order.append(("stat", LAT, layer))
            order.append(("kv", st, layer))
            if last and st is CTXS:
                continue
            order += [(k, st, layer) for k in ("attn", "mixb", "conv", "mixa", "msplit")]
            if not last and st is CTXS:
                order += [("load", LAT, layer), ("stat", LAT, layer)]
            elif not last:
                order += [("mod", None, layer + 1), ("stat", CTXS, layer + 1)]
            order.append(("wout", st, layer))
    order.append(("final", LAT, DEPTH))
    count, out = {k: v for k, v in START.items() if k not in ("slot_read", "av_done", "gb_out")}, []
    tile = slot = rnd = av = 0
    for kind, st, layer in order:
        out.append(Phase(kind, st, layer, dict(count), tile, slot, rnd, av))
        n = st.nch if st else 0
        tiles = slots = rounds = avs = 0
        gain = {}
        if kind == "mod":
            gain = {"mod_done": 1}
            if layer == 0:
                gain.update({"row_ready": SHIFT_SCALE, "row_copied": SHIFT_SCALE,
                             "row_turned": SHIFT_SCALE, "modv_ready": 1})
        elif kind == "load":
            gain = {"xt_mm": 2 * st.blocks, "xt_copied": 2 * st.blocks}
        elif kind == "stat":
            gain = {"sum_done": n, "rms_ready": n, "rstd_ready": n}
        elif kind in ("norm", "final"):
            gain = {}
            if kind == "final":
                gain = {"sum_done": n, "rms_ready": n, "rstd_ready": n}
            else:
                gain.update({"hn_ready": KT * n, "hf_ready": KT * n, "hh_ready": KT * n, "hl_pool": lows(KT * n)[0],
                             "hl_dve": lows(KT * n)[1]})
                if st.lat:
                    gain["x_spilled"] = 16
        elif kind == "kv":
            tiles, slots, rounds = 2, 2 * n, n
            gain = {"stack_hi": n, "stack_lo": n}
        elif kind == "attn":
            tiles, slots = 4 * PAIRS, 4 * PAIRS * n
            rounds = avs = PAIRS * st.round_of(st.blocks)
            nb = PAIRS * st.blocks
            gain = {"stack_hi": PAIRS * n, "stack_lo": PAIRS * n, "vcur_ready": PAIRS,
                    "qk_done": nb, "max_ready": nb, "negm_ready": nb, "sinkin_ready": nb,
                    "exp_done": 2 * nb, "den_ready": 2 * nb, "rden_ready": 2 * nb,
                    "p_ready": 2 * nb, "att_half": nb, "att_done": nb,
                    "gate_tanh": PAIRS * n, "yb_done": PAIRS}
        elif kind == "mixb":
            tiles, slots = KT // 2, KT * n
            gain = {"y_hi": CT, "y_lo": CT}
        elif kind == "conv":
            tiles, slots = 4 * CT, 4 * CT * n
            gain = {"halo_zero": 1, "gate_tanh": CT * n, "tap_done": 4 * CT,
                    "y_hi": CT * n, "y_lo": CT * n}
            groups = CT * mod_groups(out[-1])[0]
            gain.update({"wmt_in": 16 * groups, "row_ready": groups, "row_copied": groups})
            if groups:
                gain.update({"row_turned": CT, "mod_part": CT})
        elif kind == "mixa":
            tiles, slots = KT + KT // 2, 2 * KT * n
            gain = {"m_done": KT * n}
        elif kind == "msplit":
            gain = {"mh_ready": KT, "ml_ready": KT}
        elif kind == "wout":
            tiles, slots = KT, KT * n
            if st.lat:
                gain["x_in"] = 16 * X_PARTS
            if layer == DEPTH - 1:
                gain["out_scaled"] = KT * n
        if kind == "load":
            gain.update({"sq_ready": st.blocks, "sq_added": st.blocks})
        elif kind == "wout":
            gain.update({"acc_zero": 1, "sq_ready": KT * n, "sq_added": KT * n})
        if kind in ("kv", "attn") and st.lat:
            r = n if kind == "kv" else PAIRS * n
            gain.update({"rope_shuf": r, "rope_sin": r, "rope_cos": r, "rope_out": r})
        gain["w_hi"] = gain["w_lo"] = tiles
        gain["mm_done"] = slots
        gain["pt_done"] = gain["pt_hi"] = gain["pt_copied"] = rounds
        for k, v in gain.items():
            count[k] = count.get(k, 0) + v
        tile, slot, rnd, av = tile + tiles, slot + slots, rnd + rounds, av + avs
    return out, tile, sorted(count)


def hybrid_block(nc, x, c, ctx, c_ctx, norm_w, w_mod, b_mod, w_in, conv_w, w_a_out, w_b_out,
                 attn_sink, w_o, final_norm_w, cos_t, sin_t, out):
    phases, n_tiles, counters = make_phases()
    stack = ExitStack()
    with stack:
        def sb(name, shape, dt=F32):
            return stack.enter_context(nc.sbuf_tensor(name, shape, dt))

        def zone(*sets):
            made = {}
            for n, tensors in enumerate(sets):
                with ExitStack() as z:
                    for name, shape, dt in tensors:
                        if n == len(sets) - 1:
                            made[name] = sb(name, shape, dt)
                        else:
                            made[name] = z.enter_context(nc.sbuf_tensor(name, shape, dt))
            return made

        ident = sb("ident", [P, P])
        ident_b = sb("ident_b", [P, P], BF16)
        mask_prev = sb("mask_prev", [P, BLK], BF16)
        mask_next = sb("mask_next", [P, BLK], BF16)
        ones = sb("ones", [P, P])
        eps = sb("eps", [P, 1])
        cos_s = sb("cos_s", [P, SEQ])
        sin_s = sb("sin_s", [P, SEQ])
        V_NW = 2 * KT
        V_BM = V_NW + DEPTH * KT
        V_CW = V_BM + DEPTH * MODS
        V_FN = V_CW + DEPTH * CONV_K * CT
        V_ALL = V_FN + KT
        vec = sb("vec", [P, V_ALL])
        silu_t = sb("silu_t", [P, 2 * KT])
        silu_c = sb("silu_c", [P, 2 * KT])
        modv = sb("modv", [P, DEPTH, MODS, 2])
        mod_a = sb("mod_a", [P, KT, 2])
        sink = sb("sink", [P, DEPTH * HEADS])
        nsink = sb("nsink", [P, DEPTH * HEADS])
        mx, negm, sinkin, sinkexp, rsum, rden = (
            sb(n, [P, 2, 2]) for n in ("mx", "negm", "sinkin", "sinkexp", "rsum", "rden"))
        raw = sb("raw", [P, 2, KT * P])
        wH = sb("wH", [P, 2, KT * P], F32R)
        wL = sb("wL", [P, 2, KT * P], F32R)
        hH = sb("hH", [P, KT, SEQ], F32R)
        hL = sb("hL", [P, KT, SEQ], F32R)
        xc = sb("xc", [P, KT, CTX])
        rstd = sb("rstd", [P, SEQ // P])
        acc_ctx = sb("acc_ctx", [P, CTX])

        z1 = zone([("wm", [P, 4, KT, MG], F32)],
                  [("kH", [P, KV_HEADS, TOK], F32R),
                   ("kL", [P, KV_HEADS, TOK], F32R),
                   ("v_all", [P, TOK // BLK, KV_HEADS, P], F32R)],
                  [("m_lat", [P, KT, SEQ], F32)])
        z2 = zone([("q_st", [P, 2, SEQ], F32R),
                   ("prob", [P, 2, 2, 5 * BLK], F32),
                   ("ptH", [P, 2, CH], F32R), ("ptL", [P, 2, CH], F32R),
                   ("o_half", [HD, 2 * BLK], F32)],
                  [("yH", [P, CT, SEQ], F32R), ("yL", [P, CT, SEQ], F32R)],
                  [("xs", [P, KT, SEQ], F32)])
        z3 = zone([("mrow0", [2, 2, MG], F32)],
                  [("o_rows", [P, 4, D], F32)],
                  [("cb_lat", [P, SEQ], F32), ("cv_lat", [P, SEQ], F32), ("sz_lat", [P, SEQ], F32),
                   ("mrow_lat", [2, 3, MG], F32)],
                  [("yb_ctx", [P, PAIRS, CTX], F32), ("m_ctx", [P, KT, CTX], F32),
                   ("cb_ctx", [P, CTX], F32), ("cv_ctx", [P, CTX], F32), ("sz_ctx", [P, CTX], F32),
                   ("mrow_ctx", [2, 1, MG], F32)],
                  [("yb_lat", [P, PAIRS, SEQ], F32)])
        z4 = zone([("vec_rows", [V_ALL, P], F32), ("head_start", [P, len(START) + 3], F32)],
                  [("acc_lat", [P, SEQ], F32), ("sq", [P, 2, CH], F32), ("hn", [P, 4, CH], F32)],
                  [("above", [P, 2, SEQ], F32), ("x_rows", [P, 2, D], F32)],
                  [("tgb", [P, 2, SEQ], F32)],
                  [("tga", [P, 2, SEQ], F32), ("gm", [P, 2, CH], F32)],
                  [("cu", [P, SEQ + 2], F32), ("yv", [P, 2, CH], F32), ("th", [P, CH], F32),
                   ("wmt", [P, KT, MG], F32)],
                  [("v_cur", [P, TOK // BLK, P], F32R), ("szb", [P, SEQ], F32),
                   ("rraw", [P, CH], F32), ("rsh", [P, CH], F32), ("rout", [P, CH], F32),
                   ("gst", [P, 2, CH], F32)])
        wm, m_lat, kH, kL, v_all = (z1[n] for n in ("wm", "m_lat", "kH", "kL", "v_all"))
        q_st, prob, ptH, ptL, o_half = (z2[n] for n in ("q_st", "prob", "ptH", "ptL", "o_half"))
        wmt, mrow0 = z4["wmt"], z3["mrow0"]
        mrow = {"lat": z3["mrow_lat"], "ctx": z3["mrow_ctx"]}
        yH, yL, xs, o_rows = z2["yH"], z2["yL"], z2["xs"], z3["o_rows"]
        vec_rows, head_start, sq, hn, x_rows = (
            z4[n] for n in ("vec_rows", "head_start", "sq", "hn", "x_rows"))
        tgb, tga, gm, cu, yv, th = (z4[n] for n in ("tgb", "tga", "gm", "cu", "yv", "th"))
        v_cur, rraw, rsh, rout = (z4[n] for n in ("v_cur", "rraw", "rsh", "rout"))
        szb, gst = z4["szb"], z4["gst"]
        vraw = gst[:, 0]
        sq_block = sq[:].rearrange("p r (k t) -> p (r k) t", t=P)
        acc = {"lat": z4["acc_lat"], "ctx": acc_ctx}
        x_st = {"lat": xs, "ctx": xc}
        yb = {"lat": z3["yb_lat"], "ctx": z3["yb_ctx"]}
        m = {"lat": m_lat, "ctx": z3["m_ctx"]}
        cb, cv, sz = ({s: z3[f"{n}_{s}"] for s in ("lat", "ctx")} for n in ("cb", "cv", "sz"))

        x_keep = nc.dram_tensor("x_keep", (P, KT, SEQ), F32).ap()
        gb_keep = nc.dram_tensor("gb_keep", (KT, P, SEQ), F32).ap()

        pp = stack.enter_context(nc.psum_tensor("pp", [P, 2, CH], F32))
        pS = stack.enter_context(nc.psum_tensor("pS", [P, 3 * CH], F32))
        pT = stack.enter_context(nc.psum_tensor("pT", [P, 2, CH], F32))
        pO = stack.enter_context(nc.psum_tensor("pO", [P, CH], F32))

        def new_sem(name):
            return stack.enter_context(nc.semaphore(name))

        sem = {n: new_sem(n) for n in counters}
        const_ready, vec_in, tab_in, vec_mm, vec_ready, nsink_ready, silu_tanh, silu_ready, \
            out_left, out_right = (new_sem(n) for n in (
                "const_ready", "vec_in", "tab_in", "vec_mm", "vec_ready", "nsink_ready",
                "silu_tanh", "silu_ready", "out_left", "out_right"))
        wm_in = [new_sem(f"wm_in{i}") for i in range(4)]
        out_sent = [new_sem(f"out_sent{i}") for i in range(4)]
        raw_in, slot_read, av_done, gb_out, gb_in, xr_in = (
            [new_sem(f"{n}{i}") for i in range(2)] for n in
            ("raw_in", "slot_read", "av_done", "gb_out", "gb_in", "xr_in"))
        block = stack.enter_context(nc.Block())

        w_in_v, w_a_v, w_b_v, w_o_v, w_mod_v = (
            w.rearrange("l (k p) n -> l p k n", p=P) for w in (w_in, w_a_out, w_b_out, w_o, w_mod))

        def count(i, per, first):
            if type(i) is int:
                return max(i * per + first, 0)
            assert first > 0
            return i * per + first

        def at(name, ph, more=0, i=0, per=0):
            return count(i, per, ph.base.get(name, 0) + more)

        def slots_at(ph, s, i=0, per=0):
            return count(i, per, ph.slot0 + s + 1)

        def bank(ph, s):
            return (ph.slot0 + s) % 2

        def reads_at(ph, s, i=0, per=0):
            return count(i, per // 2, (ph.slot0 + s) // 2 + 1 + START["slot_read"])
        def before(ph, kind, of):
            return sum(of(p) for p in phases[:phases.index(ph)] if p.kind == kind)

        def after(ph, kind, st):
            return next(p for p in phases[phases.index(ph):] if (p.kind, p.st) == (kind, st))

        def gb_used(ph):
            return before(ph, "attn", lambda p: PAIRS * p.st.nch)

        def av_turn(ph):
            r = ph.st.round_of(ph.st.blocks)
            assert r % 2 == 0 and ph.av0 % 2 == 0 and ph.slot0 % 2 == 0 and ph.tile0 % 2 == 0
            return r

        def x_made(ph):
            made = next(p for p in phases if (p.kind, p.st, p.layer) == ("wout", LAT, ph.layer - 1))
            return (made.slot0 + KT * made.st.nch) // 2 + START["slot_read"]

        def s_of(ph):
            return 0 if ph.st.lat else 1

        def by_pair(eng, turn):
            with eng.Fori(0, KV_HEADS) as g:
                with eng.Fori(0, PAIRS // KV_HEADS) as j:
                    turn(g * (PAIRS // KV_HEADS) + j, g)

        @block.sync
        def _(sp):
            def load_tile(ph, j, src, i=0, per=0):
                n = ph.tile0 + j
                sp.wait_ge(sem["w_lo"], count(i, per, n - 1))
                dst = raw[:, n % 2, :].rearrange("p (k n) -> p k n", k=src.shape[1])
                sp.dma_start(dst, src).then_inc(raw_in[n % 2], 16)

            place_reg = sp.alloc_register("place")

            def place(value, size):
                sp.reg_mov(place_reg, value * (4 * size))
                return value

            def cols(w, layer, col, n=P):
                if type(col) is not int:
                    place(col, 1)
                return w[layer][:, :, bass.ds(col, n)]

            rows = 0
            for src in (c, c_ctx.rearrange("(a n) -> a n", a=1), norm_w, b_mod,
                        conv_w.rearrange("l k n -> (l k) n"),
                        final_norm_w.rearrange("(a n) -> a n", a=1)):
                r = src.rearrange("a (k p) -> (a k) p", p=P)
                sp.dma_start(vec_rows[rows:rows + r.shape[0], :], r).then_inc(vec_in, 16)
                rows += r.shape[0]
            assert rows == V_ALL
            sp.dma_start(sink[:], attn_sink.rearrange("(a l) h -> a (l h)", a=1)
                         .to_broadcast([P, DEPTH * HEADS])).then_inc(tab_in, 16)
            sp.dma_start(cos_s[:], cos_t).then_inc(tab_in, 16)
            sp.dma_start(sin_s[:], sin_t).then_inc(tab_in, 16)

            for ph in phases:
                L, st = ph.layer, ph.st
                if ph.kind == "mod":
                    for g in range(SHIFT_SCALE if L == 0 else 0):
                        sp.wait_ge(sem["row_ready"], at("row_ready", ph, g - 3))
                        sp.dma_start(wm[:, g % 4], w_mod_v[L][:, :, g * MG:(g + 1) * MG])\
                            .then_inc(wm_in[g % 4], 16)
                elif ph.kind == "load":
                    src = (x[0] if st.lat else ctx[0]).rearrange("(b p) n -> b p n", p=P)
                    if st.lat:
                        for j in range(2):
                            load_tile(after(ph, "wout", CTXS), j, cols(w_o_v, L, j * P))
                    sp.wait_ge(vec_mm, 1)
                    sp.wait_ge(sem["y_lo"], at("y_lo", ph))
                    sp.wait_ge(sem["row_ready"], at("row_ready", ph))
                    for b in range(st.blocks):
                        if b == 1:
                            sp.wait_ge(sem["m_done"], at("m_done", ph))
                        sp.wait_ge(sem["xt_mm"], at("xt_mm", ph, 2 * (b - 1)))
                        sp.dma_start(x_rows[:, (b + 1) % 2], src[b]).then_inc(xr_in[b % 2], 16)
                elif ph.kind == "norm":
                    kv = after(ph, "kv", st)
                    load_tile(kv, 0, cols(w_in_v, L, C_V))
                    load_tile(kv, 1, cols(w_in_v, L, C_K))
                    if st.lat:
                        sp.wait_ge(sem["xt_copied"], at("xt_copied", ph))
                        if L:
                            for b in range(2):
                                sp.wait_ge(slot_read[b], x_made(ph))
                        sp.dma_start(x_keep, xs[:]).then_inc(sem["x_spilled"], 16)
                elif ph.kind == "attn":
                    with sp.Fori(0, PAIRS) as i:
                        load_tile(ph, 0, cols(w_in_v, L, i * P + C_Q), i, 4)
                        load_tile(ph, 1, cols(w_in_v, L, i * P + C_ZB), i, 4)
                        load_tile(ph, 2, cols(w_in_v, L, i * (2 * P) + C_GB), i, 4)
                        load_tile(ph, 3, cols(w_in_v, L, i * (2 * P) + (C_GB + P)), i, 4)
                elif ph.kind == "mixb":
                    for t in range(2):
                        load_tile(ph, t, cols(w_b_v, L, 2 * t * P, 2 * P))
                    for b in range(2):
                        sp.wait_ge(gb_out[b], START["gb_out"] + 16 * gb_used(ph))
                    sp.wait_ge(sem["yb_done"], at("yb_done", ph))
                    for d in range(KT):
                        for s in ((d - 1) * st.nch - 1, (d - 1) * st.nch - 2):
                            sp.wait_ge(slot_read[bank(ph, s)], reads_at(ph, s))
                        sp.dma_start(tgb[:, d % 2, 0:st.T], gb_keep[d][:, 0:st.T])\
                            .then_inc(gb_in[d % 2], 16)
                        if d in (1, 2):
                            load_tile(ph, d + 1, cols(w_b_v, L, 2 * (d + 1) * P, 2 * P))
                elif ph.kind == "conv":
                    G, g0, ML = mod_groups(ph)
                    with sp.Fori(0, CT) as i:
                        for j, col in enumerate((C_C, C_U, C_Z, C_B)):
                            load_tile(ph, j, cols(w_in_v, L, i * P + col), i, 4)
                            q = j - 1
                            if not 0 <= q < G:
                                continue
                            src = cols(w_mod_v, ML, i * (G * MG) + (g0 + q) * MG, MG)
                            sp.wait_ge(sem["row_ready"], at("row_ready", ph, q, i, G))
                            if q == 0:
                                for s in (-2, -1):
                                    sp.wait_ge(slot_read[bank(ph, s)], reads_at(ph, s))
                            sp.dma_start(wmt[:], src).then_inc(sem["wmt_in"], 16)
                elif ph.kind == "mixa":
                    with sp.Fori(0, 2) as i:
                        for h in range(2):
                            for e in range(2):
                                load_tile(ph, 3 * h + e,
                                          cols(w_in_v, L, i * (4 * P) + (C_GA + (2 * h + e) * P)),
                                          i, 6)
                            load_tile(ph, 3 * h + 2,
                                      cols(w_a_v, L, i * (4 * P) + 2 * h * P, 2 * P), i, 6)
                elif ph.kind == "wout":
                    for j in range(KT):
                        if st.lat or j >= 2:
                            load_tile(ph, j, cols(w_o_v, L, j * P))
                        part = j - 1
                        if st.lat and 0 <= part < X_PARTS:
                            k = slice(part * KT // X_PARTS, (part + 1) * KT // X_PARTS)
                            if part == 0:
                                sp.wait_ge(sem["mm_done"], slots_at(ph, -1))
                                sp.wait_ge(sem["x_spilled"], at("x_spilled", ph))
                            else:
                                sp.wait_ge(sem["x_in"], at("x_in", ph, 16 * part))
                            sp.dma_start(xs[:, k], x_keep[:, k]).then_inc(sem["x_in"], 16)
                elif ph.kind == "final":
                    out_v = out[0].rearrange("(b p) n -> b p n", p=P)
                    for b in range(SEQ // P):
                        sp.wait_ge(out_left, b + 1)
                        sp.wait_ge(out_right, b + 1)
                        sp.dma_start(out_v[b], o_rows[:, b % 4]).then_inc(out_sent[b % 4], 16)
                    for b in range(4):
                        sp.wait_ge(out_sent[b], 16 * (SEQ // P // 4))

        @block.gpsimd
        def _(pool):
            for t, value in ((ident, 0.0), (ident_b, 0.0), (mask_prev, 0.0), (mask_next, 0.0),
                             (ones, 1.0), (eps, EPS)):
                pool.memset(t[:], value).then_inc(const_ready, 1)
            started = [(sem[n], v) for n, v in START.items() if n in sem]
            started += [(s, START["slot_read"]) for s in slot_read]
            started += [(s, START["av_done"]) for s in av_done]
            started += [(s, START["gb_out"]) for s in gb_out]
            for at_, (s, v) in enumerate(started):
                pool.memset(head_start[:, at_:at_ + 1], 0.0).then_inc(s, v)
            pool.wait_ge(const_ready, 6)
            for mat in (ident, ident_b):
                pool.affine_select(out=mat[:], in_=mat[:], compare_op=ALU.not_equal, fill=1.0, base=0,
                                   pattern=[[-1, P]], channel_multiplier=1).then_inc(const_ready, 1)
            pool.affine_select(out=mask_prev[:], in_=mask_prev[:], compare_op=ALU.is_ge, fill=NEG,
                               base=0, pattern=[[1, BLK]], channel_multiplier=-1)\
                .then_inc(const_ready, 1)
            pool.affine_select(out=mask_next[:], in_=mask_next[:], compare_op=ALU.is_ge, fill=NEG,
                               base=0, pattern=[[-1, BLK]], channel_multiplier=1)\
                .then_inc(const_ready, 1)

            def low_part(n, i=0, per=0):
                pool.wait_ge(sem["w_hi"], count(i, per, n + 1))
                pool.wait_ge(sem["w_lo"], count(i, per, n))
                pool.tensor_tensor(wL[:, n % 2, :], raw[:, n % 2, :], wH[:, n % 2, :].bitcast(F32),
                                   ALU.subtract).then_inc(sem["w_lo"], 1)

            def rope_sin(ph, n, i=0, per=0):
                off, w = ph.st.chunks[n]
                pool.wait_ge(sem["rope_shuf"], at("rope_shuf", ph, n + 1, i, per))
                pool.tensor_tensor(rsh[:, 0:w], rsh[:, 0:w], sin_s[:, off:off + w], ALU.mult)\
                    .then_inc(sem["rope_sin"], 1)

            low_part(0)
            low_part(1)
            pool.wait_ge(tab_in, 48)
            for ph in phases:
                L, st, n = ph.layer, ph.st, ph.st.nch if ph.st else 0
                if ph.kind == "norm":
                    for r, (c_, k) in enumerate((c_, k) for c_ in range(n) for k in range(KT)):
                        off, w = st.chunks[c_]
                        if r % 3 == 2:
                            continue
                        pool.wait_ge(sem["hh_ready"], at("hh_ready", ph, r + 1))
                        pool.tensor_tensor(hL[:, k, off:off + w], hn[:, r % 4, 0:w],
                                           hH[:, k, off:off + w].bitcast(F32), ALU.subtract)\
                            .then_inc(sem["hl_pool"], 1)
                elif ph.kind == "load" or not st or not st.lat:
                    continue
                elif ph.kind == "kv":
                    low_part(ph.tile0 + 2)
                    for c_ in range(n):
                        rope_sin(ph, c_)
                    low_part(ph.tile0 + 3)
                elif ph.kind == "attn":
                    def pool_pair(i, g, ph=ph, st=st, n=n):
                        rope_sin(ph, 0, i, n)
                        low_part(ph.tile0 + 2, i, 4)
                        for c_ in range(1, n):
                            rope_sin(ph, c_, i, n)
                        for b, parts in enumerate(fills(st)):
                            for t, c_ in slots_done(parts):
                                if c_ == n - 1:
                                    low_part(ph.tile0 + 3 + t, i, 4)
                    by_pair(pool, pool_pair)
                elif ph.kind in ("mixb", "conv", "mixa", "wout"):
                    turns, per = {"mixb": (2, 2), "conv": (CT, 4), "mixa": (2, 6),
                                  "wout": (KT // 2, 2)}[ph.kind]
                    if ph.tile0 + turns * per == n_tiles:
                        turns -= 1
                    with pool.Fori(0, turns) as i:
                        for j in range(per):
                            low_part(ph.tile0 + j + 2, i, per)

        @block.scalar
        def _(act):
            def high_part(ph, j, i=0):
                n, body = ph.tile0 + j + 2, BODY[ph.kind]
                if j >= 0:
                    act.wait_ge(sem["mm_done"],
                                slots_at(ph, sum(body[:j + 1]) * ph.st.nch - 1, i, sum(body) * ph.st.nch))
                act.wait_ge(raw_in[n % 2], count(i, len(body) // 2 * 16, 16 * (n // 2 + 1)))
                act.activation(wH[:, n % 2, :], raw[:, n % 2, :], ACT.Copy)\
                    .then_inc(sem["w_hi"], 1)

            def square(ph, r, k, c_, i=0, per=0):
                st = ph.st
                off, w = st.chunks[c_]
                act.wait_ge(sem["sq_added"], at("sq_added", ph, r - 1, i, per))
                act.activation(sq[:, r % 2, 0:w], x_st[st.name][:, k, off:off + w], ACT.Square)\
                    .then_inc(sem["sq_ready"], 1)

            act.preload_act_table(ACT.Exp)
            act.wait_ge(vec_ready, 1)
            act.activation(silu_t[:], vec[:, 0:2 * KT], ACT.Tanh, scale=0.5).then_inc(silu_tanh, 1)
            first_kv = next(p for p in phases if p.kind == "kv")
            for ph in phases:
                L, st, n = ph.layer, ph.st, ph.st.nch if ph.st else 0
                if ph.kind == "mod":
                    for g in range(SHIFT_SCALE if L == 0 else 0):
                        act.wait_ge(sem["row_ready"], at("row_ready", ph, g + 1))
                        act.wait_ge(sem["row_turned"], at("row_turned", ph, g - 1))
                        act.activation(mrow0[:, g % 2], pS[0:2, (g % 2) * CH:(g % 2) * CH + MG],
                                       ACT.Copy).then_inc(sem["row_copied"], 1)
                    if L == 0:
                        high_part(first_kv, -2)
                        high_part(first_kv, -1)
                elif ph.kind == "load":
                    for b in range(st.blocks):
                        act.wait_ge(sem["xt_copied"], at("xt_copied", ph, 2 * (b + 1)))
                        act.wait_ge(sem["sq_added"], at("sq_added", ph, b))
                        act.activation(sq_block, x_st[st.name][:, :, b * P:(b + 1) * P],
                                       ACT.Square).then_inc(sem["sq_ready"], 1)
                elif ph.kind == "stat":
                    act.preload_act_table(ACT.Sqrt)
                    for c_, (off, w) in enumerate(st.chunks):
                        act.wait_ge(sem["sum_done"], at("sum_done", ph, c_ + 1))
                        act.activation(acc[st.name][:, off:off + w], pS[:, c_ * CH:c_ * CH + w],
                                       ACT.Sqrt, bias=eps[:, 0:1], scale=1.0 / D)\
                            .then_inc(sem["rms_ready"], 1)
                    act.preload_act_table(ACT.Exp)
                elif ph.kind == "norm":
                    act.wait_ge(sem["mm_done"], slots_at(ph, -1))
                    for r, (c_, k) in enumerate((c_, k) for c_ in range(n) for k in range(KT)):
                        off, w = st.chunks[c_]
                        act.wait_ge(sem["hn_ready"], at("hn_ready", ph, r + 1))
                        h = hn[:, r % 4, 0:w]
                        act.activation(h, h, ACT.Identity,
                                       bias=modv[:, L, k, s_of(ph):s_of(ph) + 1])\
                            .then_inc(sem["hf_ready"], 1)
                        act.wait_ge(sem["hf_ready"], at("hf_ready", ph, r + 1))
                        act.activation(hH[:, k, off:off + w], h, ACT.Copy)\
                            .then_inc(sem["hh_ready"], 1)
                elif ph.kind == "final":
                    act.preload_act_table(ACT.Sqrt)
                    for c_ in range(n):
                        rows = slice(c_ * CH // P, (c_ + 1) * CH // P)
                        act.wait_ge(sem["sum_done"], at("sum_done", ph, c_ + 1))
                        act.activation(rstd[:, rows], pS[:, c_ * CH:c_ * CH + CH // P], ACT.Sqrt,
                                       bias=eps[:, 0:1], scale=1.0 / D)\
                            .then_inc(sem["rms_ready"], 1)
                    for b in range(SEQ // P):
                        act.wait_ge(sem["rstd_ready"], at("rstd_ready", ph, b * P // CH + 1))
                        act.wait_ge(sem["pt_done"], at("pt_done", ph, 2 * b + 1))
                        act.wait_ge(out_sent[b % 4], 16 * (b // 4))
                        act.activation(o_rows[:, b % 4, 0:CH], pT[:, ph.round0 % 2, :],
                                       ACT.Identity, scale=rstd[:, b:b + 1]).then_inc(out_left, 1)
                elif ph.kind == "kv":
                    def v_high(c_, ph=ph, st=st):
                        off, w = st.chunks[c_]
                        act.wait_ge(sem["pt_done"], at("pt_done", ph, c_ + 1))
                        t0, nt = (st.key0 + off) // BLK, w // BLK
                        act.activation(v_all[:, t0:t0 + nt, :, 0:HD],
                                       pT[:, (ph.round0 + c_) % 2, 0:w]
                                       .rearrange("p (t g d) -> p t g d", t=nt, g=KV_HEADS),
                                       ACT.Copy).then_inc(sem["pt_hi"], 1)

                    for c_, (off, w) in enumerate(st.chunks):
                        act.wait_ge(sem["mm_done"], slots_at(ph, c_))
                        act.wait_ge(sem["hl_pool"], at("hl_pool", ph))
                        act.wait_ge(sem["hl_dve"], at("hl_dve", ph))
                        act.wait_ge(sem["pt_done"], at("pt_done", ph, c_))
                        act.activation(vraw[:, 0:w], pp[:, bank(ph, c_), 0:w], ACT.Copy)\
                            .then_inc(slot_read[bank(ph, c_)], 1)
                        if c_ == n - 1:
                            high_part(ph, 0)
                        v_high(c_)
                    for c_, (off, w) in enumerate(st.chunks):
                        s = n + c_
                        act.wait_ge(sem["mm_done"], slots_at(ph, s))
                        free = "rope_out" if st.lat else "stack_lo"
                        act.wait_ge(sem[free], at(free, ph, c_))
                        act.activation(rraw[:, 0:w], pp[:, bank(ph, s), 0:w], ACT.Copy)\
                            .then_inc(slot_read[bank(ph, s)], 1)
                        if c_ == n - 1:
                            high_part(ph, 1)
                        if st.lat:
                            act.wait_ge(sem["rope_out"], at("rope_out", ph, c_ + 1))
                        else:
                            act.wait_ge(slot_read[bank(ph, s)], reads_at(ph, s))
                        r = rout if st.lat else rraw
                        cols = slice(st.key0 + off, st.key0 + off + w)
                        for g in range(KV_HEADS):
                            for half in (0, HD):
                                last = act.activation(kH[half:half + HD, g, cols],
                                                      r[g * HD:(g + 1) * HD, 0:w], ACT.Copy)
                        last.then_inc(sem["stack_hi"], 1)
                elif ph.kind == "attn":
                    nb, R, steps = st.blocks, av_turn(ph), fills(st)
                    act.wait_ge(sem["x_spilled"], at("x_spilled", ph))

                    def act_pair(i, g, ph=ph, st=st, n=n, nb=nb, R=R, steps=steps):
                        def take_q(c_):
                            off, w = st.chunks[c_]
                            act.wait_ge(sem["mm_done"], slots_at(ph, c_, i, 4 * n))
                            free = "rope_out" if st.lat else "stack_lo"
                            act.wait_ge(sem[free], at(free, ph, c_, i, n))
                            act.activation(rraw[:, 0:w], pp[:, bank(ph, c_), 0:w], ACT.Copy)\
                                .then_inc(slot_read[bank(ph, c_)], 1)

                        def stack_q(c_):
                            off, w = st.chunks[c_]
                            if st.lat:
                                act.wait_ge(sem["rope_out"], at("rope_out", ph, c_ + 1, i, n))
                            else:
                                act.wait_ge(slot_read[bank(ph, c_)], reads_at(ph, c_, i, 4 * n))
                            act.wait_ge(sem["qk_done"], at("qk_done", ph, 0, i, nb))
                            r = rout if st.lat else rraw
                            act.activation(q_st[0:HD, 0, off:off + w], r[0:HD, 0:w], ACT.Copy)
                            act.activation(q_st[HD:P, 1, off:off + w], r[HD:P, 0:w], ACT.Copy)\
                                .then_inc(sem["stack_hi"], 1)

                        def pt_high(b, r):
                            rr = st.round_of(b) + r
                            w = len(st.rounds(b)[r]) * 2 * BLK
                            act.wait_ge(sem["pt_done"], at("pt_done", ph, rr + 1, i, R))
                            act.wait_ge(av_done[rr % 2],
                                        count(i, R // 2, START["av_done"] + ph.av0 // 2 + rr // 2))
                            act.activation(ptH[:, rr % 2, 0:w], pT[:, (ph.round0 + rr) % 2, 0:w],
                                           ACT.Copy).then_inc(sem["pt_hi"], 1)

                        def side_slot(t, c_):
                            off, w = st.chunks[c_]
                            s = (t + 1) * n + c_
                            pb = bank(ph, s)
                            act.wait_ge(sem["mm_done"], slots_at(ph, s, i, 4 * n))
                            u = t * n + c_
                            buf, used = u % 2, max(0, u - n) // 2
                            act.wait_ge(gb_out[buf],
                                        count(i, 16 * n, START["gb_out"] + 16 * (gb_used(ph) + used)))
                            act.wait_ge(slot_read[bank(ph, 2 * n - 1)],
                                        reads_at(ph, 2 * n - 1 - (4 * n if t == 0 else 0), i, 4 * n))
                            gate = act.activation(gst[:, buf, 0:w], pp[:, pb, 0:w], ACT.Tanh,
                                                  scale=0.5)
                            if t == 0:
                                gate.then_inc(sem["gate_tanh"], 1)
                            else:
                                gate.then_inc(slot_read[pb], 1)
                                act.wait_ge(slot_read[bank(ph, s)], reads_at(ph, s, i, 4 * n))
                                act.dma_start(gb_keep[i * 2 + (t - 1)][:, off:off + w],
                                              gst[:, buf, 0:w]).then_inc(gb_out[buf], 16)
                            if c_ == n - 1:
                                high_part(ph, 1 + t, i)

                        def take_out(o):
                            rr = st.round_of(o + 1) - 1
                            act.wait_ge(av_done[rr % 2], count(
                                i, R // 2, START["av_done"] + ph.av0 // 2 + rr // 2 + 1))
                            act.wait_ge(sem["att_done"], at("att_done", ph, o, i, nb))
                            act.activation(o_half[:], pO[HD:P, 0:2 * BLK], ACT.Copy)\
                                .then_inc(sem["att_half"], 1)

                        take_q(0)
                        stack_q(0)
                        for c_ in range(1, n):
                            take_q(c_)
                        high_part(ph, 0, i)
                        for b, parts in enumerate(steps):
                            rounds = len(st.rounds(b - 1)) if b else 0
                            if early(st, b):
                                take_out(b - 2)
                            for r in range(min(rounds, 2)):
                                pt_high(b - 1, r)
                            if b < nb:
                                free = st.round_of(b - 1) if b else -len(st.rounds(nb - 1))
                                act.wait_ge(sem["sinkin_ready"],
                                            at("sinkin_ready", ph, b + 1, i, nb))
                                act.activation(sinkexp[:, b % 2, :], sinkin[:, b % 2, :], ACT.Exp)
                                act.wait_ge(sem["pt_done"], at("pt_done", ph, free, i, R))
                                W = len(st.key_tiles(b)) * BLK
                                for h in range(2):
                                    act.activation(prob[:, b % 2, h, 0:W], pS[:, h * W:(h + 1) * W],
                                                   ACT.Exp, bias=negm[:, b % 2, h:h + 1], scale=SCALE,
                                                   accum_out=rsum[:, b % 2, h:h + 1])\
                                        .then_inc(sem["exp_done"], 1)
                            if b == 0:
                                for c_ in range(1, n):
                                    stack_q(c_)
                            for t, c_ in slots_done(parts[:2]):
                                side_slot(t, c_)
                            for r in range(2, rounds):
                                pt_high(b - 1, r)
                            for t, c_ in slots_done(parts[2:3]):
                                side_slot(t, c_)
                            if late(st, b):
                                take_out(b - 1)
                    by_pair(act, act_pair)
                elif ph.kind == "mixb":
                    act.wait_ge(sem["yb_done"], at("yb_done", ph))
                    for k in range(CT):
                        act.activation(yH[:, k, 0:st.T], yb[st.name][:, k, :], ACT.Copy)\
                            .then_inc(sem["y_hi"], 1)
                    with act.Fori(0, 2) as i:
                        for j in range(2):
                            high_part(ph, j, i)
                elif ph.kind == "conv":
                    G = mod_groups(ph)[0]

                    def copy_row(q, i, ph=ph, st=st, G=G):
                        if q < G:
                            act.wait_ge(sem["row_ready"], at("row_ready", ph, q + 1, i, G))
                            act.wait_ge(sem["row_turned"], at("row_turned", ph, 0, i, 1))
                            act.activation(mrow[st.name][:, q], pS[0:2, q * CH:q * CH + MG],
                                           ACT.Copy).then_inc(sem["row_copied"], 1)

                    act.wait_ge(sem["mm_done"], slots_at(ph, -1))
                    act.wait_ge(sem["y_lo"], at("y_lo", ph))
                    with act.Fori(0, CT) as i:
                        for c_, (off, w) in enumerate(st.chunks):
                            act.wait_ge(sem["mm_done"], slots_at(ph, c_, i, 4 * n))
                            act.wait_ge(sem["y_lo"], at("y_lo", ph, 0, i, n))
                            act.activation(cb[st.name][:, off:off + w], pp[:, bank(ph, c_), 0:w],
                                           ACT.Copy).then_inc(slot_read[bank(ph, c_)], 1)
                        high_part(ph, 0, i)
                        high_part(ph, 1, i)
                        copy_row(0, i)
                        for c_, (off, w) in enumerate(st.chunks):
                            s = 2 * n + c_
                            act.wait_ge(sem["mm_done"], slots_at(ph, s, i, 4 * n))
                            if c_:
                                act.wait_ge(slot_read[bank(ph, s - 1)],
                                            reads_at(ph, s - 1, i, 4 * n))
                            act.activation(th[:, 0:w], pp[:, bank(ph, s), 0:w], ACT.Tanh, scale=0.5)\
                                .then_inc(sem["gate_tanh"], 1)
                        high_part(ph, 2, i)
                        copy_row(1, i)
                        copy_row(2, i)
                        for c_, (off, w) in enumerate(st.chunks):
                            act.wait_ge(slot_read[bank(ph, 3 * n + c_)],
                                        reads_at(ph, 3 * n + c_, i, 4 * n))
                            act.activation(yH[:, i, off:off + w], yv[:, c_, 0:w], ACT.Copy)\
                                .then_inc(sem["y_hi"], 1)
                        high_part(ph, 3, i)
                elif ph.kind == "mixa":
                    act.wait_ge(sem["y_lo"], at("y_lo", ph))
                    with act.Fori(0, 2) as i:
                        for h in range(2):
                            for e in range(2):
                                for c_, (off, w) in enumerate(st.chunks):
                                    s = (4 * h + e) * n + c_
                                    act.wait_ge(sem["mm_done"], slots_at(ph, s, i, 8 * n))
                                    act.wait_ge(sem["m_done"],
                                                at("m_done", ph, 2 * h * n, i, 4 * n))
                                    act.activation(tga[:, e, off:off + w], pp[:, bank(ph, s), 0:w],
                                                   ACT.Tanh, scale=0.5)\
                                        .then_inc(slot_read[bank(ph, s)], 1)
                                high_part(ph, 3 * h + e, i)
                            high_part(ph, 3 * h + 2, i)
                elif ph.kind == "msplit":
                    act.wait_ge(sem["m_done"], at("m_done", ph))
                    act.wait_ge(sem["mm_done"], slots_at(ph, -1))
                    for k in range(KT):
                        act.activation(hH[:, k, 0:st.T], m[st.name][:, k, :], ACT.Copy, scale=0.25)\
                            .then_inc(sem["mh_ready"], 1)
                elif ph.kind == "wout":
                    def wout_turn(i, more=True, ph=ph, n=n):
                        for j in range(2):
                            for c_ in range(n):
                                act.wait_ge(slot_read[bank(ph, j * n + c_)],
                                            reads_at(ph, j * n + c_, i, 2 * n))
                                square(ph, j * n + c_, i * 2 + j, c_, i, 2 * n)
                            if more:
                                high_part(ph, j, i)

                    if ph.tile0 + KT == n_tiles:
                        with act.Fori(0, KT // 2 - 1) as i:
                            wout_turn(i)
                        wout_turn(KT // 2 - 1, more=False)
                    else:
                        with act.Fori(0, KT // 2) as i:
                            wout_turn(i)

        @block.vector
        def _(dve):
            def rope(ph, n, s, i=0, turn=0, slots=0):
                off, w = ph.st.chunks[n]
                dve.wait_ge(sem["stack_lo"], at("stack_lo", ph, n, i, turn))
                dve.wait_ge(slot_read[bank(ph, s)], reads_at(ph, s, i, slots))
                dve.tensor_tensor(rout[:, 0:w], rraw[:, 0:w], cos_s[:, off:off + w], ALU.mult)\
                    .then_inc(sem["rope_cos"], 1)
                dve.stream_shuffle(rsh[:, 0:w], rraw[:, 0:w], list(range(16, 32)) + list(range(16)))\
                    .then_inc(sem["rope_shuf"], 1)
                dve.wait_ge(sem["rope_cos"], at("rope_cos", ph, n + 1, i, turn))
                dve.wait_ge(sem["rope_sin"], at("rope_sin", ph, n + 1, i, turn))
                dve.tensor_tensor(rout[:, 0:w], rout[:, 0:w], rsh[:, 0:w], ALU.add)\
                    .then_inc(sem["rope_out"], 1)

            def low_part(ph, j, i=0, per=0):
                if ph.st is CTXS:
                    n = ph.tile0 + j + 2
                    dve.wait_ge(sem["w_hi"], count(i, per, n + 1))
                    dve.wait_ge(sem["w_lo"], count(i, per, n))
                    dve.tensor_tensor(wL[:, n % 2, :], raw[:, n % 2, :],
                                      wH[:, n % 2, :].bitcast(F32), ALU.subtract)\
                        .then_inc(sem["w_lo"], 1)

            def add_square(ph, r, c_, i=0, per=0):
                off, w = ph.st.chunks[c_]
                a = acc[ph.st.name][:, off:off + w]
                dve.wait_ge(sem["sq_ready"], at("sq_ready", ph, r + 1, i, per))
                dve.wait_ge(sem["sq_added"], at("sq_added", ph, r, i, per))
                dve.tensor_tensor(a, a, sq[:, r % 2, 0:w], ALU.add).then_inc(sem["sq_added"], 1)

            dve.wait_ge(vec_mm, 1)
            dve.tensor_copy(vec[:], pO[:, 0:V_ALL]).then_inc(vec_ready, 1)
            dve.wait_ge(tab_in, 48)
            dve.tensor_scalar(nsink[:], sink[:], -1.0, None, ALU.mult).then_inc(nsink_ready, 1)
            dve.wait_ge(vec_ready, 1)
            dve.wait_ge(silu_tanh, 1)
            dve.scalar_tensor_tensor(
                out=silu_c[:].rearrange("p (k s) -> p s k", s=2),
                in0=silu_t[:].rearrange("p (s k) -> p s k", s=2), scalar=1.0,
                in1=vec[:, 0:2 * KT].rearrange("p (s k) -> p s k", s=2),
                op0=ALU.add, op1=ALU.mult).then_inc(silu_ready, 1)
            dve.wait_ge(nsink_ready, 1)

            for ph in phases:
                L, st, n = ph.layer, ph.st, ph.st.nch if ph.st else 0
                s_ = s_of(ph) if st else 0
                if ph.kind == "mod":
                    if L == 0:
                        dve.wait_ge(sem["row_turned"], at("row_turned", ph, SHIFT_SCALE))
                        for s in range(2):
                            last = dve.scalar_tensor_tensor(
                                out=modv[:, L, 0:2 * KT, s],
                                in0=pO[:, 0:4 * KT].rearrange("p (t s) -> p t s", s=2)[:, :, s],
                                scalar=0.5, in1=vec[:, V_BM:V_BM + 2 * KT],
                                op0=ALU.mult, op1=ALU.add)
                        last.then_inc(sem["modv_ready"], 1)
                        dve.wait_ge(sem["modv_ready"], at("modv_ready", ph, 1))
                    dve.wait_ge(sem["mod_part"], at("mod_part", ph))
                    for s in range(2):
                        last = dve.scalar_tensor_tensor(
                            out=mod_a[:, :, s], in0=modv[:, L, KT:2 * KT, s], scalar=1.0,
                            in1=vec[:, V_NW + L * KT:V_NW + (L + 1) * KT],
                            op0=ALU.add, op1=ALU.mult)
                    last.then_inc(sem["mod_done"], 1)
                    dve.wait_ge(sem["mod_done"], at("mod_done", ph, 1))
                elif ph.kind == "load":
                    dve.wait_ge(vec_mm, 1)
                    dve.wait_ge(sem["mm_done"], slots_at(ph, -1))
                    dve.wait_ge(sem["m_done"], at("m_done", ph))

                    def sum_squares(b, ph=ph, st=st):
                        dve.wait_ge(sem["sq_ready"], at("sq_ready", ph, b + 1))
                        dve.tensor_reduce(acc[st.name][:, b * P:(b + 1) * P],
                                          sq_block.rearrange("p k t -> p t k"), AX.X, ALU.add)\
                            .then_inc(sem["sq_added"], 1)

                    for b in range(st.blocks):
                        for h in range(2):
                            dve.wait_ge(sem["xt_mm"], at("xt_mm", ph, 2 * b + h + 1))
                            dve.tensor_copy(x_st[st.name][:, 4 * h:4 * h + 4, b * P:(b + 1) * P],
                                            pT[:, (ph.round0 + h) % 2, :]
                                            .rearrange("p (k t) -> p k t", k=4))\
                                .then_inc(sem["xt_copied"], 1)
                        if b:
                            sum_squares(b - 1)
                    sum_squares(st.blocks - 1)
                elif ph.kind == "stat":
                    rms = acc[st.name]
                    for c_, (off, w) in enumerate(st.chunks):
                        dve.wait_ge(sem["rms_ready"], at("rms_ready", ph, c_ + 1))
                        dve.reciprocal(rms[:, off:off + w], rms[:, off:off + w])\
                            .then_inc(sem["rstd_ready"], 1)
                elif ph.kind == "norm":
                    src, rms = x_st[st.name], acc[st.name]

                    def h_low(r, ph=ph):
                        off, w = ph.st.chunks[r // KT]
                        h = hH[:, r % KT, off:off + w].bitcast(F32)
                        dve.wait_ge(sem["hh_ready"], at("hh_ready", ph, r + 1))
                        dve.tensor_tensor(hL[:, r % KT, off:off + w], hn[:, r % 4, 0:w], h,
                                          ALU.subtract).then_inc(sem["hl_dve"], 1)

                    dve.wait_ge(sem["stack_lo"], at("stack_lo", ph))
                    dve.wait_ge(sem["rstd_ready"], at("rstd_ready", ph))
                    for c_, (off, w) in enumerate(st.chunks):
                        for k in range(KT):
                            r = c_ * KT + k
                            for name, done in zip(("hl_pool", "hl_dve"), lows(max(0, r - 3))):
                                dve.wait_ge(sem[name], at(name, ph, done))
                            dve.scalar_tensor_tensor(
                                out=hn[:, r % 4, 0:w], in0=src[:, k, off:off + w],
                                scalar=mod_a[:, k, s_:s_ + 1], in1=rms[:, off:off + w],
                                op0=ALU.mult, op1=ALU.mult).then_inc(sem["hn_ready"], 1)
                            if r % 3 == 0 and r:
                                h_low(r - 1)
                elif ph.kind == "final":
                    for c_ in range(n):
                        rows = slice(c_ * CH // P, (c_ + 1) * CH // P)
                        dve.wait_ge(sem["rms_ready"], at("rms_ready", ph, c_ + 1))
                        dve.reciprocal(rstd[:, rows], rstd[:, rows]).then_inc(sem["rstd_ready"], 1)
                    for b in range(SEQ // P):
                        dve.wait_ge(sem["rstd_ready"], at("rstd_ready", ph, b * P // CH + 1))
                        dve.wait_ge(sem["pt_done"], at("pt_done", ph, 2 * b + 2))
                        dve.wait_ge(out_sent[b % 4], 16 * (b // 4))
                        dve.tensor_scalar(o_rows[:, b % 4, CH:D], pT[:, (ph.round0 + 1) % 2, :],
                                          rstd[:, b:b + 1], None, ALU.mult).then_inc(out_right, 1)
                elif ph.kind == "kv":
                    low_part(ph, 0)
                    for c_, (off, w) in enumerate(st.chunks):
                        t0, nt = (st.key0 + off) // BLK, w // BLK
                        dve.wait_ge(sem["pt_hi"], at("pt_hi", ph, c_ + 1))
                        dve.tensor_tensor(v_all[:, t0:t0 + nt, :, HD:P],
                                          pT[:, (ph.round0 + c_) % 2, 0:w]
                                          .rearrange("p (t g d) -> p t g d", t=nt, g=KV_HEADS),
                                          v_all[:, t0:t0 + nt, :, 0:HD].bitcast(F32), ALU.subtract)\
                            .then_inc(sem["pt_copied"], 1)
                    low_part(ph, 1)
                    for c_, (off, w) in enumerate(st.chunks):
                        if st.lat:
                            rope(ph, c_, n + c_)
                            dve.wait_ge(sem["rope_out"], at("rope_out", ph, c_ + 1))
                        r = rout if st.lat else rraw
                        cols = slice(st.key0 + off, st.key0 + off + w)
                        dve.wait_ge(sem["stack_hi"], at("stack_hi", ph, c_ + 1))
                        for g in range(KV_HEADS):
                            own = slice(g * HD, (g + 1) * HD)
                            for half in (0, HD):
                                last = dve.tensor_tensor(kL[half:half + HD, g, cols], r[own, 0:w],
                                                         kH[own, g, cols].bitcast(F32), ALU.subtract)
                        last.then_inc(sem["stack_lo"], 1)
                elif ph.kind == "attn":
                    nb, R, steps = st.blocks, av_turn(ph), fills(st)

                    def dve_pair(i, g, ph=ph, L=L, st=st, n=n, nb=nb, R=R, steps=steps):
                        for b in range(2):
                            dve.wait_ge(av_done[b], count(i, R // 2, START["av_done"] + ph.av0 // 2))
                        dve.wait_ge(sem["pt_copied"], at("pt_copied", ph, 0, i, R))
                        mine = slice(st.key_tiles(0)[0], TOK // BLK)
                        dve.tensor_scalar(v_cur[:, mine], v_all[:, mine, g, :].bitcast(F32), 1.0,
                                          None, ALU.mult).then_inc(sem["vcur_ready"], 1)

                        def q_chunk(c_):
                            off, w = st.chunks[c_]
                            if st.lat:
                                rope(ph, c_, c_, i, n, 4 * n)
                                dve.wait_ge(sem["rope_out"], at("rope_out", ph, c_ + 1, i, n))
                            r = rout if st.lat else rraw
                            dve.wait_ge(sem["stack_hi"], at("stack_hi", ph, c_ + 1, i, n))
                            dve.tensor_tensor(q_st[HD:P, 0, off:off + w], r[0:HD, 0:w],
                                              q_st[0:HD, 0, off:off + w].bitcast(F32), ALU.subtract)
                            dve.tensor_tensor(q_st[0:HD, 1, off:off + w], r[HD:P, 0:w],
                                              q_st[HD:P, 1, off:off + w].bitcast(F32), ALU.subtract)\
                                .then_inc(sem["stack_lo"], 1)

                        def pt_low(b, r):
                            rr = st.round_of(b) + r
                            w = len(st.rounds(b)[r]) * 2 * BLK
                            dve.wait_ge(sem["pt_hi"], at("pt_hi", ph, rr + 1, i, R))
                            dve.tensor_tensor(ptL[:, rr % 2, 0:w], pT[:, (ph.round0 + rr) % 2, 0:w],
                                              ptH[:, rr % 2, 0:w].bitcast(F32), ALU.subtract)\
                                .then_inc(sem["pt_copied"], 1)

                        def side_slot(t, c_):
                            if t == 0:
                                gate_z(c_)
                            if c_ == n - 1:
                                low_part(ph, 1 + t, i, 4)

                        def gate_z(c_):
                            off, w = st.chunks[c_]
                            dve.wait_ge(sem["gate_tanh"], at("gate_tanh", ph, c_ + 1, i, n))
                            dve.scalar_tensor_tensor(out=szb[:, off:off + w],
                                                     in0=gst[:, c_ % 2, 0:w],
                                                     scalar=1.0, in1=pp[:, bank(ph, n + c_), 0:w],
                                                     op0=ALU.add, op1=ALU.mult)\
                                .then_inc(slot_read[bank(ph, n + c_)], 1)

                        def add_halves(o):
                            q = slice(o * BLK, (o + 1) * BLK)
                            y = yb[st.name]
                            dve.wait_ge(sem["att_half"], at("att_half", ph, o + 1, i, nb))
                            dve.tensor_tensor(y[0:HD, i, q], pO[0:HD, 0:BLK], o_half[:, 0:BLK],
                                              ALU.add)
                            dve.tensor_tensor(y[HD:P, i, q], pO[0:HD, BLK:2 * BLK],
                                              o_half[:, BLK:2 * BLK], ALU.add)\
                                .then_inc(sem["att_done"], 1)

                        q_chunk(0)
                        low_part(ph, 0, i, 4)
                        for b, parts in enumerate(steps):
                            rounds = len(st.rounds(b - 1)) if b else 0
                            par = b % 2
                            if b < nb:
                                W = len(st.key_tiles(b)) * BLK
                                heads = bass.ds(i * 2 + L * HEADS, 2)
                                dve.wait_ge(sem["qk_done"], at("qk_done", ph, b + 1, i, nb))
                                dve.tensor_reduce(mx[:, par, :],
                                                  pS[:, 0:2 * W].rearrange("p (h w) -> p h w", h=2),
                                                  AX.X, ALU.max).then_inc(sem["max_ready"], 1)
                                dve.wait_ge(sem["max_ready"], at("max_ready", ph, b + 1, i, nb))
                                dve.scalar_tensor_tensor(out=negm[:, par, :], in0=mx[:, par, :],
                                                         scalar=-SCALE, in1=nsink[:, heads],
                                                         op0=ALU.mult, op1=ALU.min)\
                                    .then_inc(sem["negm_ready"], 1)
                                dve.wait_ge(sem["negm_ready"], at("negm_ready", ph, b + 1, i, nb))
                                dve.tensor_tensor(sinkin[:, par, :], negm[:, par, :], sink[:, heads],
                                                  ALU.add).then_inc(sem["sinkin_ready"], 1)
                            if early(st, b):
                                add_halves(b - 2)
                            for r in range(min(rounds, 2)):
                                pt_low(b - 1, r)
                            if b < nb:
                                for h in range(2):
                                    one = (slice(None), par, slice(h, h + 1))
                                    dve.wait_ge(sem["exp_done"],
                                                at("exp_done", ph, 2 * b + h + 1, i, 2 * nb))
                                    dve.tensor_tensor(rsum[one], rsum[one], sinkexp[one], ALU.add)\
                                        .then_inc(sem["den_ready"], 1)
                                    dve.wait_ge(sem["den_ready"],
                                                at("den_ready", ph, 2 * b + h + 1, i, 2 * nb))
                                    dve.reciprocal(rden[one], rsum[one])\
                                        .then_inc(sem["rden_ready"], 1)
                                for h in range(2):
                                    pr = prob[:, par, h, 0:W]
                                    dve.wait_ge(sem["rden_ready"],
                                                at("rden_ready", ph, 2 * b + h + 1, i, 2 * nb))
                                    dve.tensor_scalar(pr, pr, rden[:, par, h:h + 1], None,
                                                      ALU.mult).then_inc(sem["p_ready"], 1)
                            if b == 0:
                                for c_ in range(1, n):
                                    q_chunk(c_)
                            for t, c_ in slots_done(parts[:2]):
                                side_slot(t, c_)
                            for r in range(2, rounds):
                                pt_low(b - 1, r)
                            for t, c_ in slots_done(parts[2:3]):
                                side_slot(t, c_)
                            if late(st, b):
                                add_halves(b - 1)
                        dve.wait_ge(sem["att_done"], at("att_done", ph, nb, i, nb))
                        for c_ in range(n):
                            dve.wait_ge(slot_read[bank(ph, n + c_)], reads_at(ph, n + c_, i, 4 * n))
                        y = yb[st.name][:, i, 0:st.T]
                        dve.tensor_tensor(y, y, szb[:, 0:st.T], ALU.mult)\
                            .then_inc(sem["yb_done"], 1)
                        dve.wait_ge(sem["yb_done"], at("yb_done", ph, 1, i, 1))
                    by_pair(dve, dve_pair)
                elif ph.kind == "mixb":
                    for k in range(CT):
                        dve.wait_ge(sem["y_hi"], at("y_hi", ph, k + 1))
                        dve.tensor_tensor(yL[:, k, 0:st.T], yb[st.name][:, k, :],
                                          yH[:, k, 0:st.T].bitcast(F32), ALU.subtract)\
                            .then_inc(sem["y_lo"], 1)
                    loads = before(ph, "mixb", lambda p: 4)
                    with dve.Fori(0, 2) as i:
                        for d in range(4):
                            dve.wait_ge(gb_in[d % 2], count(i, 32, 16 * (loads + d // 2 + 1)))
                            for c_, (off, w) in enumerate(st.chunks):
                                s = d * n + c_
                                dve.wait_ge(sem["mm_done"], slots_at(ph, s, i, 4 * n))
                                dve.scalar_tensor_tensor(
                                    out=m[st.name][:, i * 4 + d, off:off + w],
                                    in0=tgb[:, d % 2, off:off + w], scalar=1.0,
                                    in1=pp[:, bank(ph, s), 0:w], op0=ALU.add, op1=ALU.mult)\
                                    .then_inc(slot_read[bank(ph, s)], 1)
                            if d % 2:
                                low_part(ph, d // 2, i, 2)
                elif ph.kind == "conv":
                    for s in (-2, -1):
                        dve.wait_ge(slot_read[bank(ph, s)], reads_at(ph, s))
                    dve.memset(cu[:, 0:1], 0.0)
                    dve.memset(cu[:, st.T + 1:st.T + 2], 0.0).then_inc(sem["halo_zero"], 1)
                    dve.wait_ge(sem["halo_zero"], at("halo_zero", ph, 1))
                    u, v = cb[st.name], cv[st.name]
                    G, g0, ML = mod_groups(ph)
                    with dve.Fori(0, CT) as i:
                        low_part(ph, 0, i, 4)
                        for c_, (off, w) in enumerate(st.chunks):
                            s = n + c_
                            dve.wait_ge(slot_read[bank(ph, c_)], reads_at(ph, c_, i, 4 * n))
                            dve.wait_ge(sem["mm_done"], slots_at(ph, s, i, 4 * n))
                            dve.wait_ge(sem["tap_done"], at("tap_done", ph, 0, i, 4))
                            dve.tensor_tensor(cu[:, 1 + off:1 + off + w], u[:, off:off + w],
                                              pp[:, bank(ph, s), 0:w], ALU.mult)\
                                .then_inc(slot_read[bank(ph, s)], 1)
                        for c_ in range(n):
                            dve.wait_ge(slot_read[bank(ph, n + c_)], reads_at(ph, n + c_, i, 4 * n))
                        low_part(ph, 1, i, 4)
                        for tap in range(CONV_K):
                            wt = vec[:, bass.ds(i + (V_CW + (L * CONV_K + tap) * CT), 1)]
                            if tap == 0:
                                dve.tensor_scalar(v[:, 0:st.T], cu[:, 0:st.T], wt, None, ALU.mult)\
                                    .then_inc(sem["tap_done"], 1)
                            else:
                                dve.scalar_tensor_tensor(
                                    out=v[:, 0:st.T], in0=cu[:, tap:tap + st.T], scalar=wt,
                                    in1=v[:, 0:st.T], op0=ALU.mult, op1=ALU.add)\
                                    .then_inc(sem["tap_done"], 1)
                            dve.wait_ge(sem["tap_done"], at("tap_done", ph, tap + 1, i, 4))
                        for c_, (off, w) in enumerate(st.chunks):
                            s = 2 * n + c_
                            dve.wait_ge(sem["gate_tanh"], at("gate_tanh", ph, c_ + 1, i, n))
                            dve.scalar_tensor_tensor(out=sz[st.name][:, off:off + w],
                                                     in0=th[:, 0:w], scalar=1.0,
                                                     in1=pp[:, bank(ph, s), 0:w],
                                                     op0=ALU.add, op1=ALU.mult)\
                                .then_inc(slot_read[bank(ph, s)], 1)
                        for c_ in range(n):
                            dve.wait_ge(slot_read[bank(ph, 2 * n + c_)],
                                        reads_at(ph, 2 * n + c_, i, 4 * n))
                        low_part(ph, 2, i, 4)
                        dve.tensor_tensor(v[:, 0:st.T], v[:, 0:st.T], sz[st.name][:, 0:st.T],
                                          ALU.mult).then_inc(sem["tap_done"], 1)
                        dve.wait_ge(sem["tap_done"], at("tap_done", ph, 4, i, 4))
                        for c_, (off, w) in enumerate(st.chunks):
                            s = 3 * n + c_
                            dve.wait_ge(sem["mm_done"], slots_at(ph, s, i, 4 * n))
                            dve.tensor_tensor(yv[:, c_, 0:w], v[:, off:off + w],
                                              pp[:, bank(ph, s), 0:w], ALU.mult)\
                                .then_inc(slot_read[bank(ph, s)], 1)
                            dve.wait_ge(slot_read[bank(ph, s)], reads_at(ph, s, i, 4 * n))
                            dve.wait_ge(sem["y_hi"], at("y_hi", ph, c_ + 1, i, n))
                            dve.tensor_tensor(yL[:, i, off:off + w], yv[:, c_, 0:w],
                                              yH[:, i, off:off + w].bitcast(F32), ALU.subtract)\
                                .then_inc(sem["y_lo"], 1)
                        low_part(ph, 3, i, 4)
                        if G:
                            dve.wait_ge(sem["row_turned"], at("row_turned", ph, 1, i, 1))
                            for s in range(2):
                                last = dve.scalar_tensor_tensor(
                                    out=modv[:, ML, bass.ds(i * (2 * G) + 2 * g0, 2 * G), s],
                                    in0=pO[:, 0:4 * G].rearrange("p (t s) -> p t s", s=2)[:, :, s],
                                    scalar=0.5,
                                    in1=vec[:, bass.ds(i * (2 * G) + (
                                        V_BM + ML * MODS + 2 * g0), 2 * G)],
                                    op0=ALU.mult, op1=ALU.add)
                            last.then_inc(sem["mod_part"], 1)
                elif ph.kind == "mixa":
                    with dve.Fori(0, 2) as i:
                        for h in range(2):
                            for e in range(2):
                                low_part(ph, 3 * h + e, i, 6)
                            for e in range(2):
                                for c_, (off, w) in enumerate(st.chunks):
                                    s = (4 * h + 2 + e) * n + c_
                                    q = (2 * h + e) * n + c_
                                    dve.wait_ge(slot_read[bank(ph, s - 2 * n)],
                                                reads_at(ph, s - 2 * n, i, 8 * n))
                                    dve.wait_ge(sem["mm_done"], slots_at(ph, s, i, 8 * n))
                                    dve.scalar_tensor_tensor(
                                        out=gm[:, q % 2, 0:w], in0=tga[:, e, off:off + w],
                                        scalar=1.0, in1=pp[:, bank(ph, s), 0:w],
                                        op0=ALU.add, op1=ALU.mult)\
                                        .then_inc(slot_read[bank(ph, s)], 1)
                                    dve.wait_ge(slot_read[bank(ph, s)], reads_at(ph, s, i, 8 * n))
                                    md = m[st.name][:, i * 4 + (2 * h + e), off:off + w]
                                    dve.tensor_tensor(md, md, gm[:, q % 2, 0:w], ALU.add)\
                                        .then_inc(sem["m_done"], 1)
                                    dve.wait_ge(sem["m_done"], at("m_done", ph, q + 1, i, 4 * n))
                            low_part(ph, 3 * h + 2, i, 6)
                elif ph.kind == "msplit":
                    for k in range(KT):
                        dve.wait_ge(sem["mh_ready"], at("mh_ready", ph, k + 1))
                        dve.scalar_tensor_tensor(
                            out=hL[:, k, 0:st.T], in0=m[st.name][:, k, :], scalar=0.25,
                            in1=hH[:, k, 0:st.T].bitcast(F32), op0=ALU.mult, op1=ALU.subtract)\
                            .then_inc(sem["ml_ready"], 1)
                elif ph.kind == "wout":
                    dve.memset(acc[st.name][:, 0:st.T], 0.0).then_inc(sem["acc_zero"], 1)
                    dve.wait_ge(sem["acc_zero"], at("acc_zero", ph, 1))
                    dve.wait_ge(sem["mod_part"], at("mod_part", ph))
                    gates = modv[:, L].rearrange("p t s -> p (t s)")
                    with dve.Fori(0, KT // 2) as i:
                        for j in range(2):
                            for c_, (off, w) in enumerate(st.chunks):
                                s = j * n + c_
                                dve.wait_ge(sem["mm_done"], slots_at(ph, s, i, 2 * n))
                                if st.lat and j == 0 and c_ == 0:
                                    dve.wait_ge(sem["x_in"], at("x_in", ph, 16, i, 16))
                                xe = x_st[st.name][:, i * 2 + j, off:off + w]
                                dve.scalar_tensor_tensor(
                                    out=xe, in0=pp[:, bank(ph, s), 0:w],
                                    scalar=gates[:, bass.ds(i * 4 + (4 * KT + 2 * j + s_), 1)],
                                    in1=xe, op0=ALU.mult, op1=ALU.add)\
                                    .then_inc(slot_read[bank(ph, s)], 1)
                                add_square(ph, s, c_, i, 2 * n)
                                if L == DEPTH - 1:
                                    dve.tensor_scalar(xe, xe, vec[:, bass.ds(i * 2 + (V_FN + j), 1)],
                                                      None, ALU.mult).then_inc(sem["out_scaled"], 1)
                            low_part(ph, j, i, 2)

        @block.tensor
        def _(pe):
            def k_step(ph, j, s, c_, k, kts, a_hi, a_lo, e=0):
                off, w = ph.st.chunks[c_]
                wb = (ph.tile0 + j) % 2
                col = (k * (KT // kts) + e) * P
                o = pp[:, bank(ph, s), 0:w]
                hi, lo = wH[:, wb, col:col + P], wL[:, wb, col:col + P]
                ah, al = a_hi[:, k, off:off + w], a_lo[:, k, off:off + w]
                pe.matmul(o, hi, ah, start=(k == 0), stop=False)
                pe.matmul(o, hi, al, start=False, stop=False)
                return pe.matmul(o, lo, ah, start=False, stop=(k == kts - 1))

            def open_slot(ph, s, i=0, per=0):
                pe.wait_ge(slot_read[bank(ph, s - 2)], reads_at(ph, s - 2, i, per))

            def open_tile(ph, j, i=0, per=0):
                pe.wait_ge(sem["w_lo"], count(i, per, ph.tile0 + j + 1))

            def project(ph, j, s0, a_hi, a_lo, kts=KT, outs=1, i=0, tiles=0, slots=0, ready=None,
                        first=0):
                open_tile(ph, j, i, tiles)
                n = ph.st.nch
                for e in range(outs):
                    for c_ in range(n):
                        s = s0 + e * n + c_
                        open_slot(ph, s, i, slots)
                        for k in range(kts):
                            if ready and e == 0 and c_ == 0:
                                pe.wait_ge(sem[ready], at(ready, ph, first + k + 1))
                            last = k_step(ph, j, s, c_, k, kts, a_hi, a_lo, e)
                            if k == kts - 1:
                                last.then_inc(sem["mm_done"], 1)

            def score_pieces(st, b, h):
                tiles = st.key_tiles(b)
                pieces, masks = [], []
                for t, kb in enumerate(tiles):
                    col = (h * len(tiles) + t) * BLK
                    if pieces and col % CH and pieces[-1][1] + pieces[-1][2] == kb * BLK:
                        pieces[-1][2] += BLK
                    else:
                        pieces.append([col, kb * BLK, BLK])
                    if st.lat and kb < st.blocks and kb != b:
                        masks.append((col, mask_prev if kb < b else mask_next))
                return pieces, masks

            pe.wait_ge(const_ready, 10)
            pe.wait_ge(vec_in, 16 * 6)
            pe.transpose(pO[:, 0:V_ALL], vec_rows[:], ident[0:V_ALL, 0:V_ALL]).then_inc(vec_mm, 1)
            pe.wait_ge(silu_ready, 1)

            for ph in phases:
                L, st, n = ph.layer, ph.st, ph.st.nch if ph.st else 0
                if ph.kind == "mod":
                    def turn_row(g, ph=ph):
                        pe.wait_ge(sem["row_copied"], at("row_copied", ph, g + 1))
                        for h in range(2):
                            last = pe.matmul(pO[:, 4 * g + 2 * h:4 * g + 2 * h + 2],
                                             mrow0[:, g % 2, h * P:(h + 1) * P],
                                             ident[0:2, 0:2], start=True, stop=True)
                        last.then_inc(sem["row_turned"], 1)

                    pe.wait_ge(sem["rms_ready"], at("rms_ready", ph))
                    for g in range(SHIFT_SCALE if L == 0 else 0):
                        pe.wait_ge(wm_in[g % 4], 16 * (g // 4 + 1))
                        pe.wait_ge(sem["row_copied"], at("row_copied", ph, g - 1))
                        for k in range(KT):
                            last = pe.matmul(pS[0:2, (g % 2) * CH:(g % 2) * CH + MG],
                                             silu_c[:, 2 * k:2 * k + 2], wm[:, g % 4, k, :],
                                             start=(k == 0), stop=(k == KT - 1))
                        last.then_inc(sem["row_ready"], 1)
                        if g:
                            turn_row(g - 1)
                    if L == 0:
                        turn_row(SHIFT_SCALE - 1)
                elif ph.kind == "load":
                    earlier = before(ph, "load", lambda p: p.st.blocks // 2)
                    pe.wait_ge(sem["pt_copied"], at("pt_copied", ph))
                    for b in range(st.blocks):
                        pe.wait_ge(xr_in[b % 2], 16 * (earlier + b // 2 + 1))
                        for h in range(2):
                            pe.wait_ge(sem["xt_copied"], at("xt_copied", ph, 2 * b + h - 1))
                            for k in range(4):
                                last = pe.transpose(
                                    pT[:, (ph.round0 + h) % 2, k * P:(k + 1) * P],
                                    x_rows[:, (b + 1) % 2, (4 * h + k) * P:(4 * h + k + 1) * P], ident[:])
                            last.then_inc(sem["xt_mm"], 1)
                elif ph.kind in ("stat", "final"):
                    pe.wait_ge(sem["exp_done"], at("exp_done", ph))
                    pe.wait_ge(sem["row_copied"], at("row_copied", ph))
                    pe.wait_ge(sem["mod_part"], at("mod_part", ph))
                    pe.wait_ge(sem["rms_ready"], at("rms_ready", ph))
                    made = next(p for p in reversed(phases[:phases.index(ph)])
                                if p.kind in ("load", "wout") and p.st is st)
                    pe.wait_ge(sem["sq_added"], at("sq_added", made, st.blocks if made.kind == "load"
                                                   else KT * n))
                    if ph.kind == "stat":
                        for c_, (off, w) in enumerate(st.chunks):
                            pe.matmul(pS[:, c_ * CH:c_ * CH + w], ones[:],
                                      acc[st.name][:, off:off + w],
                                      start=True, stop=True).then_inc(sem["sum_done"], 1)
                    else:
                        for c_ in range(n):
                            for t in range(CH // P):
                                tok = c_ * CH + t * P
                                last = pe.matmul(pS[:, c_ * CH + t:c_ * CH + t + 1],
                                                 acc[st.name][:, tok:tok + P], ones[:, 0:1],
                                                 start=True, stop=True)
                            last.then_inc(sem["sum_done"], 1)
                        pe.wait_ge(sem["pt_copied"], at("pt_copied", ph))
                        pe.wait_ge(sem["out_scaled"], at("out_scaled", ph))
                        for b in range(SEQ // P):
                            for h in range(2):
                                pe.wait_ge((out_left, out_right)[h], b)
                                for k in range(4):
                                    last = pe.transpose(
                                        pT[:, (ph.round0 + h) % 2, k * P:(k + 1) * P],
                                        xs[:, 4 * h + k, b * P:(b + 1) * P], ident[:])
                                last.then_inc(sem["pt_done"], 1)
                elif ph.kind == "kv":
                    for j in range(2):
                        open_tile(ph, j)
                        for c_ in range(n):
                            s = j * n + c_
                            open_slot(ph, s)
                            for k in range(KT):
                                if j == 0:
                                    done, total = lows(c_ * KT + k + 1), lows(n * KT)
                                    for x, name in enumerate(("hl_pool", "hl_dve")):
                                        pe.wait_ge(sem[name], at(name, ph, done[x] - total[x]))
                                last = k_step(ph, j, s, c_, k, KT, hH, hL)
                            last.then_inc(sem["mm_done"], 1)
                            if j == 1:
                                pe.wait_ge(slot_read[bank(ph, c_)], reads_at(ph, c_))
                                pe.wait_ge(sem["pt_copied"], at("pt_copied", ph, c_ - 1))
                                for t in range(ph.st.chunks[c_][1] // P):
                                    last = pe.transpose(
                                        pT[:, (ph.round0 + c_) % 2, t * P:(t + 1) * P],
                                        vraw[:, t * P:(t + 1) * P], ident[:])
                                last.then_inc(sem["pt_done"], 1)
                elif ph.kind == "attn":
                    nb, R, steps = st.blocks, av_turn(ph), fills(st)

                    def pe_pair(i, g, ph=ph, st=st, n=n, nb=nb, R=R, steps=steps):
                        project(ph, 0, 0, hH, hL, i=i, tiles=4, slots=4 * n)

                        def side(part):
                            for t, c_, k in part:
                                s = (t + 1) * n + c_
                                if c_ == 0 and k == 0:
                                    open_tile(ph, t + 1, i, 4)
                                if k == 0:
                                    open_slot(ph, s, i, 4 * n)
                                last = k_step(ph, t + 1, s, c_, k, KT, hH, hL)
                                if k == KT - 1:
                                    last.then_inc(sem["mm_done"], 1)

                        def scores(b):
                            pe.wait_ge(sem["stack_lo"], at("stack_lo", ph, b * BLK // CH + 1, i, n))
                            pe.wait_ge(sem["exp_done"], at("exp_done", ph, 2 * b, i, 2 * nb))
                            for h in range(2):
                                q = q_st[:, h, b * BLK:(b + 1) * BLK]
                                pieces, masks = score_pieces(st, b, h)
                                for col, key, keys in pieces:
                                    inside = [x for x in masks if col <= x[0] < col + keys]
                                    o = pS[:, col:col + keys]
                                    pe.matmul(o, q, kH[:, g, key:key + keys], start=True, stop=False)
                                    last = pe.matmul(o, q, kL[:, g, key:key + keys],
                                                     start=False, stop=not inside)
                                    for x in inside:
                                        last = pe.matmul(pS[:, x[0]:x[0] + BLK], ident_b[:], x[1][:],
                                                         start=False, stop=x is inside[-1])
                            last.then_inc(sem["qk_done"], 1)

                        def turn_round(b, r):
                            rr = st.round_of(b) + r
                            pe.wait_ge(sem["pt_copied"], at("pt_copied", ph, rr - 1, i, R))
                            for t in range(len(st.rounds(b)[r])):
                                for h in range(2):
                                    key = (2 * r + t) * BLK
                                    last = pe.transpose(
                                        pT[:, (ph.round0 + rr) % 2,
                                           (2 * t + h) * BLK:(2 * t + h + 1) * BLK],
                                        prob[:, b % 2, h, key:key + BLK], ident[:])
                            last.then_inc(sem["pt_done"], 1)

                        def times_v(b, r):
                            rr = st.round_of(b) + r
                            pe.wait_ge(sem["pt_copied"], at("pt_copied", ph, rr + 1, i, R))
                            if r == 0:
                                pe.wait_ge(sem["att_done"], at("att_done", ph, b, i, nb))
                            o = pO[:, 0:2 * BLK]
                            for t, kb in enumerate(st.rounds(b)[r]):
                                cols = slice(2 * t * BLK, 2 * (t + 1) * BLK)
                                end = r == len(st.rounds(b)) - 1 and t == len(st.rounds(b)[r]) - 1
                                pe.matmul(o, v_cur[:, kb, :], ptH[:, rr % 2, cols],
                                          start=(r == 0 and t == 0), stop=False)
                                last = pe.matmul(o, v_cur[:, kb, :],
                                                 ptL[:, rr % 2, cols], start=False, stop=end)
                            last.then_inc(av_done[rr % 2], 1)

                        for b, parts in enumerate(steps):
                            rounds = len(st.rounds(b - 1)) if b else 0
                            side(parts[3])
                            if b < nb:
                                scores(b)
                            if b == 1:
                                pe.wait_ge(sem["vcur_ready"], at("vcur_ready", ph, 1, i, 1))
                            side(parts[0])
                            if b > 1:
                                for r in range(2, len(st.rounds(b - 2))):
                                    times_v(b - 2, r)
                            if b:
                                pe.wait_ge(sem["p_ready"], at("p_ready", ph, 2 * b, i, 2 * nb))
                            for r in range(min(rounds, 2)):
                                turn_round(b - 1, r)
                            side(parts[1])
                            for r in range(min(rounds, 2)):
                                times_v(b - 1, r)
                            for r in range(2, rounds):
                                turn_round(b - 1, r)
                            side(parts[2])
                    by_pair(pe, pe_pair)
                elif ph.kind == "mixb":
                    with pe.Fori(0, 2) as i:
                        for j in range(2):
                            project(ph, j, 2 * j * n, yH, yL, kts=CT, outs=2, i=i, tiles=2,
                                    slots=4 * n, ready="y_lo")
                elif ph.kind == "conv":
                    G = mod_groups(ph)[0]
                    if G:
                        pe.wait_ge(sem["exp_done"], at("exp_done", ph))
                        pe.wait_ge(sem["att_done"], at("att_done", ph))
                    with pe.Fori(0, CT) as i:
                        for j in range(4):
                            project(ph, j, j * n, hH, hL, i=i, tiles=4, slots=4 * n)
                            if j < G:
                                pe.wait_ge(sem["wmt_in"], at("wmt_in", ph, 16 * (j + 1), i, 16 * G))
                                pe.wait_ge(sem["row_copied"],
                                           at("row_copied", ph, j + 1 - G, i, G))
                                for k in range(KT):
                                    last = pe.matmul(pS[0:2, j * CH:j * CH + MG],
                                                     silu_c[:, 2 * k:2 * k + 2], wmt[:, k, :],
                                                     start=(k == 0), stop=(k == KT - 1))
                                last.then_inc(sem["row_ready"], 1)
                        if G:
                            pe.wait_ge(sem["row_copied"], at("row_copied", ph, G, i, G))
                            pe.wait_ge(sem["mod_part"], at("mod_part", ph, 0, i, 1))
                            for t in range(2 * G):
                                last = pe.matmul(
                                    pO[:, 2 * t:2 * t + 2],
                                    mrow[st.name][:, t // 2, t % 2 * P:(t % 2 + 1) * P],
                                    ident[0:2, 0:2], start=True, stop=True)
                            last.then_inc(sem["row_turned"], 1)
                elif ph.kind == "mixa":
                    pe.wait_ge(sem["y_lo"], at("y_lo", ph))
                    with pe.Fori(0, 2) as i:
                        for h in range(2):
                            for e in range(2):
                                project(ph, 3 * h + e, (4 * h + e) * n, hH, hL, i=i, tiles=6,
                                        slots=8 * n)
                            project(ph, 3 * h + 2, (4 * h + 2) * n, yH, yL, kts=CT, outs=2, i=i,
                                    tiles=6, slots=8 * n)
                elif ph.kind == "wout":
                    with pe.Fori(0, KT // 2) as i:
                        for j in range(2):
                            project(ph, j, j * n, hH, hL, i=i, tiles=2, slots=2 * n,
                                    ready="ml_ready", first=-KT)


def rope_tables():
    freqs = HD // 4
    p, t = np.arange(P)[:, None], np.arange(SEQ)[None, :]
    inv_freq = (10000.0 ** (-np.arange(freqs, dtype=np.float32) / freqs)).astype(np.float32)
    place = np.where((p // 32) % 2 == 0, t // GRID_W, t % GRID_W).astype(np.float32)
    ang = place * inv_freq[p % freqs]
    sign = np.where((p // freqs) % 2 == 0, -1.0, 1.0).astype(np.float32)
    return np.cos(ang).astype(np.float32), (np.sin(ang) * sign).astype(np.float32)


_INS = ["x", "c", "ctx", "c_ctx", "norm_w", "w_mod", "b_mod", "w_in", "conv_w", "w_a_out",
        "w_b_out", "attn_sink", "w_o", "final_norm_w"]


def kernel(**inputs):
    import concourse.bacc as bacc
    from concourse.bass_utils import run_bass_kernel_spmd as run

    nc = bacc.Bacc("TRN2", target_bir_lowering=False, num_devices=1)
    cos_t, sin_t = rope_tables()
    arrays = {f"in_{n}": np.ascontiguousarray(inputs[n]) for n in _INS}
    arrays.update({"in_cos": cos_t, "in_sin": sin_t})
    args = [nc.dram_tensor(n, a.shape, mybir.dt.from_np(a.dtype), kind="ExternalInput").ap()
            for n, a in arrays.items()]
    out = nc.dram_tensor("out", (1, SEQ, D), F32, kind="ExternalOutput").ap()
    hybrid_block(nc, *args, out)
    r = run(nc, [arrays], core_ids=[0])
    return r.results[0]["out"]
```
